# Optimizing a Trainium2 kernel written in Bass

```python
import math
import jax, jax.numpy as jnp
from jax import lax
import numpy as np

D_MODEL = 1024
BATCH = 1
SEQ = 256
DEPTH = 2

N_HEADS = 8
HEAD_DIM = 64
ATTN_WIDTH = N_HEADS * HEAD_DIM
ROT_DIM = HEAD_DIM // 4
ROPE_THETA = 500000.0
MOBA_BLOCK = 256
MOBA_TOPK = 3
Q_CHUNK = 32
CONV_WIDTH = D_MODEL // 2
CONV_KERNEL = 31
D_FF = 4 * D_MODEL
IN_COLS = 3 * ATTN_WIDTH + 2 * CONV_WIDTH + 2 * D_MODEL
DN_ALPHA = (2 * DEPTH) ** 0.25
DN_BETA = (8 * DEPTH) ** -0.25
ADA_SCALE = 0.1
LN_EPS = 1e-5
NEG_INF = -1e30


def layer_norm(x, g, b):
    xf = x.astype(jnp.float32)
    mu = jnp.mean(xf, -1, keepdims=True)
    var = jnp.mean(jnp.square(xf - mu), -1, keepdims=True)
    return ((xf - mu) * lax.rsqrt(var + LN_EPS)).astype(x.dtype) * g + b

def partial_rope(x, cos, sin):
    half = ROT_DIM // 2
    x1, x2, rest = x[..., :half], x[..., half:ROT_DIM], x[..., ROT_DIM:]
    return jnp.concatenate([x1 * cos - x2 * sin, x2 * cos + x1 * sin, rest], -1)

def moba_attention(q, k, v):
    B, H, S, hd = q.shape
    n_blk = -(-S // MOBA_BLOCK)
    pad = n_blk * MOBA_BLOCK - S
    kp = jnp.pad(k, ((0, 0), (0, 0), (0, pad), (0, 0)))
    vp = jnp.pad(v, ((0, 0), (0, 0), (0, pad), (0, 0)))
    kb = kp.reshape(B, H, n_blk, MOBA_BLOCK, hd)
    vb = vp.reshape(B, H, n_blk, MOBA_BLOCK, hd)
    k_mean = jnp.mean(kb.astype(jnp.float32), axis=3).astype(q.dtype)
    topk = min(MOBA_TOPK, n_blk)
    scale = hd ** -0.5
    n_chunks = S // Q_CHUNK
    q_chunks = jnp.moveaxis(q.reshape(B, H, n_chunks, Q_CHUNK, hd), 2, 0)
    b_idx = jnp.arange(B)[:, None, None, None]
    h_idx = jnp.arange(H)[None, :, None, None]
    blk_ids = jnp.arange(n_blk)

    def attend_chunk(args):
        ci, qc = args
        q_pos = ci * Q_CHUNK + jnp.arange(Q_CHUNK)
        own = (ci * Q_CHUNK) // MOBA_BLOCK
        gate = jnp.einsum('bhqd,bhnd->bhqn', qc, k_mean, preferred_element_type=jnp.float32)
        gate = jnp.where(blk_ids < own, gate, NEG_INF)
        _, sel = lax.top_k(gate, topk)
        sel_ok = jnp.arange(topk) < own
        k_sel = kb[b_idx, h_idx, sel]
        v_sel = vb[b_idx, h_idx, sel]
        s_sel = jnp.einsum('bhqd,bhqjtd->bhqjt', qc, k_sel, preferred_element_type=jnp.float32) * scale
        s_sel = jnp.where(sel_ok[:, None], s_sel, NEG_INF)
        k_own = lax.dynamic_slice_in_dim(kp, own * MOBA_BLOCK, MOBA_BLOCK, axis=2)
        v_own = lax.dynamic_slice_in_dim(vp, own * MOBA_BLOCK, MOBA_BLOCK, axis=2)
        s_own = jnp.einsum('bhqd,bhtd->bhqt', qc, k_own, preferred_element_type=jnp.float32) * scale
        k_pos = own * MOBA_BLOCK + jnp.arange(MOBA_BLOCK)
        s_own = jnp.where(k_pos[None, :] <= q_pos[:, None], s_own, NEG_INF)
        logits = jnp.concatenate([s_sel.reshape(B, H, Q_CHUNK, topk * MOBA_BLOCK), s_own], -1)
        p = jax.nn.softmax(logits, axis=-1).astype(v.dtype)
        p_sel = p[..., :topk * MOBA_BLOCK].reshape(B, H, Q_CHUNK, topk, MOBA_BLOCK)
        p_own = p[..., topk * MOBA_BLOCK:]
        return (jnp.einsum('bhqjt,bhqjtd->bhqd', p_sel, v_sel)
                + jnp.einsum('bhqt,bhtd->bhqd', p_own, v_own))

    out = lax.map(attend_chunk, (jnp.arange(n_chunks), q_chunks))
    return jnp.moveaxis(out, 0, 2).reshape(B, H, S, hd)

def conformer_conv(glu_in, dw_w, dw_b, ln_g, ln_b, w_pw):
    a, g = jnp.split(glu_in, 2, axis=-1)
    h = a * jax.nn.sigmoid(g)
    h = lax.conv_general_dilated(h, dw_w[:, None, :], window_strides=(1,),
                                 padding=[(CONV_KERNEL - 1, 0)],
                                 dimension_numbers=('NWC', 'WIO', 'NWC'),
                                 feature_group_count=CONV_WIDTH) + dw_b
    h = jax.nn.silu(layer_norm(h, ln_g, ln_b))
    return h @ w_pw

def mixer(u, cos, sin, w_in, w_attn_br, dw_w, dw_b, cln_g, cln_b, w_conv_pw, w_out):
    B, S, _ = u.shape
    proj = u @ w_in
    splits = [ATTN_WIDTH, 2 * ATTN_WIDTH, 3 * ATTN_WIDTH,
              3 * ATTN_WIDTH + 2 * CONV_WIDTH, 3 * ATTN_WIDTH + 2 * CONV_WIDTH + D_MODEL]
    q, k, v, glu_in, g_attn, g_conv = jnp.split(proj, splits, axis=-1)
    q = partial_rope(q.reshape(B, S, N_HEADS, HEAD_DIM), cos, sin).transpose(0, 2, 1, 3)
    k = partial_rope(k.reshape(B, S, N_HEADS, HEAD_DIM), cos, sin).transpose(0, 2, 1, 3)
    v = v.reshape(B, S, N_HEADS, HEAD_DIM).transpose(0, 2, 1, 3)
    attn = moba_attention(q, k, v).transpose(0, 2, 1, 3).reshape(B, S, ATTN_WIDTH)
    y_attn = attn @ w_attn_br
    y_conv = conformer_conv(glu_in, dw_w, dw_b, cln_g, cln_b, w_conv_pw)
    merged = jax.nn.sigmoid(g_attn) * y_attn + jax.nn.sigmoid(g_conv) * y_conv
    return merged @ w_out

def first_inputs(seed: int = 0) -> dict:
    key = jax.random.key(seed)
    ks = jax.random.split(key, 20)
    f32 = jnp.float32
    L, D, A, C = DEPTH, D_MODEL, ATTN_WIDTH, CONV_WIDTH
    nrm = lambda k, shape, s: jax.random.normal(k, shape, f32) * s
    return {
        "x": jax.random.normal(ks[0], (BATCH, SEQ, D), f32),
        "c": jax.random.normal(ks[1], (BATCH, D), f32),
        "positions": jnp.broadcast_to(jnp.arange(SEQ, dtype=jnp.int32), (BATCH, SEQ)),
        "w_in": nrm(ks[2], (L, D, IN_COLS), D ** -0.5),
        "w_attn_br": nrm(ks[3], (L, A, D), A ** -0.5),
        "conv_dw_w": nrm(ks[4], (L, CONV_KERNEL, C), CONV_KERNEL ** -0.5),
        "conv_dw_b": nrm(ks[5], (L, C), 0.02),
        "conv_ln_g": 1.0 + nrm(ks[6], (L, C), 0.02),
        "conv_ln_b": nrm(ks[7], (L, C), 0.02),
        "w_conv_pw": nrm(ks[8], (L, C, D), C ** -0.5),
        "w_out": nrm(ks[9], (L, D, D), DN_BETA * D ** -0.5),
        "w_ada": nrm(ks[10], (L, D, 6 * D), ADA_SCALE * D ** -0.5),
        "b_ada": nrm(ks[11], (L, 6 * D), 0.02),
        "ln_mix_g": 1.0 + nrm(ks[12], (L, D), 0.02),
        "ln_mix_b": nrm(ks[13], (L, D), 0.02),
        "w_up": nrm(ks[14], (L, D, D_FF), D ** -0.5),
        "w_down": nrm(ks[15], (L, D_FF, D), DN_BETA * D_FF ** -0.5),
        "ln_ffn_g": 1.0 + nrm(ks[16], (L, D), 0.02),
        "ln_ffn_b": nrm(ks[17], (L, D), 0.02),
    }

def first_block(x, c, positions, w_in, w_attn_br, conv_dw_w, conv_dw_b, conv_ln_g, conv_ln_b,
              w_conv_pw, w_out, w_ada, b_ada, ln_mix_g, ln_mix_b, w_up, w_down,
              ln_ffn_g, ln_ffn_b):
    inv_freq = ROPE_THETA ** (-jnp.arange(0, ROT_DIM, 2, dtype=jnp.float32) / ROT_DIM)
    ang = positions.astype(jnp.float32)[..., None] * inv_freq
    cos = jnp.cos(ang)[:, :, None, :].astype(x.dtype)
    sin = jnp.sin(ang)[:, :, None, :].astype(x.dtype)
    c_act = jax.nn.silu(c)
    for l in range(DEPTH):
        ada = c_act @ w_ada[l] + b_ada[l]
        sh1, sc1, gt1, sh2, sc2, gt2 = [t[:, None, :] for t in jnp.split(ada, 6, axis=-1)]
        u = x * (1.0 + sc1) + sh1
        y = mixer(u, cos, sin, w_in[l], w_attn_br[l], conv_dw_w[l], conv_dw_b[l],
                  conv_ln_g[l], conv_ln_b[l], w_conv_pw[l], w_out[l])
        x = layer_norm(DN_ALPHA * x + (1.0 + gt1) * y, ln_mix_g[l], ln_mix_b[l])
        u = x * (1.0 + sc2) + sh2
        h = jnp.square(jax.nn.relu(u @ w_up[l])) @ w_down[l]
        x = layer_norm(DN_ALPHA * x + (1.0 + gt2) * h, ln_ffn_g[l], ln_ffn_b[l])
    return x


BLOCK = 128
A_HEADS = 8
A_PATTERNS = ((128, 1), (512, 4), (2048, 16))
A_WIDTH = A_HEADS * HEAD_DIM
B_HEADS = 4
B_QK_DIM = HEAD_DIM
B_V_DIM = 2 * HEAD_DIM
B_WIDTH = B_HEADS * B_V_DIM
C_HEADS = 8
C_Q_RANK = 768
C_KV_RANK = 256
C_NOPE = 64
C_ROPE = 32
C_V = 64
C_WIDTH = C_HEADS * C_V
ROPE_THETA_2 = 10000.0
REL_BUCKETS = 32
REL_MAX_DIST = 2048
IN_SIZES = (A_WIDTH, A_WIDTH, A_WIDTH,
            2 * B_HEADS * B_QK_DIM, 2 * B_HEADS * B_QK_DIM, B_WIDTH,
            C_Q_RANK, C_KV_RANK, C_ROPE)
D_IN = 3 * A_WIDTH + 4 * B_HEADS * B_QK_DIM + B_WIDTH + C_Q_RANK + C_KV_RANK + C_ROPE
N_BRANCH = 3
FFN_HIDDEN = -(-8 * D_MODEL // (3 * 256)) * 256
EPS = 1e-6
NEG = -1e30


def rmsnorm(x, g):
    xf = x.astype(jnp.float32)
    y = xf * lax.rsqrt(jnp.mean(xf * xf, axis=-1, keepdims=True) + EPS)
    return (y * g.astype(jnp.float32)).astype(x.dtype)

def t5_bucket(dist):
    dist = jnp.maximum(dist, 0)
    exact = REL_BUCKETS // 2
    log_ratio = jnp.log(jnp.maximum(dist, 1).astype(jnp.float32) / exact) / math.log(REL_MAX_DIST / exact)
    large = jnp.minimum(exact + (log_ratio * (REL_BUCKETS - exact)).astype(jnp.int32), REL_BUCKETS - 1)
    return jnp.where(dist < exact, dist, large)

def rope(x, cos, sin):
    half = x.shape[-1] // 2
    xf = x.astype(jnp.float32)
    x1, x2 = xf[..., :half], xf[..., half:]
    return jnp.concatenate([x1 * cos - x2 * sin, x2 * cos + x1 * sin], axis=-1).astype(x.dtype)

def to_query_blocks(t):
    b, s = t.shape[:2]
    return t.reshape(b, s // BLOCK, BLOCK, *t.shape[2:]).swapaxes(0, 1)

def from_query_blocks(o):
    nq, b = o.shape[:2]
    return o.swapaxes(0, 1).reshape(b, nq * BLOCK, *o.shape[3:])

def dilated_window_attention(q, k, v, bias_table):
    b, s, h, hd = q.shape
    scale = hd ** -0.5
    outs, lses = [], []
    for window, dil in A_PATTERNS:
        n_back = window // dil
        sub_len = s // dil
        nb = -(-sub_len // BLOCK)
        lp = nb * BLOCK

        def to_sub(t):
            t = t.reshape(b, sub_len, dil, h, hd).transpose(0, 2, 1, 3, 4)
            t = jnp.pad(t, ((0, 0), (0, 0), (0, lp - sub_len), (0, 0), (0, 0)))
            return t.reshape(b, dil, nb, BLOCK, h, hd)

        def window_keys(t):
            prev = jnp.pad(t, ((0, 0), (0, 0), (1, 0), (0, 0), (0, 0), (0, 0)))[:, :, :-1]
            return jnp.concatenate([prev, t], axis=3)

        qb = to_sub(q)
        kw = window_keys(to_sub(k))
        vw = window_keys(to_sub(v))
        qi = jnp.arange(BLOCK)[:, None]
        kj = jnp.arange(2 * BLOCK)[None, :]
        step = qi + BLOCK - kj
        in_band = (step >= 0) & (step <= n_back)
        blk = jnp.arange(nb)[:, None, None]
        valid = in_band[None] & ((blk > 0) | (kj[None] >= BLOCK))
        bias = bias_table[t5_bucket(step * dil)].transpose(2, 0, 1)
        sc = jnp.einsum('brnqhc,brnkhc->brnhqk', qb, kw).astype(jnp.float32) * scale + bias
        sc = jnp.where(valid[:, None], sc, NEG)
        lse = jax.nn.logsumexp(sc, axis=-1)
        p = jnp.exp(sc - lse[..., None])
        o = jnp.einsum('brnhqk,brnkhc->brnqhc', p.astype(v.dtype), vw)
        o = o.reshape(b, dil, lp, h, hd)[:, :, :sub_len].transpose(0, 2, 1, 3, 4).reshape(b, s, h, hd)
        lse = lse.transpose(0, 1, 2, 4, 3).reshape(b, dil, lp, h)[:, :, :sub_len]
        lse = lse.transpose(0, 2, 1, 3).reshape(b, s, h)
        outs.append(o)
        lses.append(lse)
    w = jax.nn.softmax(jnp.stack(lses, axis=0), axis=0)
    out = jnp.einsum('gbsh,gbshc->bshc', w, jnp.stack(outs, axis=0).astype(jnp.float32))
    return out.astype(q.dtype).reshape(b, s, h * hd)

def differential_attention(q1, q2, k1, k2, v, lam, bias_table):
    s = q1.shape[1]
    scale = q1.shape[-1] ** -0.5
    kpos = jnp.arange(s)

    def block(args):
        i, qa, qb = args
        qpos = i * BLOCK + jnp.arange(BLOCK)
        dist = qpos[:, None] - kpos[None, :]
        causal = dist >= 0
        bias = bias_table[t5_bucket(dist)].transpose(2, 0, 1)

        def probs(qx, kx):
            sc = jnp.einsum('bqhc,bkhc->bhqk', qx, kx).astype(jnp.float32) * scale + bias
            return jax.nn.softmax(jnp.where(causal, sc, NEG), axis=-1)

        p = probs(qa, k1) - lam * probs(qb, k2)
        return jnp.einsum('bhqk,bkhc->bqhc', p.astype(v.dtype), v)

    o = lax.map(block, (jnp.arange(s // BLOCK), to_query_blocks(q1), to_query_blocks(q2)))
    return from_query_blocks(o)

def mla_attention(q_nope, q_rope, k_nope, k_rope, v):
    s = q_nope.shape[1]
    scale = (C_NOPE + C_ROPE) ** -0.5
    kpos = jnp.arange(s)

    def block(args):
        i, qn, qr = args
        qpos = i * BLOCK + jnp.arange(BLOCK)
        causal = qpos[:, None] >= kpos[None, :]
        sc = (jnp.einsum('bqhc,bkhc->bhqk', qn, k_nope)
              + jnp.einsum('bqhr,bkr->bhqk', qr, k_rope)).astype(jnp.float32) * scale
        p = jax.nn.softmax(jnp.where(causal, sc, NEG), axis=-1)
        return jnp.einsum('bhqk,bkhc->bqhc', p.astype(v.dtype), v)

    o = lax.map(block, (jnp.arange(s // BLOCK), to_query_blocks(q_nope), to_query_blocks(q_rope)))
    return from_query_blocks(o)

def second_inputs(seed: int = 0) -> dict:
    key = jax.random.key(seed)
    ks = jax.random.split(key, 24)
    f32 = jnp.float32

    def nrm(k, shape, scale):
        return jax.random.normal(k, shape, f32) * scale

    def gain(k, shape):
        return 1.0 + 0.05 * jax.random.normal(k, shape, f32)

    return {
        'x': nrm(ks[0], (BATCH, SEQ, D_MODEL), 1.0),
        'rel_bias_table': nrm(ks[1], (REL_BUCKETS, A_HEADS + B_HEADS), 0.5),
        'ln_mix_g': gain(ks[2], (DEPTH, D_MODEL)),
        'w_in': nrm(ks[3], (DEPTH, D_MODEL, D_IN), D_MODEL ** -0.5),
        'lambda_q1': nrm(ks[4], (DEPTH, B_QK_DIM), 0.1),
        'lambda_k1': nrm(ks[5], (DEPTH, B_QK_DIM), 0.1),
        'lambda_q2': nrm(ks[6], (DEPTH, B_QK_DIM), 0.1),
        'lambda_k2': nrm(ks[7], (DEPTH, B_QK_DIM), 0.1),
        'diff_subln_g': gain(ks[8], (DEPTH, B_V_DIM)),
        'mla_q_norm_g': gain(ks[9], (DEPTH, C_Q_RANK)),
        'w_uq': nrm(ks[10], (DEPTH, C_Q_RANK, C_HEADS * (C_NOPE + C_ROPE)), C_Q_RANK ** -0.5),
        'mla_kv_norm_g': gain(ks[11], (DEPTH, C_KV_RANK)),
        'w_ukv': nrm(ks[12], (DEPTH, C_KV_RANK, C_HEADS * (C_NOPE + C_V)), C_KV_RANK ** -0.5),
        'w_gate': nrm(ks[13], (DEPTH, D_MODEL, N_BRANCH * D_MODEL), D_MODEL ** -0.5),
        'b_gate': nrm(ks[14], (DEPTH, N_BRANCH * D_MODEL), 0.1),
        'w_br_a': nrm(ks[15], (DEPTH, A_WIDTH, D_MODEL), A_WIDTH ** -0.5),
        'w_br_b': nrm(ks[16], (DEPTH, B_WIDTH, D_MODEL), B_WIDTH ** -0.5),
        'w_br_c': nrm(ks[17], (DEPTH, C_WIDTH, D_MODEL), C_WIDTH ** -0.5),
        'w_o': nrm(ks[18], (DEPTH, D_MODEL, D_MODEL), D_MODEL ** -0.5),
        'ln_ffn_g': gain(ks[19], (DEPTH, D_MODEL)),
        'w_ffn_gate': nrm(ks[20], (DEPTH, D_MODEL, FFN_HIDDEN), D_MODEL ** -0.5),
        'w_ffn_up': nrm(ks[21], (DEPTH, D_MODEL, FFN_HIDDEN), D_MODEL ** -0.5),
        'w_ffn_down': nrm(ks[22], (DEPTH, FFN_HIDDEN, D_MODEL), FFN_HIDDEN ** -0.5),
        'final_norm_g': gain(ks[23], (D_MODEL,)),
    }

def second_block(x, rel_bias_table, ln_mix_g, w_in, lambda_q1, lambda_k1, lambda_q2, lambda_k2,
              diff_subln_g, mla_q_norm_g, w_uq, mla_kv_norm_g, w_ukv, w_gate, b_gate,
              w_br_a, w_br_b, w_br_c, w_o, ln_ffn_g, w_ffn_gate, w_ffn_up, w_ffn_down,
              final_norm_g):
    b, s, _ = x.shape
    f32 = jnp.float32
    split_points = [int(c) for c in np.cumsum(IN_SIZES)[:-1]]
    pos = jnp.arange(s, dtype=f32)
    inv_freq = ROPE_THETA_2 ** (-jnp.arange(0, C_ROPE, 2, dtype=f32) / C_ROPE)
    ang = pos[:, None] * inv_freq[None, :]
    cos, sin = jnp.cos(ang), jnp.sin(ang)
    bias_a = rel_bias_table[:, :A_HEADS]
    bias_b = rel_bias_table[:, A_HEADS:]

    for l in range(DEPTH):
        h = rmsnorm(x, ln_mix_g[l])
        proj = h @ w_in[l]
        qa, ka, va, qb, kb, vb, cq, ckv, kr = jnp.split(proj, split_points, axis=-1)

        ya = dilated_window_attention(qa.reshape(b, s, A_HEADS, HEAD_DIM),
                                      ka.reshape(b, s, A_HEADS, HEAD_DIM),
                                      va.reshape(b, s, A_HEADS, HEAD_DIM), bias_a)

        lam_init = 0.8 - 0.6 * math.exp(-0.3 * l)
        lam = (jnp.exp(jnp.sum(lambda_q1[l].astype(f32) * lambda_k1[l].astype(f32)))
               - jnp.exp(jnp.sum(lambda_q2[l].astype(f32) * lambda_k2[l].astype(f32))) + lam_init)
        q_pair = qb.reshape(b, s, B_HEADS, 2, B_QK_DIM)
        k_pair = kb.reshape(b, s, B_HEADS, 2, B_QK_DIM)
        ob = differential_attention(q_pair[..., 0, :], q_pair[..., 1, :],
                                    k_pair[..., 0, :], k_pair[..., 1, :],
                                    vb.reshape(b, s, B_HEADS, B_V_DIM), lam, bias_b)
        yb = (rmsnorm(ob, diff_subln_g[l]) * (1.0 - lam_init)).reshape(b, s, B_WIDTH)

        qc = (rmsnorm(cq, mla_q_norm_g[l]) @ w_uq[l]).reshape(b, s, C_HEADS, C_NOPE + C_ROPE)
        q_nope = qc[..., :C_NOPE]
        q_rope = rope(qc[..., C_NOPE:], cos[:, None, :], sin[:, None, :])
        kvc = (rmsnorm(ckv, mla_kv_norm_g[l]) @ w_ukv[l]).reshape(b, s, C_HEADS, C_NOPE + C_V)
        k_nope, vc = kvc[..., :C_NOPE], kvc[..., C_NOPE:]
        k_rope = rope(kr, cos, sin)
        yc = mla_attention(q_nope, q_rope, k_nope, k_rope, vc).reshape(b, s, C_WIDTH)

        gates = jax.nn.sigmoid((h @ w_gate[l] + b_gate[l]).astype(f32)).astype(x.dtype)
        gates = gates.reshape(b, s, N_BRANCH, D_MODEL)
        merged = (gates[:, :, 0] * (ya @ w_br_a[l]) + gates[:, :, 1] * (yb @ w_br_b[l])
                  + gates[:, :, 2] * (yc @ w_br_c[l]))
        x = x + merged @ w_o[l]

        h = rmsnorm(x, ln_ffn_g[l])
        x = x + (jax.nn.silu(h @ w_ffn_gate[l]) * (h @ w_ffn_up[l])) @ w_ffn_down[l]

    return rmsnorm(x, final_norm_g)


def setup_inputs(seed=0):
    out = dict(first_inputs(seed))
    for name, value in second_inputs(seed + 1).items():
        if name != "x":
            out[name + "_2"] = value
    return out


def reference(
    x, c, positions, w_in, w_attn_br, conv_dw_w, conv_dw_b, conv_ln_g, conv_ln_b, w_conv_pw,
    w_out, w_ada, b_ada, ln_mix_g, ln_mix_b, w_up, w_down, ln_ffn_g, ln_ffn_b, rel_bias_table_2,
    ln_mix_g_2, w_in_2, lambda_q1_2, lambda_k1_2, lambda_q2_2, lambda_k2_2, diff_subln_g_2,
    mla_q_norm_g_2, w_uq_2, mla_kv_norm_g_2, w_ukv_2, w_gate_2, b_gate_2, w_br_a_2, w_br_b_2,
    w_br_c_2, w_o_2, ln_ffn_g_2, w_ffn_gate_2, w_ffn_up_2, w_ffn_down_2, final_norm_g_2,
):
    x = first_block(
        x, c, positions, w_in, w_attn_br, conv_dw_w, conv_dw_b, conv_ln_g, conv_ln_b, w_conv_pw,
        w_out, w_ada, b_ada, ln_mix_g, ln_mix_b, w_up, w_down, ln_ffn_g, ln_ffn_b,
    )
    return second_block(
        x, rel_bias_table_2, ln_mix_g_2, w_in_2, lambda_q1_2, lambda_k1_2, lambda_q2_2,
        lambda_k2_2, diff_subln_g_2, mla_q_norm_g_2, w_uq_2, mla_kv_norm_g_2, w_ukv_2, w_gate_2,
        b_gate_2, w_br_a_2, w_br_b_2, w_br_c_2, w_o_2, ln_ffn_g_2, w_ffn_gate_2, w_ffn_up_2,
        w_ffn_down_2, final_norm_g_2,
    )


_drawn_inputs = setup_inputs


def setup_inputs(seed=0):
    import zlib

    import numpy as np

    out = dict(_drawn_inputs(seed))
    spreads = {}
    factors = {'conv_dw_b': 3.523,
     'conv_ln_g': 8.0,
     'conv_ln_b': 8.0,
     'lambda_q2_2': 3.32,
     'mla_q_norm_g_2': 8.0,
     'mla_kv_norm_g_2': 3.379}
    for name, (base, spread) in spreads.items():
        noise = np.random.default_rng([zlib.crc32(name.encode()), seed]).standard_normal(out[name].shape)
        drawn = base * np.exp(spread * noise) if base else spread * noise
        out[name] = __import__('jax').numpy.asarray(drawn.astype(out[name].dtype))
    for name, factor in factors.items():
        out[name] = (out[name] * factor).astype(out[name].dtype)
    return out
```

```python
from contextlib import ExitStack

import concourse.bass as bass
import numpy as np
from concourse import mybir

F32 = mybir.dt.float32
F32R = mybir.dt.float32r
I32 = mybir.dt.int32
ALU = mybir.AluOpType
ACT = mybir.ActivationFunctionType
AX = mybir.AxisListType.X

P = 128
SEQ = 256
TOKS = SEQ // P
D = 1024
DC = D // P
LAYERS = 2
NT = 512
KG = 2
RING = 4
HEADS, HD = 8, 64
AW = HEADS * HD
CONV_K = 31
CW = D // 2
FF1 = 4 * D
IN1 = 3 * AW + 2 * CW + 2 * D
ROT = HD // 4
RH = ROT // 2
ALPHA = (2 * LAYERS) ** 0.25
LN_EPS = 1e-5
RMS_EPS = 1e-6
BIG = 1e30
TRI = 3 * P

IN2 = 4128
IN2_W, IN2_T = 344, 12
QR, KVR = 768, 256
NOPE, ROPE, CV = 64, 32, 64
QH = NOPE + ROPE
FF2 = 2816
HT = 256
BUCKETS, AH, BH = 32, 8, 4
REL = SEQ + P


class Pos:

    def __init__(self, k, *regs):
        self.k, self.regs = k, regs

    def __add__(self, j):
        return Pos(self.k + j, *self.regs)

    def over(self, n):
        assert all(step % n == 0 for _, step in self.regs)
        return Pos(self.k // n, *((r, step // n) for r, step in self.regs))

    def slot(self, n):
        assert all(step % n == 0 for _, step in self.regs)
        return self.k % n

    def count(self, extra=0, times=1):
        value = (self.k + extra) * times
        for r, step in self.regs:
            value = r * (step * times) + value
        return value


def twice(n, h=0):
    return Pos(2 * n.k + h, *((r, 2 * s) for r, s in n.regs))


def settle(eng, passed):
    eng.sem_inc(passed, 1)


class Weights:

    def __init__(self, nc, ctx, tag, dmas):
        sb = lambda n, dt: ctx.enter_context(nc.sbuf_tensor(f"{n}_{tag}", [P, RING, KG * NT], dt))
        sem = lambda n: ctx.enter_context(nc.semaphore(f"{n}_{tag}"))
        self.raw, self.hi, self.lo = sb("w_raw", F32), sb("w_hi", F32R), sb("w_lo", F32R)
        self.raw_in = [sem(f"w_raw_in{s}") for s in range(RING)]
        self.hi_done, self.lo_done, self.used = sem("w_hi_done"), sem("w_lo_done"), sem("w_used")
        self.tile0_done = sem("tile0_done")
        self.dmas = dmas

    def load(self, sp, pos, *parts):
        s = pos.slot(RING)
        assert len(parts) == self.dmas
        sp.wait_ge(self.lo_done, pos.count(1))
        for place, src in parts:
            sp.dma_start(place(self.raw[:, s, :]), src).then_inc(self.raw_in[s], 16)

    def split_hi(self, act, pos, cols=KG * NT):
        s = pos.slot(RING)
        act.wait_ge(self.raw_in[s], pos.over(RING).count(1, 16 * self.dmas))
        act.wait_ge(self.used, pos.count(1))
        act.copy(self.hi[:, s, 0:cols], self.raw[:, s, 0:cols]).then_inc(self.hi_done, 1)

    def split_lo(self, dve, pos, cols=KG * NT):
        s = pos.slot(RING)
        dve.wait_ge(self.hi_done, pos.count(1))
        dve.tensor_tensor(self.lo[:, s, 0:cols], self.raw[:, s, 0:cols], self.hi[:, s, 0:cols].bitcast(F32),
                          ALU.subtract).then_inc(self.lo_done, 1)

    def multiply(self, pe, pos, lhs, k0, width, chunks, outs, first, last, tile_end=True,
                 vacant=None):
        s = pos.slot(RING)
        lhs_hi, lhs_lo = lhs
        pe.wait_ge(self.lo_done, pos.count(RING + 1))
        for tok, out in enumerate(outs):
            if vacant:
                vacant(tok)
            for c in range(chunks):
                a_hi = lhs_hi[:, k0 + c, tok * P:(tok + 1) * P]
                a_lo = lhs_lo[:, k0 + c, tok * P:(tok + 1) * P]
                w_hi = self.hi[:, s, c * width:(c + 1) * width]
                w_lo = self.lo[:, s, c * width:(c + 1) * width]
                pe.matmul(out, a_hi, w_hi, start=first and c == 0, stop=False)
                pe.matmul(out, a_hi, w_lo, start=False, stop=False)
                mm = pe.matmul(out, a_lo, w_hi, start=False, stop=last and c == chunks - 1)
            if last and tile_end and tok == 0:
                mm.then_inc(self.tile0_done, 1)
        mm.then_inc(self.used, 1)

    def wait_tile(self, eng, tok, tile, last_group):
        if tok == 0:
            eng.wait_ge(self.tile0_done, tile.count(1))
        else:
            eng.wait_ge(self.used, last_group.count(RING + 1))


class Turns:

    def __init__(self, nc, ctx, tag, ident):
        self.bank = [ctx.enter_context(nc.psum_tensor(f"turn{b}_{tag}", [P, NT], F32)) for b in range(2)]
        sem = lambda n: ctx.enter_context(nc.semaphore(f"{n}_{tag}"))
        self.full = sem("turn_full")
        self.hi = sem("turn_hi")
        self.free = [sem(f"turn_free{b}") for b in range(2)]
        self.ident = ident

    def turn(self, pe, pos, parts):
        b = pos.slot(2)
        pe.wait_ge(self.free[b], pos.over(2).count(1))
        for rows, cols, src in parts:
            k = src.shape[0]
            if k == P:
                t = pe.transpose(self.bank[b][0:rows, cols], src, self.ident)
            else:
                t = pe.matmul(self.bank[b][0:rows, cols], src, self.ident[0:k, 0:k], start=True, stop=True)
        t.then_inc(self.full, 1)

    def taken(self, eng, pos):
        eng.wait_ge(self.free[pos.slot(2)], pos.over(2).count(2))

    def take(self, act, pos, out, rows=P, cols=NT, scale=1.0, view=None):
        b = pos.slot(2)
        act.wait_ge(self.full, pos.count(1))
        src = self.bank[b][0:rows, 0:cols]
        return act.activation(out, view(src) if view else src, ACT.Copy, scale=scale).then_inc(self.free[b], 1)

    def take_hi(self, act, pos, out, cols=NT, scale=1.0, view=None):
        b = pos.slot(2)
        act.wait_ge(self.full, pos.count(1))
        src = self.bank[b][:, 0:cols]
        act.activation(out, view(src) if view else src, ACT.Copy, scale=scale).then_inc(self.hi, 1)

    def take_lo(self, dve, pos, split, out, hi, cols=NT, scale=1.0, view=None):
        b = pos.slot(2)
        dve.wait_ge(self.hi, split.count(1))
        src = self.bank[b][:, 0:cols]
        dve.scalar_tensor_tensor(out, view(src) if view else src, scale, hi.bitcast(F32),
                                 ALU.mult, ALU.subtract).then_inc(self.free[b], 1)


class Heads:

    def __init__(self, nc, ctx, tag, score_banks, turn_banks):
        sb = lambda n, s: ctx.enter_context(nc.sbuf_tensor(f"{n}_{tag}", s, F32))
        sem = lambda n: ctx.enter_context(nc.semaphore(f"{n}_{tag}"))
        self.qk = sb("qk_rows", [P, TOKS * 4 * QH])
        self.v = sb("v_rows", [P, TOKS, P])
        self.qkT = sb("qkT", [P, 2, 2 * SEQ])
        self.s = [sb(f"scores{h}", [P, TRI]) for h in range(2)]
        self.p = [sb(f"probs{h}", [P, TRI]) for h in range(2)]
        self.pT = [sb(f"probsT{h}", [P, TRI]) for h in range(2)]
        self.low = sb("low", [P, 2, 4])
        self.sum = sb("expsum", [P, 2, 2])
        self.inv = sb("expinv", [P, 2, 2])
        self.S, self.T = score_banks, turn_banks
        self.staged, self.v_staged, self.scored = sem("qk_staged"), sem("v_staged"), sem("scored")
        self.low_ready, self.exp_done, self.p_ready = sem("low_ready"), sem("exp_done"), sem("p_ready")
        self.pT_full, self.pT_ready = sem("pT_full"), sem("pT_ready")
        self.out_full, self.out_hi, self.out_done = sem("o_full"), sem("o_hi"), sem("o_done")

    def scores(self, pe, n, turns, turn, packed):
        turns.taken(pe, turn)
        turns.taken(pe, turn + 1)
        for h in range(2):
            if packed:
                q, k = (self.qkT[h * HD:(h + 1) * HD, x, 0:SEQ] for x in range(2))
            else:
                q, k = (self.qkT[0:QH, h, x * SEQ:(x + 1) * SEQ] for x in range(2))
            pe.matmul(self.S[h][:, 0:P], q[:, 0:P], k[:, 0:P], start=True, stop=True)
            mm = pe.matmul(self.S[h][:, P:TRI], q[:, P:SEQ], k[:, 0:SEQ], start=True, stop=True)
        mm.then_inc(self.scored, 1)

    def lows(self, dve, n, h, scale, bias):
        dve.wait_ge(self.scored, n.count(1))
        dve.scalar_tensor_tensor(self.s[h][:, :], self.S[h][:, 0:TRI], -scale, bias, ALU.mult, ALU.add)
        dve.drain()
        dve.tensor_reduce(self.low[:, h, 0:3], self.s[h][:, :].rearrange("p (b k) -> p b k", b=3), AX, ALU.min)
        dve.drain()
        dve.tensor_tensor(self.low[:, h, 3:4], self.low[:, h, 1:2], self.low[:, h, 2:3], ALU.min)\
           .then_inc(self.low_ready, 1)

    def exps(self, act, n, h):
        act.wait_ge(self.low_ready, twice(n, h).count(1))
        act.activation(self.p[h][:, 0:P], self.s[h][:, 0:P], ACT.Exp, bias=self.low[:, h, 0:1], scale=-1.0,
                       accum_out=self.sum[:, h, 0:1])
        act.activation(self.p[h][:, P:TRI], self.s[h][:, P:TRI], ACT.Exp, bias=self.low[:, h, 3:4], scale=-1.0,
                       accum_out=self.sum[:, h, 1:2]).then_inc(self.exp_done, 1)

    def norm(self, dve, n, h):
        dve.wait_ge(self.exp_done, twice(n, h).count(1))
        dve.reciprocal(self.inv[:, h, :], self.sum[:, h, :])
        dve.drain()
        dve.tensor_scalar(self.p[h][:, 0:P], self.p[h][:, 0:P], self.inv[:, h, 0:1], None, ALU.mult)
        dve.tensor_scalar(self.p[h][:, P:TRI], self.p[h][:, P:TRI], self.inv[:, h, 1:2], None, ALU.mult)\
           .then_inc(self.p_ready, 1)

    def turn(self, pe, n, h, ident):
        if h == 0:
            pe.wait_ge(self.out_done, n.count(1))
        pe.wait_ge(self.p_ready, twice(n, h).count(1))
        for b in range(3):
            t = pe.transpose(self.T[h][:, b * P:(b + 1) * P], self.p[h][:, b * P:(b + 1) * P], ident)
        t.then_inc(self.pT_full, 1)

    def take(self, act, n, h):
        act.wait_ge(self.pT_full, twice(n, h).count(1))
        act.copy(self.pT[h][:, :], self.T[h][:, 0:TRI]).then_inc(self.pT_ready, 1)

    def mix(self, pe, n):
        pe.wait_ge(self.pT_ready, twice(n, 1).count(1))
        pe.wait_ge(self.v_staged, n.count(1))
        for h in range(2):
            o = self.T[0][h * HD:(h + 1) * HD, :]
            v = self.v[:, :, h * HD:(h + 1) * HD]
            pe.matmul(o[:, 0:SEQ], v[:, 0, :], self.pT[h][:, 0:SEQ], start=True, stop=False)
            mm = pe.matmul(o[:, P:SEQ], v[:, 1, :], self.pT[h][:, SEQ:TRI], start=False, stop=True)
        mm.then_inc(self.out_full, 1)

    def out_hi_part(self, act, n, out):
        act.wait_ge(self.out_full, n.count(1))
        act.copy(out, self.T[0][:, 0:SEQ]).then_inc(self.out_hi, 1)

    def out_lo_part(self, dve, n, out, hi):
        dve.wait_ge(self.out_hi, n.count(1))
        dve.tensor_tensor(out, self.T[0][:, 0:SEQ], hi.bitcast(F32), ALU.subtract).then_inc(self.out_done, 1)


def rope(dve, rows, cos, sin, half, tmp):
    x1, x2 = rows[..., 0:half], rows[..., half:2 * half]
    a, b, c, d = tmp
    dve.tensor_tensor(a, x1, cos, ALU.mult)
    dve.tensor_tensor(b, x2, sin, ALU.mult)
    dve.tensor_tensor(c, x2, cos, ALU.mult)
    dve.tensor_tensor(d, x1, sin, ALU.mult)
    dve.drain()
    dve.tensor_tensor(x1, a, b, ALU.subtract)
    dve.tensor_tensor(x2, c, d, ALU.add)
    dve.drain()



T_IN, T_FF = IN1 // NT, FF1 // NT
Q0, K0, V0, A0, G0 = (n * AW for n in range(5))
GA0 = 5 * AW
GC0 = GA0 + D
PAIRS = HEADS // 2
G_IN, G_SQ, G_HALF = T_IN * 4, 8, 4
G1 = G_IN + 2 * G_HALF + G_SQ + T_FF * 8
N_TILES = T_IN + 2 + 2 + 2 + T_FF
F_W, F_U, F_PAIR = 0, 2, 6
F_CONV = F_PAIR + 4 * PAIRS
F_M = F_CONV + 2
F_U2 = F_M + 4
F_H = F_U2 + 4
F_ALL = F_H + 2 * T_FF
S_U, S_CONV, S_M, S_U2, S_H = 0, 4, 6, 10, 14
S_ALL = S_H + 2 * T_FF
N_LN = 6
TWO_PI_PARTS = (6.28125, 0.0019340515136718750, 1.2556659146e-06)
MAGIC = 12582912.0
PI_BELOW = 3.1415925


def first_block(nc, dr, x_res, ident, hide, ones, small):
    ctx = ExitStack()
    with ctx:
        sb = lambda n, s, dt=F32: ctx.enter_context(nc.sbuf_tensor(n, s, dt))
        sem = lambda n: ctx.enter_context(nc.semaphore(n))
        bank = lambda n: ctx.enter_context(nc.psum_tensor(n, [P, NT], F32))

        W = Weights(nc, ctx, "a", 1)
        prod = [bank(f"prod{t}_a") for t in range(TOKS)]
        acc = [bank(f"acc{n}_a") for n in range(4)]
        T = Turns(nc, ctx, "a", ident)
        H = Heads(nc, ctx, "a", acc[0:2], acc[2:4])

        uT = (sb("uT_hi", [P, DC, SEQ], F32R), sb("uT_lo", [P, DC, SEQ], F32R))
        aT = (sb("aT_hi", [P, 4, SEQ], F32R), sb("aT_lo", [P, 4, SEQ], F32R))
        cT = tuple(part[:, 4:8, :] for part in uT)
        proj = sb("proj", [P, TOKS, IN1])
        u_rows, y_rows = proj[:, :, 0:D], proj[:, :, 0:D]
        u2_rows, tmp_rows = proj[:, :, D:2 * D], proj[:, :, 2 * D:2 * D + NT]
        conv_tok, conv_sig = proj[:, :, A0:A0 + CW], proj[:, :, G0:G0 + CW]
        r_rows, h_rows = proj[:, :, 2 * D + NT:3 * D], proj[:, :, 3 * D:3 * D + NT]

        ada_raw = sb("ada_raw", [P, 4, D])
        ada_acc = proj[:, 0, 0:D]
        ada_b = (sb("ada_b", [1, D])[:, :], proj[0:1, 1, 0:D])
        ada_first = sb("ada_first", [P, LAYERS, 2, D])
        ada_rest = sb("ada_rest", [P, 4, D])
        ln_vec = sb("ln_vec", [P, 2, D])
        cln_vec = ln_vec[:, 0, :].rearrange("p (n c) -> p n c", n=2)
        conv_rows = proj[0:CONV_K + 1, 0, GC0:GC0 + CW]
        conv_wT = sb("conv_wT", [P, 4, CONV_K + 1])
        conv_w = sb("conv_w", [P, CONV_K + 1])
        glu_rows = sb("glu_rows", [P, TOKS, P])
        hpad = sb("hpad", [P, CONV_K - 1 + SEQ])
        conv_acc = [sb(f"conv_acc{n}", [P, SEQ]) for n in range(2)]
        c_wide = sb("c_wide", [P, DC, P])
        c_col, c_act = sb("c_col", [P, DC]), sb("c_act", [P, DC])
        pos_i, pos_f = sb("pos_i", [P, TOKS], I32), sb("pos_f", [P, TOKS])
        freq = sb("freq", [P, RH])
        ang, turns_k = sb("ang", [P, 2, TOKS, RH]), sb("turns_k", [P, 2, TOKS, RH])
        trig = sb("trig", [P, 2, TOKS, RH])
        rope_tmp = [sb(f"rope_tmp{n}", [P, TOKS, HEADS, RH]) for n in range(4)]
        stats, mv = sb("stats", [P, TOKS, 2, 6]), sb("mv", [P, TOKS, 2])
        var_eps, rstd = sb("var_eps", [P, TOKS]), sb("rstd", [P, TOKS])
        eps, half_neg = small[:, 0, 0:1], small[:, 2, 0:1]

        ada_in = [sem(f"ada_in{s}") for s in range(4)]
        ada_used = [sem(f"ada_used{s}") for s in range(2)]
        ada_b_in = [sem(f"ada_b_in{s}") for s in range(2)]
        passed = sem("passed")
        ada_acc_done, ada_summed, ada_taken = sem("ada_acc_done"), sem("ada_summed"), sem("ada_taken")
        first_in, freq_in, c_tanh, c_ready = sem("first_in"), sem("freq_in"), sem("c_tanh"), sem("c_ready")
        ang_ready, trig_ready = sem("ang_ready"), sem("trig_ready")
        vec_in, u_ready, u2_ready = sem("vec_in"), sem("u_ready"), sem("u2_ready")
        prod_free = [sem(f"prod_free{t}_a") for t in range(TOKS)]
        proj_in, glu_sig = sem("proj_in"), sem("glu_sig")
        conv_done, conv_mv, conv_rstd = sem("conv_done"), sem("conv_mv"), sem("conv_rstd")
        conv_y, conv_tanh, conv_ready = sem("conv_y"), sem("conv_tanh"), sem("conv_ready")
        merged, h_ready = sem("merged"), sem("h_ready")
        ln_stats, ln_rstd, x_normed, x_ready = sem("ln_stats"), sem("ln_rstd"), sem("x_normed"), sem("x_ready")

        ADA_N = LAYERS * 2

        def layer(r, const, per):
            return Pos(const, (r, per))

        block = ctx.enter_context(nc.Block())

        @block.sync
        def _(sp):
            def ada_chunk(n, used_n, row, l, cols):
                sp.wait_ge(ada_used[n.slot(2)], used_n.count(1))
                sp.dma_start(ada_raw[:, n.slot(4), :], dr["w_ada"][bass.ds(l, 1), row:row + P, cols]
                             .rearrange("a p n -> (a p) n")).then_inc(ada_in[n.slot(4)], 16)

            def ada_bias(place, l, cols):
                sp.dma_start(ada_b[place], dr["b_ada"][bass.ds(l, 1), cols]).then_inc(ada_b_in[place], 16)

            def weights(pos, src, rows, col):
                W.load(sp, pos, (lambda place: place.rearrange("p (c n) -> p c n", c=KG),
                                 src[:, rows if not isinstance(rows, int) else slice(rows, rows + KG * P), col]
                                 .rearrange("a (c p) n -> p (a c) n", p=P)))

            sp.dma_start(c_col[:, :], dr["c"].rearrange("a (k p) -> p (a k)", p=P),
                         allow_slow_non_contiguous=True).then_inc(first_in, 16)
            sp.dma_start(pos_i[:, :], dr["positions"].rearrange("a (t p) -> p (a t)", p=P),
                         allow_slow_non_contiguous=True).then_inc(first_in, 16)
            sp.dma_start(freq[:, :], dr["inv_freq"].to_broadcast([P, RH])).then_inc(freq_in, 16)
            with sp.Fori(0, LAYERS) as l:
                for v in range(2):
                    sp.wait_ge(ada_summed, layer(l, 1 - v, 2).count(1))
                    ada_bias(v, l, slice(v * D, (v + 1) * D))
                for k in range(DC):
                    for v in range(2):
                        ada_chunk(layer(l, 2 * k + v, 2 * DC), layer(l, k, DC), k * P, l, slice(v * D, (v + 1) * D))
            with sp.Fori(0, LAYERS) as l:
                ls = bass.ds(l, 1)
                w_in, w_up, w_down = dr["w_in"][ls], dr["w_up"][ls], dr["w_down"][ls]
                def in_tile(t, pos):
                    for g in range(4):
                        weights(pos + g, w_in, g * KG * P, bass.ds(t * NT, NT))

                def ada_vector(t, n, chunk, used):
                    sp.wait_ge(ada_summed, n.count(2))
                    ada_bias(0, l, bass.ds(t * D + 2 * D, D))
                    for k in range(DC):
                        ada_chunk(chunk + k, used + k // 2, k * P, l, bass.ds(t * D + 2 * D, D))

                with sp.Fori(0, T_IN - PAIRS + 1) as t:
                    in_tile(t, Pos(0, (l, G1), (t, 4)))
                with sp.Fori(0, PAIRS - 1) as t:
                    in_tile(t + (T_IN - PAIRS + 1), Pos(4 * (T_IN - PAIRS + 1), (l, G1), (t, 4)))
                    ada_vector(t, Pos(ADA_N, (l, 4), (t, 1)), Pos(ADA_N * DC, (l, 4 * DC), (t, DC)),
                               Pos(LAYERS * DC, (l, 2 * DC), (t, DC // 2)))
                at = G_IN
                for w, groups in ((dr["w_attn_br"][ls], 2), (dr["w_conv_pw"][ls], 2), (dr["w_out"][ls], 4)):
                    for t in range(2):
                        for g in range(groups):
                            weights(layer(l, at, G1), w, g * KG * P, slice(t * NT, (t + 1) * NT))
                            at += 1
                    if at == G_IN + G_HALF:
                        ada_vector(3, layer(l, ADA_N + 3, 4), layer(l, (ADA_N + 3) * DC, 4 * DC),
                                   layer(l, LAYERS * DC + 3 * DC // 2, 2 * DC))

                def up(f, pos):
                    for g in range(4):
                        weights(pos + g, w_up, g * KG * P, bass.ds(f * NT, NT) if not isinstance(f, int)
                                else slice(f * NT, (f + 1) * NT))

                def down(f, pos):
                    for t in range(2):
                        for g in range(2):
                            weights(pos + (2 * t + g), w_down, bass.ds(f * NT + g * KG * P, KG * P)
                                    if not isinstance(f, int) else f * NT + g * KG * P, slice(t * NT, (t + 1) * NT))

                up(0, layer(l, at, G1))
                with sp.Fori(0, T_FF - 1) as f:
                    up(f + 1, Pos(at + 4, (l, G1), (f, 8)))
                    down(f, Pos(at + 8, (l, G1), (f, 8)))
                down(T_FF - 1, layer(l, at + 4 + 8 * (T_FF - 1), G1))

        @block.gpsimd
        def _(pool):
            def norm_rstd(n, ready, done, tok):
                pool.wait_ge(ready, n)
                pool.tensor_tensor(var_eps[:, tok:tok + 1], mv[:, tok, 1:2], eps, ALU.add)
                pool.drain()
                pool.tensor_tensor(rstd[:, tok:tok + 1], var_eps[:, tok:tok + 1], half_neg, ALU.pow).then_inc(done, 1)

            with pool.Fori(0, LAYERS) as l:
                pool.wait_ge(x_ready, layer(l, 0, TOKS).count(1))
                settle(pool, passed)
                ls = bass.ds(l, 1)
                pool.dma_start(conv_rows[0:CONV_K, :], dr["conv_dw_w"][ls].rearrange("a k c -> (a k) c")).then_inc(vec_in, 16)
                pool.dma_start(conv_rows[CONV_K:CONV_K + 1, :], dr["conv_dw_b"][ls, :]).then_inc(vec_in, 16)
                for n, name in enumerate(("conv_ln_g", "conv_ln_b")):
                    pool.dma_start(cln_vec[:, n, :], dr[name][ls, :].to_broadcast([P, CW])).then_inc(vec_in, 16)
                for tok in range(TOKS):
                    norm_rstd(layer(l, tok, TOKS).count(1), conv_mv, conv_rstd, tok)
                pool.wait_ge(conv_y, layer(l, TOKS - 1, TOKS).count(1))
                settle(pool, passed)
                for n, name in enumerate(("ln_mix_g", "ln_mix_b")):
                    pool.dma_start(ln_vec[:, n, :], dr[name][ls, :].to_broadcast([P, D])).then_inc(vec_in, 16)
                for m in range(2):
                    if m == 1:
                        pool.wait_ge(x_normed, layer(l, 0, 1).count(1))
                        settle(pool, passed)
                        for n, name in enumerate(("ln_ffn_g", "ln_ffn_b")):
                            pool.dma_start(ln_vec[:, n, :], dr[name][ls, :].to_broadcast([P, D])).then_inc(vec_in, 16)
                    for tok in range(TOKS):
                        norm_rstd(layer(l, 2 * m + tok, 2 * TOKS).count(1), ln_stats, ln_rstd, tok)

        @block.scalar
        def _(act):
            def split(pos, n=4):
                for g in range(n):
                    W.split_hi(act, pos + g)

            def take_tile(tile, last_group, outs, func=ACT.Copy, scale=1.0, done=None):
                for tok, out in enumerate(outs):
                    W.wait_tile(act, tok, tile, last_group)
                    act.activation(out, prod[tok][:, :], func, scale=scale).then_inc(prod_free[tok], 1)

            def ada_take(n, out, banks=acc[0:2]):
                act.wait_ge(ada_summed, n.count(3))
                act.copy(out[:, 0:NT], banks[0][:, :])
                act.copy(out[:, NT:D], banks[1][:, :]).then_inc(ada_taken, 1)

            act.wait_ge(first_in, 32)
            act.activation(c_act[:, :], c_col[:, :], ACT.Tanh, scale=0.5).then_inc(c_tanh, 1)
            act.wait_ge(ang_ready, 1)
            act.activation(trig[:, :, :, :], ang[:, :, :, :], ACT.Sin).then_inc(trig_ready, 1)
            with act.Fori(0, LAYERS) as l:
                for n, v, banks in ((0, 1, acc[2:4]), (1, 0, acc[0:2])):
                    ada_take(layer(l, n, 2), ada_first[:, bass.ds(l, 1), v, :].rearrange("p a n -> p (a n)"), banks)

            with act.Fori(0, LAYERS) as l:
                split(layer(l, 0, G1))
                for n in range(2):
                    T.take(act, layer(l, F_W + n, F_ALL), conv_wT[:, 2 * n:2 * n + 2, :], cols=2 * (CONV_K + 1),
                           view=lambda s: s.rearrange("p (c k) -> p c k", c=2))
                for n in range(4):
                    T.take_hi(act, layer(l, F_U + n, F_ALL),
                              uT[0][:, 4 * (n % 2):4 * (n % 2) + 4, n // 2 * P:(n // 2 + 1) * P],
                              view=lambda s: s.rearrange("p (c t) -> p c t", c=4))
                with act.Fori(0, 4) as t:
                    split(Pos(4, (l, G1), (t, 4)), 3)
                    take_tile(Pos(0, (l, N_TILES), (t, 1)), Pos(3, (l, G1), (t, 4)),
                              [proj[:, tok, bass.ds(t * NT, NT)] for tok in range(TOKS)])
                    split(Pos(7, (l, G1), (t, 4)), 1)
                split(layer(l, 20, G1), 3)
                for tok in range(TOKS):
                    W.wait_tile(act, tok, layer(l, 4, N_TILES), layer(l, 19, G1))
                    act.activation(proj[:, tok, G0:G0 + CW], prod[tok][:, :], ACT.Tanh, scale=0.5)\
                       .then_inc(prod_free[tok], 1)
                split(layer(l, 23, G1), 1)

                def conv_take(t, fill):
                    cols = bass.ds(t * P, P) if not isinstance(t, int) else slice(t * P, (t + 1) * P)
                    T.take(act, fill + 3, conv_tok[:, :, cols], cols=SEQ, view=lambda s: s.rearrange("p (t c) -> p t c", t=TOKS))

                def pair(t, first):
                    per = (lambda c: ()) if first else (lambda c: ((t, c),))
                    chunk = lambda a, n, at=0: a[..., at:at + n] if first else a[..., bass.ds(t * n + at, n)]
                    n, fill = Pos(0, (l, PAIRS), *per(1)), Pos(F_PAIR, (l, F_ALL), *per(4))
                    this, nt = Pos(20, (l, G1), *per(4)), Pos(5, (l, N_TILES), *per(1))
                    nxt = this + 4
                    W.split_hi(act, nxt)
                    W.split_hi(act, nxt + 1)
                    if not first:
                        conv_take(t - 1, fill + (-4))
                    T.take(act, fill, H.qkT[:, 0, 0:SEQ], cols=SEQ)
                    T.take(act, fill + 1, H.qkT[:, 1, 0:SEQ], cols=SEQ)
                    T.take(act, fill + 2, hpad[:, CONV_K - 1:], cols=SEQ, scale=0.5)
                    for h in range(2):
                        H.exps(act, n, h)
                    W.split_hi(act, nxt + 2)
                    take_tile(nt, this + 3, [chunk(proj[:, tok, :], NT, GA0) for tok in range(TOKS)], ACT.Tanh, 0.5)
                    W.split_hi(act, nxt + 3)
                    for h in range(2):
                        H.take(act, n, h)
                    H.out_hi_part(act, n, aT[0][:, 0, :] if first else aT[0][:, bass.ds(t, 1), :].rearrange("p a s -> p (a s)"))
                    ada_take(Pos(ADA_N, (l, 4), *per(1)), ada_rest[:, 0, :] if first else
                             ada_rest[:, bass.ds(t, 1), :].rearrange("p a n -> p (a n)"))

                pair(0, True)
                with act.Fori(1, PAIRS) as t:
                    pair(t, False)
                conv_take(PAIRS - 1, layer(l, F_PAIR + 4 * (PAIRS - 1), F_ALL))
                for tok in range(TOKS):
                    act.wait_ge(conv_y, layer(l, tok, TOKS).count(1))
                    act.activation(conv_sig[:, tok, :], conv_tok[:, tok, :], ACT.Tanh, scale=0.5).then_inc(conv_tanh, 1)
                split(layer(l, G_IN + G_HALF, G1))
                for n in range(2):
                    T.take_hi(act, layer(l, F_CONV + n, F_ALL), cT[0][:, :, n * P:(n + 1) * P], scale=0.5,
                              view=lambda s: s.rearrange("p (c t) -> p c t", c=4))
                at = G_IN + 2 * G_HALF
                for j in range(2):
                    split(layer(l, at + 2 * j, G1), 2)
                    for tok in range(TOKS):
                        T.take_hi(act, layer(l, F_M + 2 * j + tok, F_ALL), uT[0][:, 4 * j:4 * j + 4, tok * P:(tok + 1) * P],
                                  scale=0.5, view=lambda s: s.rearrange("p (c t) -> p c t", c=4))
                at += 4
                split(layer(l, at, G1))
                split(layer(l, at + 4, G1))
                for n in range(4):
                    T.take_hi(act, layer(l, F_U2 + n, F_ALL),
                              uT[0][:, 4 * (n % 2):4 * (n % 2) + 4, n // 2 * P:(n // 2 + 1) * P],
                              view=lambda s: s.rearrange("p (c t) -> p c t", c=4))
                at += 4

                def hidden(tile, last_group, fill):
                    for tok in range(TOKS):
                        W.wait_tile(act, tok, tile, last_group)
                        act.activation(r_rows[:, tok, :], prod[tok][:, :], ACT.Relu).then_inc(prod_free[tok], 1)
                    for tok in range(TOKS):
                        T.take_hi(act, fill + tok, aT[0][:, :, tok * P:(tok + 1) * P],
                                  view=lambda s: s.rearrange("p (c t) -> p c t", c=4))

                split(layer(l, at + 4, G1))
                hidden(layer(l, N_TILES - T_FF, N_TILES), layer(l, at + 3, G1), layer(l, F_H, F_ALL))
                with act.Fori(1, T_FF) as f:
                    split(Pos(at, (l, G1), (f, 8)))
                    split(Pos(at + 4, (l, G1), (f, 8)))
                    hidden(Pos(N_TILES - T_FF, (l, N_TILES), (f, 1)), Pos(at - 1, (l, G1), (f, 8)),
                           Pos(F_H, (l, F_ALL), (f, 2)))

        @block.vector
        def _(dve):
            def split(pos, n=4):
                for g in range(n):
                    W.split_lo(dve, pos + g)

            def ada_chunk(l, k):
                n = layer(l, 2 * k, 2 * DC)
                raw = ada_raw[:, n.slot(4), :]
                if k > 0:
                    dve.drain()
                dve.wait_ge(ada_in[n.slot(4)], n.over(4).count(1, 16))
                if k == 0:
                    dve.wait_ge(ada_summed, layer(l, 1, 2).count(1))
                    dve.tensor_scalar(ada_acc, raw, c_act[:, 0:1], None, ALU.mult).then_inc(ada_used[0], 1)
                else:
                    dve.scalar_tensor_tensor(ada_acc, raw, c_act[:, k:k + 1], ada_acc, ALU.mult, ALU.add).then_inc(ada_used[0], 1)
                if k == DC - 1:
                    dve.drain().then_inc(ada_acc_done, 1)

            def modulate(out, x, scale, shift):
                dve.scalar_tensor_tensor(out, scale, 1.0, x, ALU.add, ALU.mult)
                dve.drain()
                return dve.tensor_tensor(out, out, shift, ALU.add)

            def part_stats(rows, tok, h):
                dve.bn_stats(stats[:, tok, h, :], rows[:, h * NT:(h + 1) * NT])

            def mean_var(tok, parts, done):
                dve.drain()
                dve.bn_aggr(mv[:, tok, :], stats[:, tok, 0:parts, :].rearrange("p a s -> p (a s)")).then_inc(done, 1)

            def normed(out, rows, tok, g, b):
                dve.scalar_tensor_tensor(out, rows, mv[:, tok, 0:1], g, ALU.subtract, ALU.mult)
                dve.drain()
                return dve.scalar_tensor_tensor(out, out, rstd[:, tok:tok + 1], b, ALU.mult, ALU.add)

            for s, n in ((W.lo_done, RING), (W.used, RING), (ada_used[0], 2), (ada_used[1], 2), (ada_summed, 2), (ada_taken, 2), (x_ready, 1),
                         (prod_free[0], 1), (prod_free[1], 1), (T.free[0], 1), (T.free[1], 1), (H.out_done, 1)):
                dve.sem_inc(s, n)
            dve.memset(hpad[:, 0:CONV_K - 1], 0.0)
            dve.wait_ge(c_tanh, 1)
            dve.scalar_tensor_tensor(c_act[:, :], c_act[:, :], 1.0, c_col[:, :], ALU.add, ALU.mult)
            dve.drain()
            dve.tensor_scalar(c_act[:, :], c_act[:, :], 0.5, None, ALU.mult)
            dve.drain()
            for k in range(DC):
                dve.tensor_scalar(c_wide[:, k, :], ones[:, :], c_act[:, k:k + 1], None, ALU.mult)
            dve.drain().then_inc(c_ready, 1)
            dve.wait_ge(freq_in, 16)
            dve.tensor_copy(pos_f[:, :], pos_i[:, :])
            dve.drain()
            for f in range(2):
                for tok in range(TOKS):
                    dve.tensor_scalar(ang[:, f, tok, :], freq[:, :], pos_f[:, tok:tok + 1], None, ALU.mult)
            dve.drain()
            for f in range(2):
                dve.tensor_scalar(turns_k[:, f], ang[:, f], 0.5 / np.pi, 0.25 * (1 - f), ALU.mult, ALU.add)
            dve.drain()
            dve.tensor_scalar(turns_k[:, :], turns_k[:, :], MAGIC, None, ALU.add)
            dve.drain()
            dve.tensor_scalar(turns_k[:, :], turns_k[:, :], MAGIC, None, ALU.subtract)
            flat = lambda t: t[:, :, :, :].rearrange("p f t r -> p (f t r)")
            for part in TWO_PI_PARTS:
                dve.drain()
                dve.scalar_tensor_tensor(flat(ang), flat(turns_k), -part, flat(ang), ALU.mult, ALU.add)
            dve.drain()
            dve.tensor_scalar(ang[:, 0], ang[:, 0], 0.5 * np.pi, None, ALU.add)
            dve.drain()
            dve.tensor_scalar(flat(ang), flat(ang), PI_BELOW, -PI_BELOW, ALU.min, ALU.max).then_inc(ang_ready, 1)
            with dve.Fori(0, LAYERS) as l:
                for k in range(DC):
                    ada_chunk(l, k)

            with dve.Fori(0, LAYERS) as l:
                first = lambda v: ada_first[:, bass.ds(l, 1), v, :].rearrange("p a n -> p (a n)")
                dve.wait_ge(ada_taken, ADA_N + 2)
                for tok in range(TOKS):
                    dve.drain()
                    modulate(u_rows[:, tok, :], x_res[:, tok, :], first(1), first(0)).then_inc(u_ready, 1)
                split(layer(l, 0, G1))
                for n in range(4):
                    place = lambda p: p[:, 4 * (n % 2):4 * (n % 2) + 4, n // 2 * P:(n // 2 + 1) * P]
                    T.take_lo(dve, layer(l, F_U + n, F_ALL), layer(l, S_U + n, S_ALL), place(uT[1]), place(uT[0]),
                              view=lambda s: s.rearrange("p (c t) -> p c t", c=4))
                with dve.Fori(0, 4) as t:
                    split(Pos(4, (l, G1), (t, 4)))
                split(layer(l, 20, G1))
                dve.wait_ge(trig_ready, 1)
                for tok in range(TOKS):
                    dve.wait_ge(prod_free[tok], layer(l, 4, N_TILES).count(2))
                cos, sin = (trig[:, f].unsqueeze(2).to_broadcast([P, TOKS, HEADS, RH]) for f in range(2))
                for col in (Q0, K0):
                    rope(dve, proj[:, :, col:col + AW].rearrange("p t (h e) -> p t h e", h=HEADS), cos, sin, RH,
                         [t[:, :, :, :] for t in rope_tmp])
                with dve.Fori(0, PAIRS) as t:
                    n = Pos(0, (l, PAIRS), (t, 1))
                    fill = Pos(F_PAIR, (l, F_ALL), (t, 4))
                    nxt = Pos(24, (l, G1), (t, 4))
                    cols = proj[:, :, 0:2 * AW].rearrange("p t (x c) -> p t x c", x=2)
                    dve.tensor_copy(H.qk[:, 0:TOKS * 2 * P].rearrange("p (t x c) -> p t x c", t=TOKS, x=2),
                                    cols[:, :, :, bass.ds(t * P, P)])
                    dve.tensor_copy(H.v[:, :, :], proj[:, :, bass.ds(t * P + V0, P)]).then_inc(H.v_staged, 1)
                    dve.scalar_tensor_tensor(glu_rows[:, :, :], proj[:, :, bass.ds(t * P + G0, P)], 1.0,
                                             proj[:, :, bass.ds(t * P + A0, P)], ALU.add, ALU.mult)
                    T.taken(dve, layer(l, F_W, F_ALL))
                    T.taken(dve, layer(l, F_W + 1, F_ALL))
                    dve.tensor_copy(conv_w[:, :], conv_wT[:, bass.ds(t, 1), :].rearrange("p a k -> p (a k)"))
                    dve.drain().then_inc(H.staged, 1)
                    W.split_lo(dve, nxt)
                    W.split_lo(dve, nxt + 1)
                    for h in range(2):
                        H.lows(dve, n, h, HD ** -0.5, hide)
                    for h in range(2):
                        H.norm(dve, n, h)
                    W.split_lo(dve, nxt + 2)
                    W.split_lo(dve, nxt + 3)
                    flat_t = lambda p: p[:, bass.ds(t, 1), :].rearrange("p a s -> p (a s)")
                    H.out_lo_part(dve, n, flat_t(aT[1]), flat_t(aT[0]))
                    T.taken(dve, fill + 2)
                    dve.tensor_scalar(conv_acc[0][:, :], hpad[:, 0:SEQ], conv_w[:, 0:1],
                                      conv_w[:, CONV_K:CONV_K + 1], ALU.mult, ALU.add)
                    dve.tensor_scalar(conv_acc[1][:, :], hpad[:, 1:1 + SEQ], conv_w[:, 1:2], None, ALU.mult)
                    for k in range(2, CONV_K):
                        if k % 2 == 0:
                            dve.drain()
                        dve.scalar_tensor_tensor(conv_acc[k % 2][:, :], hpad[:, k:k + SEQ], conv_w[:, k:k + 1],
                                                 conv_acc[k % 2][:, :], ALU.mult, ALU.add)
                    dve.drain()
                    dve.tensor_tensor(conv_acc[0][:, :], conv_acc[0][:, :], conv_acc[1][:, :], ALU.add)\
                       .then_inc(conv_done, 1)
                dve.wait_ge(vec_in, layer(l, 4, 8).count(0, 16))
                T.taken(dve, layer(l, F_PAIR + 4 * PAIRS - 1, F_ALL))
                for tok in range(TOKS):
                    part_stats(conv_tok[:, tok, :], tok, 0)
                    mean_var(tok, 1, conv_mv)
                for tok in range(TOKS):
                    dve.wait_ge(conv_rstd, layer(l, tok, TOKS).count(1))
                    normed(conv_tok[:, tok, :], conv_tok[:, tok, :], tok, cln_vec[:, 0, :], cln_vec[:, 1, :])\
                        .then_inc(conv_y, 1)
                at = G_IN
                for j in range(2):
                    for tok in range(TOKS):
                        W.wait_tile(dve, tok, layer(l, T_IN + j, N_TILES), layer(l, at + 2 * j + 1, G1))
                        dve.scalar_tensor_tensor(y_rows[:, tok, j * NT:(j + 1) * NT],
                                                 proj[:, tok, GA0 + j * NT:GA0 + (j + 1) * NT], 1.0, prod[tok][:, :],
                                                 ALU.add, ALU.mult).then_inc(prod_free[tok], 1)
                    if j == 0:
                        for tok in range(TOKS):
                            dve.wait_ge(conv_tanh, layer(l, tok, TOKS).count(1))
                            dve.scalar_tensor_tensor(conv_tok[:, tok, :], conv_sig[:, tok, :], 1.0, conv_tok[:, tok, :],
                                                     ALU.add, ALU.mult).then_inc(conv_ready, 1)
                    W.split_lo(dve, layer(l, at + 4 + 2 * j, G1))
                    W.split_lo(dve, layer(l, at + 5 + 2 * j, G1))
                for n in range(2):
                    place = lambda p: p[:, :, n * P:(n + 1) * P]
                    T.take_lo(dve, layer(l, F_CONV + n, F_ALL), layer(l, S_CONV + n, S_ALL), place(cT[1]), place(cT[0]),
                              scale=0.5, view=lambda s: s.rearrange("p (c t) -> p c t", c=4))
                at += G_HALF
                for j in range(2):
                    W.split_lo(dve, layer(l, at + 4 + 2 * j, G1))
                    for tok in range(TOKS):
                        W.wait_tile(dve, tok, layer(l, T_IN + 2 + j, N_TILES), layer(l, at + 2 * j + 1, G1))
                        dve.scalar_tensor_tensor(tmp_rows[:, tok, :], proj[:, tok, GC0 + j * NT:GC0 + (j + 1) * NT],
                                                 1.0, prod[tok][:, :], ALU.add, ALU.mult).then_inc(prod_free[tok], 1)
                    dve.drain()
                    for tok in range(TOKS):
                        y = y_rows[:, tok, j * NT:(j + 1) * NT]
                        dve.tensor_tensor(y, y, tmp_rows[:, tok, :], ALU.add).then_inc(merged, 1)
                    dve.drain()
                    W.split_lo(dve, layer(l, at + 5 + 2 * j, G1))
                    for tok in range(TOKS):
                        place = lambda p: p[:, 4 * j:4 * j + 4, tok * P:(tok + 1) * P]
                        T.take_lo(dve, layer(l, F_M + 2 * j + tok, F_ALL), layer(l, S_M + 2 * j + tok, S_ALL),
                                  place(uT[1]), place(uT[0]), scale=0.5, view=lambda s: s.rearrange("p (c t) -> p c t", c=4))
                at += G_HALF

                def residual(j, tok, psum, gate, left=None):
                    cols = slice(j * NT, (j + 1) * NT)
                    y = dve.scalar_tensor_tensor(tmp_rows[:, tok, :], ada_rest[:, gate, cols], 1.0, psum, ALU.add, ALU.mult)
                    if left:
                        y.then_inc(left, 1)
                    dve.drain()
                    dve.scalar_tensor_tensor(x_res[:, tok, cols], x_res[:, tok, cols], ALPHA, tmp_rows[:, tok, :],
                                             ALU.mult, ALU.add)
                    dve.drain()
                    part_stats(x_res[:, tok, :], tok, j)
                    if j == 1:
                        mean_var(tok, 2, ln_stats)

                dve.wait_ge(ada_taken, Pos(ADA_N + 3, (l, 4)).count(3))
                dve.wait_ge(vec_in, layer(l, 6, 8).count(0, 16))
                shift, scale = ada_rest[:, 1, :], ada_rest[:, 2, :]
                dve.scalar_tensor_tensor(u2_rows[:, 0, :], scale, 1.0, ln_vec[:, 1, :], ALU.add, ALU.mult)
                dve.scalar_tensor_tensor(scale, scale, 1.0, ln_vec[:, 0, :], ALU.add, ALU.mult)
                dve.drain()
                dve.tensor_tensor(shift, shift, u2_rows[:, 0, :], ALU.add)
                for j in range(2):
                    split(layer(l, at + 4 + 4 * j, G1), 3)
                    for tok in range(TOKS):
                        W.wait_tile(dve, tok, layer(l, T_IN + 4 + j, N_TILES), layer(l, at + 4 * j + 3, G1))
                        residual(j, tok, prod[tok][:, :], 0, prod_free[tok])
                    if j == 0:
                        split(layer(l, at + 7, G1), 1)
                for tok in range(TOKS):
                    dve.wait_ge(ln_rstd, layer(l, tok, 2 * TOKS).count(1))
                    normed(u2_rows[:, tok, :], x_res[:, tok, :], tok, scale, shift).then_inc(u2_ready, 1)
                split(layer(l, at + 11, G1), 1)
                for n in range(4):
                    place = lambda p: p[:, 4 * (n % 2):4 * (n % 2) + 4, n // 2 * P:(n // 2 + 1) * P]
                    T.take_lo(dve, layer(l, F_U2 + n, F_ALL), layer(l, S_U2 + n, S_ALL), place(uT[1]), place(uT[0]),
                              view=lambda s: s.rearrange("p (c t) -> p c t", c=4))
                at += G_SQ

                def hidden(tile, fill, split_n):
                    for tok in range(TOKS):
                        dve.wait_ge(prod_free[tok], tile.count(2))
                        dve.tensor_tensor(h_rows[:, tok, :], r_rows[:, tok, :], r_rows[:, tok, :], ALU.mult)\
                           .then_inc(h_ready, 1)
                    for tok in range(TOKS):
                        place = lambda p: p[:, :, tok * P:(tok + 1) * P]
                        T.take_lo(dve, fill + tok, split_n + tok, place(aT[1]), place(aT[0]),
                                  view=lambda s: s.rearrange("p (c t) -> p c t", c=4))

                split(layer(l, at + 4, G1))
                for tok in range(TOKS):
                    normed(x_res[:, tok, :], x_res[:, tok, :], tok, ln_vec[:, 0, :], ln_vec[:, 1, :])
                dve.drain().then_inc(x_normed, 1)
                hidden(layer(l, N_TILES - T_FF, N_TILES), layer(l, F_H, F_ALL), layer(l, S_H, S_ALL))
                with dve.Fori(1, T_FF) as f:
                    split(Pos(at, (l, G1), (f, 8)))
                    split(Pos(at + 4, (l, G1), (f, 8)))
                    hidden(Pos(N_TILES - T_FF, (l, N_TILES), (f, 1)), Pos(F_H, (l, F_ALL), (f, 2)),
                           Pos(S_H, (l, S_ALL), (f, 2)))
                for j in range(2):
                    dve.wait_ge(W.used, layer(l, G1 - 3 + 2 * j, G1).count(RING + 1))
                    for tok in range(TOKS):
                        residual(j, tok, acc[2 * j + tok][:, :], 3)
                dve.wait_ge(vec_in, layer(l, 8, 8).count(0, 16))
                for tok in range(TOKS):
                    dve.wait_ge(ln_rstd, layer(l, TOKS + tok, 2 * TOKS).count(1))
                    normed(x_res[:, tok, :], x_res[:, tok, :], tok, ln_vec[:, 0, :], ln_vec[:, 1, :]).then_inc(x_ready, 1)

        @block.tensor
        def _(pe):
            def vacated(tile_n):
                return lambda tok: pe.wait_ge(prod_free[tok], tile_n.count(1))

            def tile(pos, tile_n, lhs, k0, groups, outs):
                for g in range(groups):
                    W.multiply(pe, pos + g, lhs, k0 + KG * g, NT, KG, outs, g == 0, g == groups - 1,
                               vacant=vacated(tile_n) if g == 0 else None)

            def ada_add_bias(place, n, banks):
                pe.wait_ge(ada_b_in[place], n.count(1, 16))
                for h, bank in enumerate(banks):
                    mm = pe.matmul(bank[:, :], ones[0:1, :], ada_b[place][:, h * NT:(h + 1) * NT], start=False, stop=True)
                mm.then_inc(ada_summed, 1)

            def ada_product(chunk, step, banks):
                for k in range(DC):
                    n = Pos(chunk.k + step * k, *chunk.regs)
                    pe.wait_ge(ada_in[n.slot(4)], n.over(4).count(1, 16))
                    for h in range(2):
                        mm = pe.matmul(banks[h][:, :], c_wide[:, k, :], ada_raw[:, n.slot(4), h * NT:(h + 1) * NT],
                                       start=k == 0, stop=False)
                    mm.then_inc(ada_used[n.slot(2)], 1)

            def rows_turn(pos, rows, chunk0):
                T.turn(pe, pos, [(P, slice(c * P, (c + 1) * P), rows[:, (chunk0 + c) * P:(chunk0 + c + 1) * P])
                                 for c in range(4)])

            outs = [prod[tok][:, :] for tok in range(TOKS)]
            with pe.Fori(0, LAYERS) as l:
                pe.wait_ge(c_ready, 1)
                pe.wait_ge(ada_taken, layer(l, 0, 2).count(1))
                ada_product(layer(l, 1, 2 * DC), 2, acc[2:4])
                ada_add_bias(1, layer(l, 0, 1), acc[2:4])
                pe.wait_ge(ada_taken, layer(l, 1, 2).count(1))
                pe.wait_ge(ada_acc_done, layer(l, 0, 1).count(1))
                for h in range(2):
                    pe.matmul(acc[h][:, :], ones[:, :], ada_acc[:, h * NT:(h + 1) * NT], start=True, stop=False)
                ada_add_bias(0, layer(l, 0, 1), acc[0:2])
            with pe.Fori(0, LAYERS) as l:
                pe.wait_ge(vec_in, layer(l, 4, 8).count(0, 16))
                for n in range(2):
                    T.turn(pe, layer(l, F_W + n, F_ALL),
                           [(P, slice(c * (CONV_K + 1), (c + 1) * (CONV_K + 1)),
                             conv_rows[:, (2 * n + c) * P:(2 * n + c + 1) * P]) for c in range(2)])
                for n in range(4):
                    pe.wait_ge(u_ready, layer(l, n // 2, TOKS).count(1))
                    rows_turn(layer(l, F_U + n, F_ALL), u_rows[:, n // 2, :], 4 * (n % 2))
                with pe.Fori(0, 4) as t:
                    for n in range(2, 4):
                        T.taken(pe, layer(l, F_U + n, F_ALL))
                    tile(Pos(0, (l, G1), (t, 4)), Pos(0, (l, N_TILES), (t, 1)), uT, 0, 4, outs)
                tile(layer(l, 16, G1), layer(l, 4, N_TILES), uT, 0, 4, outs)

                def conv_turn(fill, n):
                    pe.wait_ge(conv_done, n.count(1))
                    T.turn(pe, fill + 3, [(P, slice(tok * P, (tok + 1) * P), conv_acc[0][:, tok * P:(tok + 1) * P])
                                          for tok in range(TOKS)])

                def pair(t, first):
                    per = (lambda c: ()) if first else (lambda c: ((t, c),))
                    n, fill = Pos(0, (l, PAIRS), *per(1)), Pos(F_PAIR, (l, F_ALL), *per(4))
                    this, nt = Pos(20, (l, G1), *per(4)), Pos(5, (l, N_TILES), *per(1))
                    ada = Pos(ADA_N, (l, 4), *per(1))
                    W.multiply(pe, this, uT, 0, NT, KG, outs, True, False, vacant=vacated(nt))
                    W.multiply(pe, this + 1, uT, 2, NT, KG, outs, False, False)
                    if not first:
                        conv_turn(fill + (-4), n + (-1))
                    pe.wait_ge(H.staged, n.count(1))
                    rows = H.qk[:, 0:TOKS * 2 * P].rearrange("p (t x c) -> p t x c", t=TOKS, x=2)
                    for x in range(2):
                        T.turn(pe, fill + x, [(P, slice(tok * P, (tok + 1) * P), rows[:, tok, x, :]) for tok in range(TOKS)])
                    T.turn(pe, fill + 2, [(P, slice(tok * P, (tok + 1) * P), glu_rows[:, tok, :]) for tok in range(TOKS)])
                    pe.wait_ge(ada_taken, ada.count(2))
                    H.scores(pe, n, T, fill, True)
                    W.multiply(pe, this + 2, uT, 4, NT, KG, outs, False, False)
                    W.multiply(pe, this + 3, uT, 6, NT, KG, outs, False, True)
                    for h in range(2):
                        H.turn(pe, n, h, ident)
                    H.mix(pe, n)
                    ada_product(Pos(ADA_N * DC, (l, 4 * DC), *per(DC)), 1, acc[0:2])
                    ada_add_bias(0, Pos(LAYERS, (l, 4), *per(1)), acc[0:2])

                pair(0, True)
                with pe.Fori(1, PAIRS) as t:
                    pair(t, False)
                conv_turn(layer(l, F_PAIR + 4 * (PAIRS - 1), F_ALL), layer(l, PAIRS - 1, PAIRS))
                pe.wait_ge(H.out_done, layer(l, PAIRS - 1, PAIRS).count(2))
                at = G_IN
                for j in range(2):
                    tile(layer(l, at + 2 * j, G1), layer(l, T_IN + j, N_TILES), aT, 0, 2, outs)
                for n in range(2):
                    pe.wait_ge(conv_ready, layer(l, n, TOKS).count(1))
                    rows_turn(layer(l, F_CONV + n, F_ALL), conv_tok[:, n, :], 0)
                for n in range(2):
                    T.taken(pe, layer(l, F_CONV + n, F_ALL))
                at += G_HALF

                def merged_turns(j):
                    for tok in range(TOKS):
                        pe.wait_ge(merged, layer(l, 2 * j + tok, 4).count(1))
                        rows_turn(layer(l, F_M + 2 * j + tok, F_ALL), y_rows[:, tok, :], 4 * j)

                tile(layer(l, at, G1), layer(l, T_IN + 2, N_TILES), cT, 0, 2, outs)
                W.multiply(pe, layer(l, at + 2, G1), cT, 0, NT, KG, outs, True, False, vacant=vacated(layer(l, T_IN + 3, N_TILES)))
                merged_turns(0)
                W.multiply(pe, layer(l, at + 3, G1), cT, 2, NT, KG, outs, False, True)
                at += G_HALF
                for j in range(2):
                    for g in range(4):
                        if j == 0 and g == 2:
                            merged_turns(1)
                        if j == 0 and g % 2 == 0:
                            for tok in range(TOKS):
                                T.taken(pe, layer(l, F_M + g + tok, F_ALL))
                        W.multiply(pe, layer(l, at + 4 * j + g, G1), uT, KG * g, NT, KG, outs, g == 0, g == 3,
                                   vacant=vacated(layer(l, T_IN + 4 + j, N_TILES)) if g == 0 else None)
                for n in range(4):
                    pe.wait_ge(u2_ready, layer(l, n // 2, TOKS).count(1))
                    rows_turn(layer(l, F_U2 + n, F_ALL), u2_rows[:, n // 2, :], 4 * (n % 2))
                for n in range(2, 4):
                    T.taken(pe, layer(l, F_U2 + n, F_ALL))
                at += G_SQ

                def hidden_turn(f, per):
                    for tok in range(TOKS):
                        pe.wait_ge(h_ready, Pos(tok, (l, TOKS * T_FF), *per(TOKS)).count(f * TOKS + 1))
                        rows_turn(Pos(F_H + tok + 2 * f, (l, F_ALL), *per(2)), h_rows[:, tok, :], 0)

                def down(pos, first, last, fill):
                    for tok in range(TOKS):
                        T.taken(pe, fill + tok)
                    for j in range(2):
                        for g in range(2):
                            W.multiply(pe, pos + (2 * j + g), aT, KG * g, NT, KG,
                                       [acc[2 * j + tok][:, :] for tok in range(TOKS)],
                                       first and g == 0, last and g == 1, tile_end=False)

                tile(layer(l, at, G1), layer(l, N_TILES - T_FF, N_TILES), uT, 0, 4, outs)

                def step(f, first):
                    per = (lambda c: ()) if isinstance(f, int) else (lambda c: ((f, c),))
                    k = f if isinstance(f, int) else 0
                    up, nt = Pos(at + 4 + 8 * k, (l, G1), *per(8)), Pos(N_TILES - T_FF + 1 + k, (l, N_TILES), *per(1))
                    W.multiply(pe, up, uT, 0, NT, KG, outs, True, False, vacant=vacated(nt))
                    W.multiply(pe, up + 1, uT, 2, NT, KG, outs, False, False)
                    hidden_turn(k, per)
                    W.multiply(pe, up + 2, uT, 4, NT, KG, outs, False, False)
                    W.multiply(pe, up + 3, uT, 6, NT, KG, outs, False, True)
                    down(up + 4, first, False, Pos(F_H + 2 * k, (l, F_ALL), *per(2)))

                step(0, True)
                with pe.Fori(1, T_FF - 1) as f:
                    step(f, False)
                hidden_turn(T_FF - 1, lambda c: ())
                down(layer(l, G1 - 4, G1), False, True, layer(l, F_ALL - 2, F_ALL))



HTILES = FF2 // HT
QA, KA, VA, QB, KB, VB, CQ = (n * AW for n in range(7))
CKV = CQ + QR
KR = CKV + KVR
UQ_W, UKV = QR // 2, CV * 2 * HEADS
LAT_TILES = 4
G2_UQ = IN2_T * 4
G2_UKV = G2_UQ + 6
G2_GATE = G2_UKV + 4
G2_AB = G2_GATE + 24
G2_C = G2_AB + 8
G2_O = G2_C + 4
G2_FF = G2_O + 8
G2 = G2_FF + HTILES * 6
N2_UQ, N2_UKV, N2_GATE = IN2_T, IN2_T + 2, IN2_T + 4
N2_AB = N2_GATE + 6
N2_C = N2_AB + 4
N2_O = N2_C + 2
N2_FF = N2_O + 2
N2 = N2_FF + HTILES
F2_LAT, F2_A = 4, 8
F2_B = F2_A + 2 * PAIRS
F2_M = F2_B + 3 * BH + 2 * PAIRS
F2_U2 = F2_M + 4
F2_H = F2_U2 + 4
F2 = F2_H + 2 * HTILES
S2_LAT, S2_B = 4, 8
S2_M = S2_B + BH
S2_U2 = S2_M + 4
S2_H = S2_U2 + 4
S2 = S2_H + 2 * HTILES
PER = PAIRS + BH + PAIRS
N_VEC = 10


def qk_turn(l, n):
    b = n - PAIRS
    return Pos(F2_A + 2 * n if b <= 2 else F2_B + (3 * b - 2 if b < BH + 2 else 2 * b + BH), (l, F2))


def out_turn(l, b):
    return Pos(F2_B + 6 + 3 * b, (l, F2))


def second_block(nc, dr, scratch, x_res, ident, hide, ones, small):
    ctx = ExitStack()
    with ctx:
        sb = lambda n, s, dt=F32: ctx.enter_context(nc.sbuf_tensor(n, s, dt))
        sem = lambda n: ctx.enter_context(nc.semaphore(n))
        bank = lambda n: ctx.enter_context(nc.psum_tensor(n, [P, NT], F32))

        W = Weights(nc, ctx, "b", 2)
        prod = [bank(f"prod{t}_b") for t in range(TOKS)]
        acc = [bank(f"acc{n}_b") for n in range(4)]
        T = Turns(nc, ctx, "b", ident)
        H = Heads(nc, ctx, "b", acc[0:2], acc[2:4])

        uT = (sb("hT_hi", [P, DC, SEQ], F32R), sb("hT_lo", [P, DC, SEQ], F32R))
        aT = (sb("yaT_hi", [P, 4, SEQ], F32R), sb("yaT_lo", [P, 4, SEQ], F32R))
        bT = (sb("ybT_hi", [P, 4, SEQ], F32R), sb("ybT_lo", [P, 4, SEQ], F32R))
        cT = tuple(part[:, 4:8, :] for part in uT)
        proj = sb("proj_b", [P, TOKS, IN2])
        h_rows, y_rows, u2_rows = (proj[:, :, 0:D] for _ in range(3))
        tmp_rows = proj[:, :, D:D + NT]
        act_rows, hid_rows = proj[:, :, D:D + HT], proj[:, :, D + NT:D + NT + HT]
        q_up = proj[:, :, CQ:CQ + QR]
        kv_up = sb("kv_up", [P, TOKS, UKV])
        gates = sb("gates", [P, TOKS, 3 * D])
        bias = sb("bias", [P, AH + BH, TRI])
        mix_g, ffn_g = sb("mix_g", [P, D]), sb("ffn_g", [P, D])
        lat_g = sb("lat_g", [P, QR + KVR])
        sub_g = sb("sub_g", [P, 2 * HD])
        lam_vec, lam_prod = sb("lam_vec", [P, 4, HD]), sb("lam_prod", [P, 2, HD])
        lam_const = sb("lam_const", [P, 2])
        lam_sum, lam_exp = sb("lam_sum", [P, 2]), sb("lam_exp", [P, 2])
        lam_neg = sb("lam_neg", [P, 1])
        trig = sb("trig_b", [P, TOKS, ROPE])
        rope_tmp = [proj[:, 0, n * HT:(n + 1) * HT].rearrange("p (t h e) -> p t h e", t=TOKS, h=HEADS)
                    for n in range(4)]
        rope_tmp_k = [gates[:, 1, n * ROPE:(n + 1) * ROPE].rearrange("p (t e) -> p t e", t=TOKS) for n in range(4)]
        yb_rows = sb("yb_rows", [P, TOKS, 2 * HD])
        x_sq, x_squares, x_rstd = sb("x_sq", [P, 2, TOKS]), sb("x_squares", [P, TOKS]), sb("x_rstd", [P, TOKS])
        lat_squares, lat_rstd = sb("lat_squares", [P, 4]), sb("lat_rstd", [P, 4])
        sub_squares, sub_rstd = sb("sub_squares", [P, TOKS]), sb("sub_rstd", [P, TOKS])
        bias_one = proj[0:BUCKETS + 2, 0, 2 * D:2 * D + REL]
        bias_tab = proj[0:BUCKETS + 2, 0, 2 * D + REL:2 * D + REL + AH + BH]
        bias_row = proj[0:AH + BH, 1, 2 * D:2 * D + REL]
        flip = proj[:, 1, 2 * D + REL:2 * D + REL + P]
        bias_flipped = gates[:, 1, :].rearrange("p (h k) -> p h k", h=AH + BH)

        consts_in, rows_ready, rows_copied, rows_out, bias_in, bias_turned = (
            sem(n) for n in ("consts_in_b", "rows_ready", "rows_copied", "rows_out", "bias_in", "bias_turned"))
        mix_in, vec_in = sem("mix_g_in"), sem("vec_in_b")
        vec_free = sem("vec_free")
        x_halves, x_sq_done, x_rstd_done = sem("x_halves"), sem("x_sq_done"), sem("x_rstd_done")
        lat_sq_done, lat_rstd_done = sem("lat_sq_done"), sem("lat_rstd_done")
        lam_ready, lam_exped = sem("lam_ready"), sem("lam_exped")
        h_ready, lat_ready, u2_ready = sem("h_ready_b"), sem("lat_ready"), sem("u2_ready_b")
        prod_free = [sem(f"prod_free{t}_b") for t in range(TOKS)]
        gate_done, sub_done, yb_ready = sem("gate_done"), sem("sub_done"), sem("yb_ready")
        merged, act_done = sem("merged_b"), sem("act_done")
        four = lambda s: s.rearrange("p (c t) -> p c t", c=4)
        two = lambda s: s.rearrange("p (c t) -> p c t", c=2)
        flat = lambda a: a.rearrange("p a k -> p (a k)")

        def layer(r, const, per):
            return Pos(const, (r, per))

        def pair(l, n, *regs):
            return Pos(n, (l, PER), *regs)

        def gate_tile(l, n, *regs):
            return Pos(N2_GATE + n, (l, N2), *regs)

        block = ctx.enter_context(nc.Block())

        @block.sync
        def _(sp):
            def rows(pos, src, row, col, width):
                part = lambda c: ((lambda place: place[:, c * width:(c + 1) * width]),
                                  src[:, bass.ds(row + c * P, P), col].rearrange("a p n -> (a p) n"))
                W.load(sp, pos, part(0), part(1))

            sp.dma_start(bias_one[:, :], dr["bias_rows"]).then_inc(consts_in, 16)
            sp.dma_start(bias_tab[0:BUCKETS, :], dr["rel_bias_table_2"]).then_inc(consts_in, 16)
            sp.dma_start(bias_tab[BUCKETS:BUCKETS + 2, :], dr["bias_kinds"]).then_inc(consts_in, 16)
            sp.dma_start(flip, dr["flip"]).then_inc(consts_in, 16)
            sp.dma_start(trig[:, :, :], dr["trig_2"].rearrange("(t p) e -> p t e", p=P)).then_inc(consts_in, 16)
            with sp.Fori(0, LAYERS) as l:
                ls = bass.ds(l, 1)
                ws = {n: dr[n + "_2"][ls] for n in ("w_in", "w_uq", "w_ukv", "w_gate", "w_br_a", "w_br_b", "w_br_c",
                                                    "w_o", "w_ffn_gate", "w_ffn_up", "w_ffn_down")}

                def in_tile(t, pos):
                    for g in range(4):
                        rows(pos + g, ws["w_in"], g * KG * P, bass.ds(t * IN2_W, IN2_W), IN2_W)

                sp.wait_ge(vec_free, layer(l, 0, 1).count(1))
                row = lambda name, n: dr[name + "_2"][ls, :].to_broadcast([P, n])
                sp.dma_start(mix_g[:, :], row("ln_mix_g", D)).then_inc(mix_in, 16)
                in_tile(IN2_T - LAT_TILES, layer(l, 0, G2))
                sp.dma_start(lat_g[:, 0:QR], row("mla_q_norm_g", QR)).then_inc(vec_in, 16)
                sp.dma_start(lat_g[:, QR:QR + KVR], row("mla_kv_norm_g", KVR)).then_inc(vec_in, 16)
                for n, name in enumerate(("lambda_q1", "lambda_q2", "lambda_k1", "lambda_k2")):
                    sp.dma_start(lam_vec[:, n, :], row(name, HD)).then_inc(vec_in, 16)
                sp.dma_start(lam_const[:, :], dr["lam_const"][ls, :].to_broadcast([P, 2])).then_inc(vec_in, 16)
                sp.dma_start(sub_g[:, :], row("diff_subln_g", 2 * HD)).then_inc(vec_in, 16)
                sp.dma_start(gates[:, 0, :], row("b_gate", 3 * D)).then_inc(vec_in, 16)
                sp.dma_start(ffn_g[:, :], row("ln_ffn_g", D)).then_inc(vec_in, 16)
                with sp.Fori(1, LAT_TILES) as t:
                    in_tile(t + (IN2_T - LAT_TILES), Pos(0, (l, G2), (t, 4)))
                with sp.Fori(0, IN2_T - LAT_TILES) as t:
                    in_tile(t, Pos(4 * LAT_TILES, (l, G2), (t, 4)))
                for t in range(2):
                    for g in range(3):
                        rows(layer(l, G2_UQ + 3 * t + g, G2), ws["w_uq"], g * KG * P, bass.ds(t * UQ_W, UQ_W), UQ_W)
                for t in range(2):
                    for c in range(2):
                        part = lambda h: ((lambda place: place[:, h * HT:(h + 1) * HT]),
                                          ws["w_ukv"][:, c * P:(c + 1) * P, t * NT + h * HT:t * NT + (h + 1) * HT]
                                          .rearrange("a p n -> (a p) n"))
                        W.load(sp, layer(l, G2_UKV + 2 * t + c, G2), part(0), part(1))
                with sp.Fori(0, 6) as t:
                    for g in range(4):
                        rows(Pos(G2_GATE + g, (l, G2), (t, 4)), ws["w_gate"], g * KG * P, bass.ds(t * NT, NT), NT)
                with sp.Fori(0, 2) as t:
                    for b, name in enumerate(("w_br_a", "w_br_b")):
                        for g in range(2):
                            rows(Pos(G2_AB + 2 * b + g, (l, G2), (t, 4)), ws[name], g * KG * P, bass.ds(t * NT, NT), NT)
                for name, at, groups in (("w_br_c", G2_C, 2), ("w_o", G2_O, 4)):
                    for t in range(2):
                        for g in range(groups):
                            rows(layer(l, at + groups * t + g, G2), ws[name], g * KG * P, bass.ds(t * NT, NT), NT)

                def gate_up(k, pos):
                    for g in range(4):
                        part = lambda h, name: (
                            (lambda place: place.rearrange("p (c n) -> p c n", c=KG)[:, :, h * HT:(h + 1) * HT]),
                            ws[name][:, g * KG * P:(g + 1) * KG * P, bass.ds(k * HT, HT)]
                            .rearrange("a (c p) n -> p (a c) n", p=P))
                        W.load(sp, pos + g, part(0, "w_ffn_gate"), part(1, "w_ffn_up"))

                def down(k, pos):
                    for j in range(2):
                        rows(pos + j, ws["w_ffn_down"], k * HT, bass.ds(j * NT, NT), NT)

                gate_up(0, layer(l, G2_FF, G2))
                with sp.Fori(0, HTILES // 2) as i:
                    for e in range(2):
                        at = Pos(G2_FF + 4 + 6 * e, (l, G2), (i, 12))
                        gate_up(i * 2 + (1 + e), at)
                        down(i * 2 + e, at + 4)
                down(HTILES - 1, layer(l, G2 - 2, G2))
            sp.wait_ge(vec_free, LAYERS + 1)
            sp.dma_start(mix_g[:, :], dr["final_norm_g_2"].rearrange("(a n) -> a n", a=1).to_broadcast([P, D]))\
              .then_inc(mix_in, 16)

        @block.gpsimd
        def _(pool):
            pool.wait_ge(rows_copied, 1)
            pool.dma_start(scratch, bias_row[:, :]).then_inc(rows_out, 16)
            pool.wait_ge(rows_out, 16)
            pool.dma_start(bias_flipped, bass.AP(tensor=scratch.tensor, offset=0,
                                                 ap=[[1, P], [REL, AH + BH], [1, SEQ]])).then_inc(bias_in, 16)

            def root(out, sq, n):
                pool.tensor_tensor(sq, sq, small[:, 1, 0:n], ALU.add)
                pool.drain()
                return pool.tensor_tensor(out, sq, small[:, 2, 0:n], ALU.pow)

            def x_root(n):
                for tok in range(TOKS):
                    pool.wait_ge(x_sq_done, Pos(4 * n.k + 2 + tok, *((r, 4 * s) for r, s in n.regs)).count(1))
                    pool.tensor_tensor(x_squares[:, tok:tok + 1], x_sq[:, 0, tok:tok + 1], x_sq[:, 1, tok:tok + 1], ALU.add)
                    pool.drain()
                    root(x_rstd[:, tok:tok + 1], x_squares[:, tok:tok + 1], 1).then_inc(x_rstd_done, 1)

            with pool.Fori(0, LAYERS) as l:
                x_root(layer(l, 0, 2))
                pool.wait_ge(lat_sq_done, layer(l, 0, 1).count(1))
                root(lat_rstd[:, :], lat_squares[:, :], 4).then_inc(lat_rstd_done, 1)
                with pool.Fori(0, BH) as b:
                    pool.wait_ge(H.out_hi, pair(l, PAIRS, (b, 1)).count(1))
                    root(sub_rstd[:, :], sub_squares[:, :], TOKS).then_inc(sub_done, 1)
                x_root(layer(l, 1, 2))
            x_root(Pos(2 * LAYERS))

        @block.scalar
        def _(act):
            def split(pos, n, cols=KG * NT):
                for g in range(n):
                    W.split_hi(act, pos + g, cols)

            def take_tile(tile, last_group, outs, cols):
                for tok, out in enumerate(outs):
                    W.wait_tile(act, tok, tile, last_group)
                    act.copy(out, prod[tok][:, 0:cols]).then_inc(prod_free[tok], 1)

            def mean_squares(rows, n, place):
                return act.activation(kv_up[:, place % 2, 0:n], rows, ACT.Square, scale=float(n) ** -0.5,
                                      accum_out=lat_squares[:, place:place + 1])

            def square_x(n):
                for j in range(2):
                    for tok in range(TOKS):
                        half = Pos(4 * n.k + TOKS * j + tok, *((r, 4 * s) for r, s in n.regs))
                        act.wait_ge(x_halves, half.count(1))
                        act.activation(kv_up[:, tok, j * NT:(j + 1) * NT], x_res[:, tok, j * NT:(j + 1) * NT], ACT.Square,
                                       scale=float(D) ** -0.5, accum_out=x_sq[:, j, tok:tok + 1]).then_inc(x_sq_done, 1)

            def gate_tanh(tile, cols):
                for tok in range(TOKS):
                    act.wait_ge(prod_free[tok], tile.count(2))
                    act.activation(gates[:, tok, cols], gates[:, tok, cols], ACT.Tanh, scale=0.5).then_inc(gate_done, 1)

            act.wait_ge(rows_ready, 1)
            act.copy(bias_row[:, :], prod[0][0:AH + BH, 0:REL]).then_inc(rows_copied, 1)
            with act.Fori(0, LAYERS) as l:
                square_x(layer(l, 0, 2))
                split(layer(l, 0, G2), 4, KG * IN2_W)
                for n in range(4):
                    T.take_hi(act, layer(l, n, F2), uT[0][:, 4 * (n % 2):4 * (n % 2) + 4, n // 2 * P:(n // 2 + 1) * P],
                              view=four)
                in_cols = lambda t: [proj[:, tok, bass.ds(t * IN2_W, IN2_W)] for tok in range(TOKS)]
                with act.Fori(0, LAT_TILES) as t:
                    split(Pos(4, (l, G2), (t, 4)), 3, KG * IN2_W)
                    take_tile(Pos(0, (l, N2), (t, 1)), Pos(3, (l, G2), (t, 4)), in_cols(t + (IN2_T - LAT_TILES)), IN2_W)
                    split(Pos(7, (l, G2), (t, 4)), 1, KG * IN2_W)
                act.wait_ge(lam_ready, layer(l, 0, 1).count(1))
                act.activation(lam_exp[:, :], lam_sum[:, :], ACT.Exp).then_inc(lam_exped, 1)
                act.drain()
                for tok in range(TOKS):
                    mean_squares(proj[:, tok, CQ:CQ + QR], QR, tok)
                act.drain()
                for tok in range(TOKS):
                    sq = mean_squares(proj[:, tok, CKV:CKV + KVR], KVR, 2 + tok)
                sq.then_inc(lat_sq_done, 1)
                with act.Fori(0, IN2_T - LAT_TILES - 1) as t:
                    split(Pos(4 + 4 * LAT_TILES, (l, G2), (t, 4)), 3, KG * IN2_W)
                    take_tile(Pos(LAT_TILES, (l, N2), (t, 1)), Pos(4 * LAT_TILES + 3, (l, G2), (t, 4)), in_cols(t), IN2_W)
                    split(Pos(7 + 4 * LAT_TILES, (l, G2), (t, 4)), 1, KG * IN2_W)
                split(layer(l, G2_UQ, G2), 3, KG * UQ_W)
                take_tile(layer(l, IN2_T - 1, N2), layer(l, G2_UQ - 1, G2), in_cols(IN2_T - LAT_TILES - 1), IN2_W)
                split(layer(l, G2_UQ + 3, G2), 1, KG * UQ_W)
                for n in range(4):
                    T.take_hi(act, layer(l, F2_LAT + n, F2), (aT, bT)[n % 2][0][:, :, n // 2 * P:(n // 2 + 1) * P], view=four)
                split(layer(l, G2_UQ + 4, G2), 2, KG * UQ_W)
                take_tile(layer(l, N2_UQ, N2), layer(l, G2_UQ + 2, G2), [q_up[:, tok, 0:UQ_W] for tok in range(TOKS)], UQ_W)
                split(layer(l, G2_UKV, G2), 3, NT)
                take_tile(layer(l, N2_UQ + 1, N2), layer(l, G2_UQ + 5, G2),
                          [q_up[:, tok, UQ_W:QR] for tok in range(TOKS)], UQ_W)
                split(layer(l, G2_UKV + 3, G2), 1, NT)
                for j in range(2):
                    split(layer(l, G2_GATE + 2 * j, G2), 2)
                    take_tile(layer(l, N2_UKV + j, N2), layer(l, G2_UKV + 2 * j + 1, G2),
                              [kv_up[:, tok, j * NT:(j + 1) * NT] for tok in range(TOKS)], NT)
                def take_qk(fill):
                    for x in range(2):
                        T.take(act, fill + x, H.qkT[:, x, 0:SEQ], cols=SEQ)

                take_qk(qk_turn(l, 0))
                with act.Fori(0, PAIRS) as t:
                    n = pair(l, 0, (t, 1))
                    nxt = Pos(G2_GATE + 4, (l, G2), (t, 4))
                    for h in range(2):
                        H.exps(act, n, h)
                    split(nxt, 2)
                    take_qk(Pos(F2_A + 2, (l, F2), (t, 2)))
                    split(nxt + 2, 1)
                    for h in range(2):
                        H.take(act, n, h)
                    H.out_hi_part(act, n, flat(aT[0][:, bass.ds(t, 1), :]))
                    split(nxt + 3, 1)
                    gate_tanh(gate_tile(l, 0, (t, 1)), bass.ds(t * NT, NT))

                def take_rows(m):
                    for h in range(2):
                        T.take(act, qk_turn(l, m) + h, H.qkT[0:QH, h, :], rows=QH)

                for b in range(BH):
                    m = PAIRS + b
                    n, nxt = pair(l, m), layer(l, G2_GATE + 20 + 2 * b, G2)
                    H.exps(act, n, 0)
                    if b < BH - 1:
                        take_qk(qk_turn(l, m + 1))
                    else:
                        take_rows(m + 1)
                    H.exps(act, n, 1)
                    split(nxt, 1)
                    if b > 0:
                        T.take_hi(act, out_turn(l, b - 1), bT[0][:, b - 1, :], cols=SEQ)
                    act.wait_ge(H.pT_full, twice(n, 1).count(1))
                    act.copy(H.pT[0][:, :], H.T[0][:, 0:TRI]).then_inc(H.pT_ready, 2)
                    act.wait_ge(H.out_full, n.count(1))
                    for tok in range(TOKS):
                        sq = act.activation(H.p[1][:, tok * P:(tok + 1) * P], H.T[1][:, tok * P:(tok + 1) * P],
                                            ACT.Square, scale=float(2 * HD) ** -0.5,
                                            accum_out=sub_squares[:, tok:tok + 1])
                    sq.then_inc(H.out_hi, 1)
                    split(nxt + 1, 1)
                    if b % 2:
                        gate_tanh(gate_tile(l, 4 + b // 2), slice(2 * D + b // 2 * NT, 2 * D + (b // 2 + 1) * NT))
                for c in range(PAIRS):
                    m = PAIRS + BH + c
                    n, nxt = pair(l, m), layer(l, G2_AB + 4 + 2 * c, G2)
                    H.exps(act, n, 0)
                    if c < PAIRS - 1:
                        take_rows(m + 1)
                    H.exps(act, n, 1)
                    split(nxt, 1)
                    if c == 0:
                        T.take_hi(act, out_turn(l, BH - 1), bT[0][:, BH - 1, :], cols=SEQ)
                    for h in range(2):
                        H.take(act, n, h)
                    H.out_hi_part(act, n, cT[0][:, c, :])
                    split(nxt + 1, 1)
                for j in range(2):
                    split(layer(l, G2_O + 2 * j, G2), 2)
                    for tok in range(TOKS):
                        T.take_hi(act, layer(l, F2_M + 2 * j + tok, F2), uT[0][:, 4 * j:4 * j + 4, tok * P:(tok + 1) * P],
                                  scale=0.5, view=four)
                split(layer(l, G2_O + 4, G2), 7)
                square_x(layer(l, 1, 2))
                split(layer(l, G2_FF + 3, G2), 1)
                for n in range(4):
                    T.take_hi(act, layer(l, F2_U2 + n, F2),
                              uT[0][:, 4 * (n % 2):4 * (n % 2) + 4, n // 2 * P:(n // 2 + 1) * P], view=four)

                def take_hidden(fill, out):
                    for tok in range(TOKS):
                        T.take_hi(act, fill + tok, out[0][:, 0:2, tok * P:(tok + 1) * P], cols=SEQ, scale=0.5, view=two)

                def gated(tile, last_group):
                    for tok in range(TOKS):
                        W.wait_tile(act, tok, tile, last_group)
                        act.activation(act_rows[:, tok, :], prod[tok][:, 0:HT], ACT.Tanh, scale=0.5).then_inc(act_done, 1)

                gated(layer(l, N2_FF, N2), layer(l, G2_FF + 3, G2))
                split(layer(l, G2_FF + 4, G2), 2)
                with act.Fori(0, HTILES // 2) as i:
                    for e in range(2):
                        at = Pos(G2_FF + 4 + 6 * e, (l, G2), (i, 12))
                        split(at + 2, 2)
                        take_hidden(Pos(F2_H + 2 * e, (l, F2), (i, 4)), (aT, bT)[e])
                        split(at + 4, 2)
                        gated(Pos(N2_FF + 1 + e, (l, N2), (i, 2)), at + 3)
                        split(at + 6, 2)
                take_hidden(layer(l, F2 - 2, F2), aT)
            square_x(Pos(2 * LAYERS))

        @block.vector
        def _(dve):
            def split(pos, n, cols=KG * NT):
                for g in range(n):
                    W.split_lo(dve, pos + g, cols)

            def rms(out, rows, scale, g):
                return dve.scalar_tensor_tensor(out, rows, scale, g, ALU.mult, ALU.mult)

            def x_norm(n, out, g, ready=None):
                for tok in range(TOKS):
                    dve.wait_ge(x_rstd_done, Pos(TOKS * n.k + tok, *((r, TOKS * s) for r, s in n.regs)).count(1))
                    y = rms(out[:, tok, :], x_res[:, tok, :], x_rstd[:, tok:tok + 1], g[:, :])
                    if ready:
                        y.then_inc(ready, 1)

            def times_gate(out, gate_cols, tok):
                return dve.scalar_tensor_tensor(out, gates[:, tok, gate_cols], 1.0, prod[tok][:, :], ALU.add, ALU.mult)

            def add_gate_bias(tile, last_group, cols):
                for tok in range(TOKS):
                    W.wait_tile(dve, tok, tile, last_group)
                for tok in (1, 0):
                    dve.tensor_tensor(gates[:, tok, cols], gates[:, 0, cols], prod[tok][:, :], ALU.add)\
                       .then_inc(prod_free[tok], 1)

            def stage_qk(qk_cols):
                dve.tensor_copy(H.qk[:, 0:TOKS * 2 * P].rearrange("p (t x c) -> p t x c", t=TOKS, x=2),
                                qk_cols).then_inc(H.staged, 1)

            def stage_v(v_cols):
                dve.tensor_copy(H.v[:, :, :], v_cols).then_inc(H.v_staged, 1)

            for b, flipped in enumerate(prod + acc):
                dve.wait_ge(bias_turned, b + 1)
                rows = flipped[:, :].rearrange("p (h k) -> p h k", h=2)
                dve.tensor_copy(bias[:, 2 * b:2 * b + 2, P:TRI], rows)
                dve.tensor_copy(bias[:, 2 * b:2 * b + 2, 0:P], rows[:, :, P:SEQ])
            dve.drain()
            for s, n in ((W.lo_done, RING), (W.used, RING), (prod_free[0], 1), (prod_free[1], 1),
                         (T.free[0], 1), (T.free[1], 1), (H.out_done, 1), (vec_free, 1), (x_halves, 4)):
                dve.sem_inc(s, n)
            with dve.Fori(0, LAYERS) as l:
                dve.wait_ge(mix_in, layer(l, 0, 1).count(1, 16))
                x_norm(layer(l, 0, 2), h_rows, mix_g, h_ready)
                split(layer(l, 0, G2), 4, KG * IN2_W)
                for n in range(4):
                    place = lambda p: p[:, 4 * (n % 2):4 * (n % 2) + 4, n // 2 * P:(n // 2 + 1) * P]
                    T.take_lo(dve, layer(l, n, F2), layer(l, n, S2), place(uT[1]), place(uT[0]), view=four)
                dve.wait_ge(vec_in, layer(l, N_VEC, N_VEC).count(0, 16))
                dve.tensor_tensor(lam_prod[:, :, :], lam_vec[:, 0:2, :], lam_vec[:, 2:4, :], ALU.mult)
                dve.tensor_scalar(sub_g[:, :], sub_g[:, :], lam_const[:, 1:2], None, ALU.mult)
                dve.drain()
                dve.tensor_reduce(lam_sum[:, :], lam_prod[:, :, :], AX, ALU.add).then_inc(lam_ready, 1)
                with dve.Fori(0, LAT_TILES) as t:
                    split(Pos(4, (l, G2), (t, 4)), 4, KG * IN2_W)
                dve.wait_ge(lam_exped, layer(l, 0, 1).count(1))
                dve.scalar_tensor_tensor(lam_neg[:, :], lam_exp[:, 1:2], lam_exp[:, 0:1], lam_const[:, 0:1],
                                         ALU.subtract, ALU.add)
                dve.wait_ge(lat_rstd_done, layer(l, 0, 1).count(1))
                for tok in range(TOKS):
                    rms(proj[:, tok, CQ:CKV], proj[:, tok, CQ:CKV], lat_rstd[:, tok:tok + 1], lat_g[:, 0:QR])
                    rms(proj[:, tok, CKV:KR], proj[:, tok, CKV:KR], lat_rstd[:, 2 + tok:3 + tok], lat_g[:, QR:])\
                        .then_inc(lat_ready, 1)
                cos, sin = trig[:, :, 0:ROPE // 2], trig[:, :, ROPE // 2:]
                dve.wait_ge(consts_in, 16 * 5)
                rope(dve, proj[:, :, KR:], cos, sin, ROPE // 2, rope_tmp_k)
                with dve.Fori(0, IN2_T - LAT_TILES - 1) as t:
                    split(Pos(4 + 4 * LAT_TILES, (l, G2), (t, 4)), 4, KG * IN2_W)
                split(layer(l, G2_UQ, G2), 4, KG * UQ_W)
                for n in range(4):
                    place = lambda p: p[:, :, n // 2 * P:(n // 2 + 1) * P]
                    lat = (aT, bT)[n % 2]
                    T.take_lo(dve, layer(l, F2_LAT + n, F2), layer(l, S2_LAT + n, S2), place(lat[1]), place(lat[0]), view=four)
                two_cols = lambda col: proj[:, :, col:col + 2 * AW].rearrange("p t (x c) -> p t x c", x=2)
                for tok in range(TOKS):
                    dve.wait_ge(prod_free[tok], layer(l, IN2_T - 1, N2).count(2))
                stage_qk(two_cols(QA)[..., 0:P])
                split(layer(l, G2_UQ + 4, G2), 2, KG * UQ_W)
                split(layer(l, G2_UKV, G2), 4, NT)
                split(layer(l, G2_GATE, G2), 4)
                rope_q = lambda: rope(dve, q_up.rearrange("p t (h e) -> p t h e", h=HEADS)[..., NOPE:QH],
                     *(f.unsqueeze(2).to_broadcast([P, TOKS, HEADS, ROPE // 2]) for f in (cos, sin)), ROPE // 2,
                     [t[:, :, :, :] for t in rope_tmp])
                def branch_a(t, last):
                    per = (lambda c: ()) if last else (lambda c: ((t, c),))
                    k = t if last else 0
                    of = lambda a, at, size: a[..., at:at + size] if last else a[..., bass.ds(at, size)]
                    n, nxt = pair(l, k, *per(1)), Pos(G2_GATE + 4 + 4 * k, (l, G2), *per(4))
                    row = lambda a, at: a[:, at, :] if last else flat(a[:, bass.ds(at, 1), :])
                    for h in range(2):
                        H.lows(dve, n, h, HD ** -0.5, row(bias, t * 2 + h))
                    stage_qk(two_cols(QB)[..., 0:P] if last else two_cols(QA)[:, :, :, bass.ds(t * P + P, P)])
                    stage_v(of(proj, t * P + VA, P))
                    for h in range(2):
                        H.norm(dve, n, h)
                    split(nxt, 3)
                    add_gate_bias(gate_tile(l, k, *per(1)), nxt + (-1), slice(t * NT, (t + 1) * NT) if last else bass.ds(t * NT, NT))
                    H.out_lo_part(dve, n, row(aT[1], t), row(aT[0], t))
                    if not last:
                        split(nxt + 3, 1)

                with dve.Fori(0, PAIRS - 1) as t:
                    branch_a(t, False)
                for tok in range(TOKS):
                    dve.wait_ge(prod_free[tok], layer(l, N2_UKV + 1, N2).count(2))
                rope_q()
                branch_a(PAIRS - 1, True)

                def stage_c(c):
                    qk = H.qk[:, :].rearrange("p (t h x c) -> p t h x c", t=TOKS, h=2, x=2)
                    kv = kv_up[:, :, c * 2 * P:(c + 1) * 2 * P].rearrange("p t (h c) -> p t h c", h=2)
                    dve.tensor_copy(qk[:, :, :, 0, :], q_up[:, :, c * 2 * QH:(c + 1) * 2 * QH].rearrange("p t (h c) -> p t h c", h=2))
                    dve.tensor_copy(qk[:, :, :, 1, 0:NOPE], kv[:, :, :, 0:NOPE])
                    dve.tensor_copy(qk[:, :, :, 1, NOPE:], proj[:, :, KR:].unsqueeze(2).to_broadcast([P, TOKS, 2, ROPE]))
                    dve.drain().then_inc(H.staged, 1)
                    return kv[:, :, :, NOPE:]

                def branch_b_out(b):
                    dve.wait_ge(sub_done, layer(l, b, BH).count(1))
                    for tok in range(TOKS):
                        y = rms(yb_rows[:, tok, :], H.T[1][:, tok * P:(tok + 1) * P], sub_rstd[:, tok:tok + 1], sub_g[:, :])
                    y.then_inc(H.out_done, 1)

                def branch_b_lo(b):
                    T.take_lo(dve, out_turn(l, b), layer(l, S2_B + b, S2), bT[1][:, b, :], bT[0][:, b, :], cols=SEQ)

                for b in range(BH):
                    n, nxt = pair(l, PAIRS + b), layer(l, G2_GATE + 20 + 2 * b, G2)
                    dve.wait_ge(H.scored, n.count(1))
                    if b > 0:
                        branch_b_out(b - 1)
                    if b < BH - 1:
                        stage_qk(two_cols(QB)[..., (b + 1) * P:(b + 2) * P])
                    else:
                        v_c = stage_c(0)
                    for h in range(2):
                        H.lows(dve, n, h, HD ** -0.5, bias[:, AH + b, :])
                    stage_v(proj[:, :, VB + b * P:VB + (b + 1) * P])
                    dve.wait_ge(H.exp_done, twice(n, 1).count(1))
                    dve.reciprocal(H.inv[:, :, :], H.sum[:, :, :])
                    dve.drain()
                    dve.tensor_scalar(H.inv[:, 1, :], H.inv[:, 1, :], lam_neg[:, 0:1], None, ALU.mult)
                    tiles = ((slice(0, P), 0), (slice(P, TRI), 1))
                    for cols, tok in tiles:
                        dve.tensor_scalar(H.p[0][:, cols], H.p[0][:, cols], H.inv[:, 0, tok:tok + 1], None, ALU.mult)
                    dve.drain()
                    for cols, tok in tiles:
                        p = dve.scalar_tensor_tensor(H.p[0][:, cols], H.p[1][:, cols], H.inv[:, 1, tok:tok + 1],
                                                     H.p[0][:, cols], ALU.mult, ALU.add)
                    p.then_inc(H.p_ready, 2)
                    split(nxt + (-1), 2)
                    if b > 0:
                        branch_b_lo(b - 1)
                    if b % 2:
                        add_gate_bias(gate_tile(l, 4 + b // 2), nxt + (-3), slice(2 * D + b // 2 * NT, 2 * D + (b // 2 + 1) * NT))
                for c in range(PAIRS):
                    n, nxt = pair(l, PAIRS + BH + c), layer(l, G2_AB + 4 + 2 * c, G2)
                    i, e = c // 2, c % 2
                    cols = slice(i * NT, (i + 1) * NT)
                    dve.wait_ge(H.scored, n.count(1))
                    if c == 0:
                        branch_b_out(BH - 1)
                    v_now = v_c
                    if c < PAIRS - 1:
                        v_c = stage_c(c + 1)
                    for h in range(2):
                        H.lows(dve, n, h, QH ** -0.5, hide)
                    dve.tensor_copy(H.v[:, :, :].rearrange("p t (h c) -> p t h c", h=2), v_now).then_inc(H.v_staged, 1)
                    for h in range(2):
                        H.norm(dve, n, h)
                    split(nxt + (-1), 2)
                    if c == 0:
                        branch_b_lo(BH - 1)
                        dve.wait_ge(gate_done, layer(l, 6 * TOKS, 6 * TOKS).count(0))
                    for tok in range(TOKS):
                        W.wait_tile(dve, tok, layer(l, N2_AB + c, N2), nxt + (-3))
                        times_gate(tmp_rows[:, tok, :] if e else y_rows[:, tok, cols], slice(e * D + i * NT, e * D + (i + 1) * NT), tok)\
                            .then_inc(prod_free[tok], 1)
                    H.out_lo_part(dve, n, cT[1][:, c, :], cT[0][:, c, :])
                    if c == PAIRS - 1:
                        split(nxt + 1, 1)
                    if e:
                        dve.drain()
                        dve.tensor_tensor(y_rows[:, :, cols], y_rows[:, :, cols], tmp_rows, ALU.add)
                        dve.drain()
                for j in range(2):
                    split(layer(l, G2_O + 2 * j, G2), 1)
                    for tok in range(TOKS):
                        W.wait_tile(dve, tok, layer(l, N2_C + j, N2), layer(l, G2_C + 2 * j + 1, G2))
                        times_gate(tmp_rows[:, tok, :], slice(2 * D + j * NT, 2 * D + (j + 1) * NT), tok).then_inc(prod_free[tok], 1)
                    dve.drain()
                    for tok in range(TOKS):
                        y = y_rows[:, tok, j * NT:(j + 1) * NT]
                        dve.tensor_tensor(y, y, tmp_rows[:, tok, :], ALU.add).then_inc(merged, 1)
                    dve.drain()
                    split(layer(l, G2_O + 2 * j + 1, G2), 1)
                    for tok in range(TOKS):
                        place = lambda p: p[:, 4 * j:4 * j + 4, tok * P:(tok + 1) * P]
                        T.take_lo(dve, layer(l, F2_M + 2 * j + tok, F2), layer(l, S2_M + 2 * j + tok, S2), place(uT[1]), place(uT[0]),
                                  scale=0.5, view=four)
                for j in range(2):
                    split(layer(l, G2_O + 4 + 4 * j, G2), 3)
                    for tok in range(TOKS):
                        W.wait_tile(dve, tok, layer(l, N2_O + j, N2), layer(l, G2_O + 4 * j + 3, G2))
                        x = x_res[:, tok, j * NT:(j + 1) * NT]
                        dve.tensor_tensor(x, x, prod[tok][:, :], ALU.add).then_inc(prod_free[tok], 1)
                        dve.drain().then_inc(x_halves, 1)
                    if j == 0:
                        split(layer(l, G2_O + 7, G2), 1)
                x_norm(layer(l, 1, 2), u2_rows, ffn_g, u2_ready)
                dve.drain().then_inc(vec_free, 1)
                split(layer(l, G2_FF + 3, G2), 1)
                for n in range(4):
                    place = lambda p: p[:, 4 * (n % 2):4 * (n % 2) + 4, n // 2 * P:(n // 2 + 1) * P]
                    T.take_lo(dve, layer(l, F2_U2 + n, F2), layer(l, S2_U2 + n, S2), place(uT[1]), place(uT[0]), view=four)

                def take_hidden(fill, split_n, out):
                    for tok in range(TOKS):
                        place = lambda p: p[:, 0:2, tok * P:(tok + 1) * P]
                        T.take_lo(dve, fill + tok, split_n + tok, place(out[1]), place(out[0]), cols=SEQ, scale=0.5, view=two)

                def gated(tile, last_group, n):
                    for tok in range(TOKS):
                        dve.wait_ge(act_done, n.count(tok + 1))
                        dve.scalar_tensor_tensor(act_rows[:, tok, :], act_rows[:, tok, :], 1.0, prod[tok][:, 0:HT],
                                                 ALU.add, ALU.mult)
                    dve.drain()
                    for tok in range(TOKS):
                        dve.tensor_tensor(hid_rows[:, tok, :], act_rows[:, tok, :], prod[tok][:, HT:NT], ALU.mult)\
                           .then_inc(prod_free[tok], 1)

                gated(layer(l, N2_FF, N2), layer(l, G2_FF + 3, G2), layer(l, 0, TOKS * HTILES))
                split(layer(l, G2_FF + 4, G2), 2)
                with dve.Fori(0, HTILES // 2) as i:
                    for e in range(2):
                        at = Pos(G2_FF + 4 + 6 * e, (l, G2), (i, 12))
                        split(at + 2, 2)
                        take_hidden(Pos(F2_H + 2 * e, (l, F2), (i, 4)), Pos(S2_H + 2 * e, (l, S2), (i, 4)), (aT, bT)[e])
                        split(at + 4, 2)
                        gated(Pos(N2_FF + 1 + e, (l, N2), (i, 2)), at + 3, Pos(TOKS * (1 + e), (l, TOKS * HTILES), (i, 2 * TOKS)))
                        split(at + 6, 2)
                take_hidden(layer(l, F2 - 2, F2), layer(l, S2 - 2, S2), aT)
                for j in range(2):
                    dve.wait_ge(W.used, layer(l, G2 - 2 + j, G2).count(RING + 1))
                    for tok in range(TOKS):
                        x = x_res[:, tok, j * NT:(j + 1) * NT]
                        dve.tensor_tensor(x, x, acc[2 * j + tok][:, :], ALU.add).then_inc(x_halves, 1)
            dve.wait_ge(mix_in, 16 * (LAYERS + 1))
            x_norm(Pos(2 * LAYERS), x_res, mix_g)

        @block.tensor
        def _(pe):
            outs = lambda width: [prod[tok][:, 0:width] for tok in range(TOKS)]

            def vacated(tile_n):
                return lambda tok: pe.wait_ge(prod_free[tok], tile_n.count(1))

            def tile(pos, tile_n, lhs, k0, groups, width=NT):
                for g in range(groups):
                    W.multiply(pe, pos + g, lhs, k0 + KG * g, width, KG, outs(width), g == 0, g == groups - 1,
                               vacant=vacated(tile_n) if g == 0 else None)

            def rows_turn(pos, rows, chunk0, n=4):
                T.turn(pe, pos, [(P, slice(c * P, (c + 1) * P), rows[:, (chunk0 + c) * P:(chunk0 + c + 1) * P])
                                 for c in range(n)])

            def qk_turns(n, fill):
                pe.wait_ge(H.staged, n.count(1))
                rows = H.qk[:, 0:TOKS * 2 * P].rearrange("p (t x c) -> p t x c", t=TOKS, x=2)
                for x in range(2):
                    T.turn(pe, fill + x, [(P, slice(tok * P, (tok + 1) * P), rows[:, tok, x, :]) for tok in range(TOKS)])

            pe.wait_ge(consts_in, 16 * 5)
            pe.matmul(prod[0][0:AH + BH, 0:REL], bias_tab[:, :], bias_one[:, :], start=True, stop=True).then_inc(rows_ready, 1)
            pe.wait_ge(rows_copied, 1)
            pe.wait_ge(bias_in, 16)
            for b, flipped in enumerate(prod + acc):
                for h in range(2):
                    mm = pe.matmul(flipped[:, h * SEQ:(h + 1) * SEQ], flip, bias_flipped[:, 2 * b + h, :], start=True, stop=True)
                mm.then_inc(bias_turned, 1)
            with pe.Fori(0, LAYERS) as l:
                for n in range(4):
                    pe.wait_ge(h_ready, layer(l, n // 2, TOKS).count(1))
                    rows_turn(layer(l, n, F2), h_rows[:, n // 2, :], 4 * (n % 2))
                with pe.Fori(0, IN2_T) as t:
                    for n in range(2, 4):
                        T.taken(pe, layer(l, n, F2))
                    tile(Pos(0, (l, G2), (t, 4)), Pos(0, (l, N2), (t, 1)), uT, 0, 4, IN2_W)
                for n in range(4):
                    pe.wait_ge(lat_ready, layer(l, n // 2, TOKS).count(1))
                    rows_turn(layer(l, F2_LAT + n, F2), proj[:, n // 2, CQ:KR], 4 * (n % 2))
                for n in range(2, 4):
                    T.taken(pe, layer(l, F2_LAT + n, F2))
                for j in range(2):
                    for g, (lhs, k0) in enumerate(((aT, 0), (aT, 2), (bT, 0))):
                        W.multiply(pe, layer(l, G2_UQ + 3 * j + g, G2), lhs, k0, UQ_W, KG, outs(UQ_W), g == 0, g == 2,
                                   vacant=vacated(layer(l, N2_UQ + j, N2)) if g == 0 else None)
                for j in range(2):
                    for g in range(2):
                        W.multiply(pe, layer(l, G2_UKV + 2 * j + g, G2), bT, 2 + g, NT, 1, outs(NT), g == 0, g == 1,
                                   vacant=vacated(layer(l, N2_UKV + j, N2)) if g == 0 else None)
                qk_turns(pair(l, 0), qk_turn(l, 0))
                with pe.Fori(0, PAIRS) as t:
                    n, fill = pair(l, 0, (t, 1)), Pos(F2_A, (l, F2), (t, 2))
                    this = Pos(G2_GATE, (l, G2), (t, 4))
                    H.scores(pe, n, T, fill, True)
                    W.multiply(pe, this, uT, 0, NT, KG, outs(NT), True, False, vacant=vacated(gate_tile(l, 0, (t, 1))))
                    W.multiply(pe, this + 1, uT, 2, NT, KG, outs(NT), False, False)
                    qk_turns(n + 1, fill + 2)
                    W.multiply(pe, this + 2, uT, 4, NT, KG, outs(NT), False, False)
                    W.multiply(pe, this + 3, uT, 6, NT, KG, outs(NT), False, True)
                    for h in range(2):
                        H.turn(pe, n, h, ident)
                    H.mix(pe, n)

                def row_turns(m):
                    pe.wait_ge(H.staged, pair(l, m).count(1))
                    qk = H.qk[:, :].rearrange("p (t h x c) -> p t h x c", t=TOKS, h=2, x=2)
                    for h in range(2):
                        T.turn(pe, qk_turn(l, m) + h, [(QH, slice(x * SEQ + tok * P, x * SEQ + (tok + 1) * P), qk[:, tok, h, x, :])
                                                       for x in range(2) for tok in range(TOKS)])

                def branch_b_turn(b):
                    pe.wait_ge(H.out_done, pair(l, PAIRS + b).count(2))
                    T.turn(pe, out_turn(l, b), [(P, slice(tok * P, (tok + 1) * P), yb_rows[:, tok, :]) for tok in range(TOKS)])

                for b in range(BH):
                    m, e = PAIRS + b, b % 2
                    n, this = pair(l, m), layer(l, G2_GATE + 16 + 2 * b, G2)
                    H.scores(pe, n, T, qk_turn(l, m), True)
                    W.multiply(pe, this, uT, 4 * e, NT, KG, outs(NT), e == 0, False,
                               vacant=vacated(gate_tile(l, 4 + b // 2)) if e == 0 else None)
                    if b < BH - 1:
                        qk_turns(n + 1, qk_turn(l, m + 1))
                    else:
                        row_turns(m + 1)
                    if b > 0:
                        branch_b_turn(b - 1)
                    W.multiply(pe, this + 1, uT, 4 * e + 2, NT, KG, outs(NT), False, e == 1)
                    pe.wait_ge(H.p_ready, twice(n, 1).count(1))
                    pe.wait_ge(H.out_done, n.count(1))
                    for k in range(3):
                        turned = pe.transpose(H.T[0][:, k * P:(k + 1) * P], H.p[0][:, k * P:(k + 1) * P], ident)
                    turned.then_inc(H.pT_full, 2)
                    pe.wait_ge(H.pT_ready, twice(n, 1).count(1))
                    pe.wait_ge(H.v_staged, n.count(1))
                    o = [H.T[1][:, tok * P:(tok + 1) * P] for tok in range(TOKS)]
                    pe.matmul(o[0], H.pT[0][:, 0:P], H.v[:, 0, :], start=True, stop=True)
                    pe.matmul(o[1], H.pT[0][:, P:2 * P], H.v[:, 0, :], start=True, stop=False)
                    pe.matmul(o[1], H.pT[0][:, 2 * P:3 * P], H.v[:, 1, :], start=False, stop=True).then_inc(H.out_full, 1)
                for c in range(PAIRS):
                    m, lhs = PAIRS + BH + c, (aT, bT)[c % 2]
                    n, this = pair(l, m), layer(l, G2_AB + 2 * c, G2)
                    H.scores(pe, n, T, qk_turn(l, m), False)
                    if c == 1:
                        T.taken(pe, out_turn(l, BH - 1))
                    W.multiply(pe, this, lhs, 0, NT, KG, outs(NT), True, False, vacant=vacated(layer(l, N2_AB + c, N2)))
                    if c < PAIRS - 1:
                        row_turns(m + 1)
                    if c == 0:
                        branch_b_turn(BH - 1)
                    W.multiply(pe, this + 1, lhs, 2, NT, KG, outs(NT), False, True)
                    for h in range(2):
                        H.turn(pe, n, h, ident)
                    H.mix(pe, n)
                pe.wait_ge(H.out_done, pair(l, PER - 1).count(2))
                def merged_turns(j):
                    for tok in range(TOKS):
                        pe.wait_ge(merged, layer(l, 2 * j + tok, 4).count(1))
                        rows_turn(layer(l, F2_M + 2 * j + tok, F2), y_rows[:, tok, :], 4 * j)

                tile(layer(l, G2_C, G2), layer(l, N2_C, N2), cT, 0, 2)
                W.multiply(pe, layer(l, G2_C + 2, G2), cT, 0, NT, KG, outs(NT), True, False, vacant=vacated(layer(l, N2_C + 1, N2)))
                merged_turns(0)
                W.multiply(pe, layer(l, G2_C + 3, G2), cT, 2, NT, KG, outs(NT), False, True)
                for j in range(2):
                    for g in range(4):
                        if j == 0 and g == 2:
                            merged_turns(1)
                        if j == 0 and g % 2 == 0:
                            for tok in range(TOKS):
                                T.taken(pe, layer(l, F2_M + g + tok, F2))
                        W.multiply(pe, layer(l, G2_O + 4 * j + g, G2), uT, KG * g, NT, KG, outs(NT), g == 0, g == 3,
                                   vacant=vacated(layer(l, N2_O + j, N2)) if g == 0 else None)
                for n in range(4):
                    pe.wait_ge(u2_ready, layer(l, n // 2, TOKS).count(1))
                    rows_turn(layer(l, F2_U2 + n, F2), u2_rows[:, n // 2, :], 4 * (n % 2))
                for n in range(2, 4):
                    T.taken(pe, layer(l, F2_U2 + n, F2))

                def hidden_turn(tile_n, fill):
                    for tok in range(TOKS):
                        pe.wait_ge(prod_free[tok], tile_n.count(2))
                        rows_turn(fill + tok, hid_rows[:, tok, :], 0, 2)

                def down(pos, lhs, fill, first, last):
                    for tok in range(TOKS):
                        T.taken(pe, fill + tok)
                    for j in range(2):
                        W.multiply(pe, pos + j, lhs, 0, NT, KG, [acc[2 * j + tok][:, :] for tok in range(TOKS)],
                                   first, last, tile_end=False)

                def step(at, tile_n, fill, lhs, first):
                    W.multiply(pe, at, uT, 0, NT, KG, outs(NT), True, False, vacant=vacated(tile_n))
                    W.multiply(pe, at + 1, uT, 2, NT, KG, outs(NT), False, False)
                    hidden_turn(tile_n + (-1), fill)
                    W.multiply(pe, at + 2, uT, 4, NT, KG, outs(NT), False, False)
                    W.multiply(pe, at + 3, uT, 6, NT, KG, outs(NT), False, True)
                    down(at + 4, lhs, fill, first, False)

                tile(layer(l, G2_FF, G2), layer(l, N2_FF, N2), uT, 0, 4)
                for e in range(2):
                    step(layer(l, G2_FF + 4 + 6 * e, G2), layer(l, N2_FF + 1 + e, N2), layer(l, F2_H + 2 * e, F2),
                         (aT, bT)[e], e == 0)
                with pe.Fori(1, HTILES // 2) as i:
                    for e in range(2):
                        step(Pos(G2_FF + 4 + 6 * e, (l, G2), (i, 12)), Pos(N2_FF + 1 + e, (l, N2), (i, 2)),
                             Pos(F2_H + 2 * e, (l, F2), (i, 4)), (aT, bT)[e], False)
                hidden_turn(layer(l, N2 - 1, N2), layer(l, F2 - 2, F2))
                down(layer(l, G2 - 2, G2), aT, layer(l, F2 - 2, F2), False, True)



def program(nc, dr, out, scratch, blocks=(1, 2)):
    with ExitStack() as ctx:
        sb = lambda n, s, dt=F32: ctx.enter_context(nc.sbuf_tensor(n, s, dt))
        x_res = sb("x_res", [P, TOKS, D])
        ident, hide = sb("ident", [P, P]), sb("hide", [P, TRI])
        ones, small = sb("ones", [P, P]), sb("small", [P, 3, 4])
        consts_in, filled = ctx.enter_context(nc.semaphore("consts_in")), ctx.enter_context(nc.semaphore("filled"))
        with nc.Block() as block:
            @block.sync
            def _(sp):
                sp.dma_start(x_res[:, :, :], dr["x"].rearrange("a (t p) d -> p (a t) d", p=P)).then_inc(consts_in, 16)
                sp.dma_start(ident[:, :], dr["identity"]).then_inc(consts_in, 16)
                sp.dma_start(hide[:, :], dr["causal"]).then_inc(consts_in, 16)
                sp.wait_ge(consts_in, 48)
                sp.wait_ge(filled, 1)

            @block.vector
            def _(dve):
                dve.memset(ones[:, :], 1.0)
                for n, value in enumerate((LN_EPS, RMS_EPS, -0.5)):
                    dve.memset(small[:, n, :], value)
                dve.drain().then_inc(filled, 1)

        if 1 in blocks:
            first_block(nc, dr, x_res, ident[:, :], hide[:, :], ones, small)
        if 2 in blocks:
            second_block(nc, dr, scratch, x_res, ident[:, :], hide[:, :], ones, small)
        out_done = ctx.enter_context(nc.semaphore("out_done"))
        with nc.Block() as block:
            @block.sync
            def _(sp):
                sp.dma_start(out.rearrange("a (t p) d -> p (a t) d", p=P), x_res[:, :, :]).then_inc(out_done, 16)
                sp.wait_ge(out_done, 16)


def shape_constants():
    pos = np.arange(SEQ)
    keys = np.concatenate([np.arange(P), np.arange(SEQ)])
    queries = np.arange(P)[:, None] + np.repeat([0, P], [P, SEQ])[None, :]
    dist = SEQ - 1 - np.arange(REL)
    far = np.log(np.maximum(dist, 1).astype(np.float32) / 16) / np.float32(np.log(128.0)) * 16
    bucket = np.where(dist < 16, np.maximum(dist, 0), np.minimum(16 + far.astype(np.int32), BUCKETS - 1))
    past = dist >= 0
    patterns = ((dist <= P) & past).astype(int) + ((dist % 4 == 0) & past) + ((dist % 16 == 0) & past)
    rows = np.zeros((BUCKETS + 2, REL), np.float32)
    rows[bucket[past], np.arange(REL)[past]] = -1.0
    rows[BUCKETS] = np.where(patterns > 0, -np.log(np.maximum(patterns, 1)), BIG)
    rows[BUCKETS + 1] = np.where(past, 0.0, BIG)
    kinds = np.zeros((2, AH + BH), np.float32)
    kinds[0, :AH], kinds[1, AH:] = 1.0, 1.0
    lam_init = [0.8 - 0.6 * np.exp(-0.3 * l) for l in range(LAYERS)]
    theta = lambda base, n: (base ** (-np.arange(0, n, 2, dtype=np.float32) / n)).astype(np.float32)
    angles = pos.astype(np.float32)[:, None] * theta(np.float32(10000.0), ROPE)[None, :]
    return {
        "flip": np.eye(P, dtype=np.float32)[::-1],
        "bias_rows": rows,
        "bias_kinds": kinds,
        "trig_2": np.concatenate([np.cos(angles), np.sin(angles)], 1).astype(np.float32),
        "lam_const": np.array([[-x, 1.0 - x] for x in lam_init], np.float32),
        "identity": np.eye(P, dtype=np.float32),
        "causal": np.where(keys[None, :] <= queries, 0.0, BIG).astype(np.float32),
        "inv_freq": theta(np.float32(500000.0), ROT)[None, :],
    }


def kernel(**inputs):
    import concourse.bacc as _bacc
    from concourse.bass_utils import run_bass_kernel_spmd as _run

    nc = _bacc.Bacc("TRN2", target_bir_lowering=False, num_devices=1)
    arrays, dr = {}, {}
    for name, value in {**inputs, **shape_constants()}.items():
        a = np.ascontiguousarray(value)
        arrays[f"in_{name}_dram"] = a
        dr[name] = nc.dram_tensor(f"in_{name}_dram", a.shape, mybir.dt.from_np(a.dtype), kind="ExternalInput").ap()
    out = nc.dram_tensor("out_0_dram", (1, SEQ, D), F32, kind="ExternalOutput").ap()
    scratch = nc.dram_tensor("bias_rows_dram", (AH + BH, REL), F32, kind="Internal").ap()
    program(nc, dr, out, scratch)
    r = _run(nc, [arrays], core_ids=[0])
    return r.results[0]["out_0_dram"]
```

```python
from contextlib import ExitStack

import concourse.bass as bass
import numpy as np
from concourse import mybir

F32 = mybir.dt.float32
F32R = mybir.dt.float32r
I32 = mybir.dt.int32
ALU = mybir.AluOpType
ACT = mybir.ActivationFunctionType
AX = mybir.AxisListType.X

P = 128
SEQ = 256
TOKS = SEQ // P
D = 1024
DC = D // P
LAYERS = 2
NT = 512
KG = 2
RING = 4
HEADS, HD = 8, 64
AW = HEADS * HD
CONV_K = 31
CW = D // 2
FF1 = 4 * D
IN1 = 3 * AW + 2 * CW + 2 * D
ROT = HD // 4
RH = ROT // 2
ALPHA = (2 * LAYERS) ** 0.25
LN_EPS = 1e-5
RMS_EPS = 1e-6
BIG = 1e30
OUT_ORDER = [(j, g) for h in range(2) for j in range(2) for g in (2 * h, 2 * h + 1)]
OUT_LAST = (5, 7)
TRI = 3 * P

IN2 = 4128
IN2_W, IN2_T = 344, 12
QR, KVR = 768, 256
NOPE, ROPE, CV = 64, 32, 64
QH = NOPE + ROPE
FF2 = 2816
HT = 256
BUCKETS, AH, BH = 32, 8, 4
REL = SEQ + P


class Pos:

    def __init__(self, k, *regs):
        self.k, self.regs = k, regs

    def __add__(self, j):
        return Pos(self.k + j, *self.regs)

    def over(self, n):
        assert all(step % n == 0 for _, step in self.regs)
        return Pos(self.k // n, *((r, step // n) for r, step in self.regs))

    def slot(self, n):
        assert all(step % n == 0 for _, step in self.regs)
        return self.k % n

    def count(self, extra=0, times=1):
        value = (self.k + extra) * times
        for r, step in self.regs:
            value = r * (step * times) + value
        return value


def twice(n, h=0):
    return Pos(2 * n.k + h, *((r, 2 * s) for r, s in n.regs))


def settle(eng, passed):
    eng.sem_inc(passed, 1)


class Weights:

    def __init__(self, nc, ctx, tag, dmas):
        sb = lambda n, dt: ctx.enter_context(nc.sbuf_tensor(f"{n}_{tag}", [P, RING, KG * NT], dt))
        sem = lambda n: ctx.enter_context(nc.semaphore(f"{n}_{tag}"))
        self.raw, self.hi, self.lo = sb("w_raw", F32), sb("w_hi", F32R), sb("w_lo", F32R)
        self.raw_in = [sem(f"w_raw_in{s}") for s in range(RING)]
        self.hi_done, self.lo_done, self.used = sem("w_hi_done"), sem("w_lo_done"), sem("w_used")
        self.tile0_done = sem("tile0_done")
        self.dmas = dmas

    def load(self, sp, pos, *parts):
        s = pos.slot(RING)
        assert len(parts) == self.dmas
        sp.wait_ge(self.lo_done, pos.count(1))
        for place, src in parts:
            sp.dma_start(place(self.raw[:, s, :]), src).then_inc(self.raw_in[s], 16)

    def split_hi(self, act, pos, cols=KG * NT):
        s = pos.slot(RING)
        act.wait_ge(self.raw_in[s], pos.over(RING).count(1, 16 * self.dmas))
        act.wait_ge(self.used, pos.count(1))
        act.copy(self.hi[:, s, 0:cols], self.raw[:, s, 0:cols]).then_inc(self.hi_done, 1)

    def split_lo(self, dve, pos, cols=KG * NT):
        s = pos.slot(RING)
        dve.wait_ge(self.hi_done, pos.count(1))
        dve.tensor_tensor(self.lo[:, s, 0:cols], self.raw[:, s, 0:cols], self.hi[:, s, 0:cols].bitcast(F32),
                          ALU.subtract).then_inc(self.lo_done, 1)

    def multiply(self, pe, pos, lhs, k0, width, chunks, outs, first, last, tile_end=True,
                 vacant=None, between=None):
        s = pos.slot(RING)
        lhs_hi, lhs_lo = lhs
        pe.wait_ge(self.lo_done, pos.count(RING + 1))
        for tok, out in enumerate(outs):
            if vacant:
                vacant(tok)
            for c in range(chunks):
                a_hi = lhs_hi[:, k0 + c, tok * P:(tok + 1) * P]
                a_lo = lhs_lo[:, k0 + c, tok * P:(tok + 1) * P]
                w_hi = self.hi[:, s, c * width:(c + 1) * width]
                w_lo = self.lo[:, s, c * width:(c + 1) * width]
                pe.matmul(out, a_hi, w_hi, start=first and c == 0, stop=False)
                pe.matmul(out, a_hi, w_lo, start=False, stop=False)
                mm = pe.matmul(out, a_lo, w_hi, start=False, stop=last and c == chunks - 1)
            if last and tile_end and tok == 0:
                mm.then_inc(self.tile0_done, 1)
            if between and tok == 0:
                between()
        mm.then_inc(self.used, 1)

    def wait_tile(self, eng, tok, tile, last_group):
        if tok == 0:
            eng.wait_ge(self.tile0_done, tile.count(1))
        else:
            eng.wait_ge(self.used, last_group.count(RING + 1))


class Turns:

    def __init__(self, nc, ctx, tag, ident):
        self.bank = [ctx.enter_context(nc.psum_tensor(f"turn{b}_{tag}", [P, NT], F32)) for b in range(2)]
        sem = lambda n: ctx.enter_context(nc.semaphore(f"{n}_{tag}"))
        self.full = sem("turn_full")
        self.hi = sem("turn_hi")
        self.free = [sem(f"turn_free{b}") for b in range(2)]
        self.ident = ident

    def turn(self, pe, pos, parts):
        b = pos.slot(2)
        pe.wait_ge(self.free[b], pos.over(2).count(1))
        for rows, cols, src in parts:
            k = src.shape[0]
            if k == P:
                t = pe.transpose(self.bank[b][0:rows, cols], src, self.ident)
            else:
                t = pe.matmul(self.bank[b][0:rows, cols], src, self.ident[0:k, 0:k], start=True, stop=True)
        t.then_inc(self.full, 1)

    def taken(self, eng, pos):
        eng.wait_ge(self.free[pos.slot(2)], pos.over(2).count(2))

    def take(self, act, pos, out, rows=P, cols=NT, scale=1.0, view=None):
        b = pos.slot(2)
        act.wait_ge(self.full, pos.count(1))
        src = self.bank[b][0:rows, 0:cols]
        return act.activation(out, view(src) if view else src, ACT.Copy, scale=scale).then_inc(self.free[b], 1)

    def take_hi(self, act, pos, out, cols=NT, scale=1.0, view=None):
        b = pos.slot(2)
        act.wait_ge(self.full, pos.count(1))
        src = self.bank[b][:, 0:cols]
        act.activation(out, view(src) if view else src, ACT.Copy, scale=scale).then_inc(self.hi, 1)

    def take_lo(self, dve, pos, split, out, hi, cols=NT, scale=1.0, view=None):
        b = pos.slot(2)
        dve.wait_ge(self.hi, split.count(1))
        src = self.bank[b][:, 0:cols]
        dve.scalar_tensor_tensor(out, view(src) if view else src, scale, hi.bitcast(F32),
                                 ALU.mult, ALU.subtract).then_inc(self.free[b], 1)


class Heads:

    def __init__(self, nc, ctx, tag, score_banks, turn_banks):
        sb = lambda n, s: ctx.enter_context(nc.sbuf_tensor(f"{n}_{tag}", s, F32))
        sem = lambda n: ctx.enter_context(nc.semaphore(f"{n}_{tag}"))
        self.qk = sb("qk_rows", [P, TOKS * 4 * QH])
        self.v = sb("v_rows", [P, TOKS, P])
        self.qkT = sb("qkT", [P, 2, 2 * SEQ])
        self.s = [sb(f"scores{h}", [P, TRI]) for h in range(2)]
        self.p = [sb(f"probs{h}", [P, TRI]) for h in range(2)]
        self.pT = [sb(f"probsT{h}", [P, TRI]) for h in range(2)]
        self.low = sb("low", [P, 2, 4])
        self.sum = sb("expsum", [P, 2, 2])
        self.inv = sb("expinv", [P, 2, 2])
        self.S, self.T = score_banks, turn_banks
        self.staged, self.v_staged, self.scored = sem("qk_staged"), sem("v_staged"), sem("scored")
        self.low_ready, self.exp_done, self.p_ready = sem("low_ready"), sem("exp_done"), sem("p_ready")
        self.pT_full, self.pT_ready = sem("pT_full"), sem("pT_ready")
        self.out_full, self.out_hi, self.out_done = sem("o_full"), sem("o_hi"), sem("o_done")

    def scores(self, pe, n, turns, turn, packed):
        turns.taken(pe, turn)
        turns.taken(pe, turn + 1)
        for h in range(2):
            if packed:
                q, k = (self.qkT[h * HD:(h + 1) * HD, x, 0:SEQ] for x in range(2))
            else:
                q, k = (self.qkT[0:QH, h, x * SEQ:(x + 1) * SEQ] for x in range(2))
            pe.matmul(self.S[h][:, 0:P], q[:, 0:P], k[:, 0:P], start=True, stop=True)
            mm = pe.matmul(self.S[h][:, P:TRI], q[:, P:SEQ], k[:, 0:SEQ], start=True, stop=True)
        mm.then_inc(self.scored, 1)

    def lows(self, dve, n, h, scale, bias):
        dve.wait_ge(self.scored, n.count(1))
        dve.scalar_tensor_tensor(self.s[h][:, :], self.S[h][:, 0:TRI], -scale, bias, ALU.mult, ALU.add)
        dve.drain()
        dve.tensor_reduce(self.low[:, h, 0:3], self.s[h][:, :].rearrange("p (b k) -> p b k", b=3), AX, ALU.min)
        dve.drain()
        dve.tensor_tensor(self.low[:, h, 3:4], self.low[:, h, 1:2], self.low[:, h, 2:3], ALU.min)\
           .then_inc(self.low_ready, 1)

    def exps(self, act, n, h):
        act.wait_ge(self.low_ready, twice(n, h).count(1))
        act.activation(self.p[h][:, 0:P], self.s[h][:, 0:P], ACT.Exp, bias=self.low[:, h, 0:1], scale=-1.0,
                       accum_out=self.sum[:, h, 0:1])
        act.activation(self.p[h][:, P:TRI], self.s[h][:, P:TRI], ACT.Exp, bias=self.low[:, h, 3:4], scale=-1.0,
                       accum_out=self.sum[:, h, 1:2]).then_inc(self.exp_done, 1)

    def norm(self, dve, n, h):
        dve.wait_ge(self.exp_done, twice(n, h).count(1))
        dve.reciprocal(self.inv[:, h, :], self.sum[:, h, :])
        dve.drain()
        dve.tensor_scalar(self.p[h][:, 0:P], self.p[h][:, 0:P], self.inv[:, h, 0:1], None, ALU.mult)
        dve.tensor_scalar(self.p[h][:, P:TRI], self.p[h][:, P:TRI], self.inv[:, h, 1:2], None, ALU.mult)\
           .then_inc(self.p_ready, 1)

    def turn(self, pe, n, h, ident):
        if h == 0:
            pe.wait_ge(self.out_done, n.count(1))
        pe.wait_ge(self.p_ready, twice(n, h).count(1))
        for b in range(3):
            t = pe.transpose(self.T[h][:, b * P:(b + 1) * P], self.p[h][:, b * P:(b + 1) * P], ident)
        t.then_inc(self.pT_full, 1)

    def take(self, act, n, h):
        act.wait_ge(self.pT_full, twice(n, h).count(1))
        act.copy(self.pT[h][:, :], self.T[h][:, 0:TRI]).then_inc(self.pT_ready, 1)

    def mix(self, pe, n):
        pe.wait_ge(self.pT_ready, twice(n, 1).count(1))
        pe.wait_ge(self.v_staged, n.count(1))
        for h in range(2):
            o = self.T[0][h * HD:(h + 1) * HD, :]
            v = self.v[:, :, h * HD:(h + 1) * HD]
            pe.matmul(o[:, 0:SEQ], v[:, 0, :], self.pT[h][:, 0:SEQ], start=True, stop=False)
            mm = pe.matmul(o[:, P:SEQ], v[:, 1, :], self.pT[h][:, SEQ:TRI], start=False, stop=True)
        mm.then_inc(self.out_full, 1)

    def out_hi_part(self, act, n, out):
        act.wait_ge(self.out_full, n.count(1))
        act.copy(out, self.T[0][:, 0:SEQ]).then_inc(self.out_hi, 1)

    def out_lo_part(self, dve, n, out, hi):
        dve.wait_ge(self.out_hi, n.count(1))
        dve.tensor_tensor(out, self.T[0][:, 0:SEQ], hi.bitcast(F32), ALU.subtract).then_inc(self.out_done, 1)


def rope(dve, rows, cos, sin, half, tmp):
    x1, x2 = rows[..., 0:half], rows[..., half:2 * half]
    a, b, c, d = tmp
    dve.tensor_tensor(a, x1, cos, ALU.mult)
    dve.tensor_tensor(b, x2, sin, ALU.mult)
    dve.tensor_tensor(c, x2, cos, ALU.mult)
    dve.tensor_tensor(d, x1, sin, ALU.mult)
    dve.drain()
    dve.tensor_tensor(x1, a, b, ALU.subtract)
    dve.tensor_tensor(x2, c, d, ALU.add)
    dve.drain()



T_IN, T_FF = IN1 // NT, FF1 // NT
Q0, K0, V0, A0, G0 = (n * AW for n in range(5))
GA0 = 5 * AW
GC0 = GA0 + D
PAIRS = HEADS // 2
G_IN, G_SQ, G_HALF = T_IN * 4, 8, 4
G1 = G_IN + 2 * G_HALF + G_SQ + T_FF * 8
N_TILES = T_IN + 2 + 2 + 2 + T_FF
F_U, F_W, F_PAIR = 0, 4, 6
F_CONV = F_PAIR + 4 * PAIRS
F_M = F_CONV + 2
F_U2 = F_M + 4
F_H = F_U2 + 4
F_ALL = F_H + 2 * T_FF
S_U, S_CONV, S_M, S_U2, S_H = 0, 4, 6, 10, 14
S_ALL = S_H + 2 * T_FF
TWO_PI_PARTS = (6.28125, 0.0019340515136718750, 1.2556659146e-06)
MAGIC = 12582912.0
PI_BELOW = 3.1415925


def first_block(nc, dr, x_res, ident, hide, ones, small, load_constants, consts_in, bias_rows):
    ctx = ExitStack()
    with ctx:
        sb = lambda n, s, dt=F32: ctx.enter_context(nc.sbuf_tensor(n, s, dt))
        sem = lambda n: ctx.enter_context(nc.semaphore(n))
        bank = lambda n: ctx.enter_context(nc.psum_tensor(n, [P, NT], F32))

        W = Weights(nc, ctx, "a", 1)
        prod = [bank(f"prod{t}_a") for t in range(TOKS)]
        acc = [bank(f"acc{n}_a") for n in range(4)]
        T = Turns(nc, ctx, "a", ident)
        H = Heads(nc, ctx, "a", acc[0:2], acc[2:4])

        uT = (sb("uT_hi", [P, DC, SEQ], F32R), sb("uT_lo", [P, DC, SEQ], F32R))
        aT = (sb("aT_hi", [P, 4, SEQ], F32R), sb("aT_lo", [P, 4, SEQ], F32R))
        cT = tuple(part[:, 4:8, :] for part in uT)
        proj = sb("proj", [P, TOKS, IN1])
        u_rows, y_rows = proj[:, :, 0:D], proj[:, :, 0:D]
        u2_rows, tmp_rows = proj[:, :, D:2 * D], proj[:, :, 2 * D:2 * D + NT]
        conv_tok, conv_sig = proj[:, :, A0:A0 + CW], proj[:, :, G0:G0 + CW]
        r_rows, h_rows = proj[:, :, 2 * D + NT:3 * D], proj[:, :, 3 * D:3 * D + NT]

        ada_raw = sb("ada_raw", [P, 4, D])
        ada_acc = proj[:, 0, 0:D]
        gate1_acc = proj[:, 1, GA0:GA0 + D]
        gate2_raw = proj[:, 1, 0:D]
        first_b = proj[0:1, 1, 0:LAYERS * 2 * D]
        bias_rows.lay(proj[:, 0, D:2 * D])
        ada_b = sb("ada_b", [1, D])
        ada_first = sb("ada_first", [P, LAYERS, 2, D])
        ada_rest = sb("ada_rest", [P, 4, D])
        ln_vec = sb("ln_vec", [P, 2, D])
        cln_vec = ln_vec[:, 0, :].rearrange("p (n c) -> p n c", n=2)
        conv_rows = proj[0:CONV_K + 1, 0, GC0:GC0 + CW]
        conv_wT = sb("conv_wT", [P, 4, CONV_K + 1])
        conv_w = sb("conv_w", [P, CONV_K + 1])
        glu_rows = sb("glu_rows", [P, TOKS, P])
        hpad = sb("hpad", [P, CONV_K - 1 + SEQ])
        conv_acc = [sb(f"conv_acc{n}", [P, SEQ]) for n in range(2)]
        c_wide = sb("c_wide", [P, DC, P])
        c_col, c_act = sb("c_col", [P, DC]), sb("c_act", [P, DC])
        pos_i, pos_f = sb("pos_i", [P, TOKS], I32), sb("pos_f", [P, TOKS])
        freq = sb("freq", [P, RH])
        ang, turns_k = sb("ang", [P, 2, TOKS, RH]), sb("turns_k", [P, 2, TOKS, RH])
        trig = sb("trig", [P, 2, TOKS, RH])
        rope_tmp = [sb(f"rope_tmp{n}", [P, TOKS, HEADS, RH]) for n in range(4)]
        stats, mv = sb("stats", [P, TOKS, 2, 6]), sb("mv", [P, TOKS, 2])
        var_eps, rstd = sb("var_eps", [P, TOKS]), sb("rstd", [P, TOKS])
        mod2 = ada_rest[:, 1:3, :].rearrange("p v n -> p (v n)")
        eps, half_neg = small[:, 0, 0:1], small[:, 2, 0:1]

        ada_in = [sem(f"ada_in{s}") for s in range(4)]
        ada_used = [sem(f"ada_used{s}") for s in range(2)]
        first_b_in, ada_b_in = sem("first_b_in"), sem("ada_b_in")
        gate1_done = sem("gate1_done")
        gate2_in, gate2_used = sem("gate2_in"), sem("gate2_used")
        passed = sem("passed")
        ada_acc_done, ada_summed, ada_taken = sem("ada_acc_done"), sem("ada_summed"), sem("ada_taken")
        first_in, freq_in, c_tanh, c_ready = sem("first_in"), sem("freq_in"), sem("c_tanh"), sem("c_ready")
        ang_ready, trig_ready = sem("ang_ready"), sem("trig_ready")
        vec_in, u_ready, u2_ready = sem("vec_in"), sem("u_ready"), sem("u2_ready")
        prod_free = [sem(f"prod_free{t}_a") for t in range(TOKS)]
        glu_staged = sem("glu_staged")
        conv_done, conv_mv, conv_rstd = sem("conv_done"), sem("conv_mv"), sem("conv_rstd")
        conv_y, conv_tanh, conv_ready = sem("conv_y"), sem("conv_tanh"), sem("conv_ready")
        merged, h_ready = sem("merged"), sem("h_ready")
        ln_stats, ln_rstd, x_normed, x_ready = sem("ln_stats"), sem("ln_rstd"), sem("x_normed"), sem("x_ready")

        ADA_N, ADA_FILLS = LAYERS * 2, LAYERS * 2 * DC
        SUMS, FILLS = 6, 2 * DC + 4 * 4

        def layer(r, const, per):
            return Pos(const, (r, per))

        def in_pair(l, t, const, per, step):
            return Pos(const + step * t, (l, per)) if isinstance(t, int) else Pos(const, (l, per), (t, step))

        block = ctx.enter_context(nc.Block())

        @block.sync
        def _(sp):
            def ada_fill(n, used_n, l, rows, cols, width):
                chunks = (rows.size if isinstance(rows, bass.DynSlice) else rows.stop - rows.start) // P
                sp.wait_ge(ada_used[n.slot(2)], used_n.count(1))
                sp.dma_start(ada_raw[:, n.slot(4), 0:chunks * width].rearrange("p (k n) -> p k n", k=chunks),
                             dr["w_ada"][bass.ds(l, 1), rows, cols].rearrange("a (k p) n -> p (a k) n", p=P))\
                    .then_inc(ada_in[n.slot(4)], 16)

            def ada_bias(n, l, cols, width):
                sp.wait_ge(ada_summed, n.count(2))
                sp.dma_start(ada_b[:, 0:width], dr["b_ada"][bass.ds(l, 1), cols]).then_inc(ada_b_in, 16)

            def weights(pos, src, rows, col):
                W.load(sp, pos, (lambda place: place.rearrange("p (c n) -> p c n", c=KG),
                                 src[:, rows if not isinstance(rows, int) else slice(rows, rows + KG * P), col]
                                 .rearrange("a (c p) n -> p (a c) n", p=P)))

            sp.dma_start(c_col[:, :], dr["c"].rearrange("a (k p) -> p (a k)", p=P),
                         allow_slow_non_contiguous=True).then_inc(first_in, 16)
            sp.dma_start(pos_i[:, :], dr["positions"].rearrange("a (t p) -> p (a t)", p=P),
                         allow_slow_non_contiguous=True).then_inc(first_in, 16)
            sp.dma_start(freq[:, :], dr["inv_freq"].to_broadcast([P, RH])).then_inc(freq_in, 16)
            sp.dma_start(first_b.rearrange("p (l n) -> p l n", l=LAYERS),
                         dr["b_ada"].unsqueeze(0)[:, :, 0:2 * D]).then_inc(first_b_in, 16)
            bias_rows.load(sp)
            with sp.Fori(0, LAYERS) as l:
                for k in range(DC):
                    for v in range(2):
                        ada_fill(layer(l, 2 * k + v, 2 * DC), layer(l, k, DC), l, slice(k * P, (k + 1) * P),
                                 slice(v * D, (v + 1) * D), D)
            load_constants(sp)
            with sp.Fori(0, LAYERS) as l:
                ls = bass.ds(l, 1)
                w_in, w_up, w_down = dr["w_in"][ls], dr["w_up"][ls], dr["w_down"][ls]
                def in_tile(t, pos):
                    for g in range(4):
                        weights(pos + g, w_in, g * KG * P, bass.ds(t * NT, NT) if not isinstance(t, int)
                                else slice(t * NT, (t + 1) * NT))

                def ada_half(t, n, fill, used):
                    cols = bass.ds(t * NT + 3 * D, NT) if not isinstance(t, int) else slice(t * NT + 3 * D, t * NT + 3 * D + NT)
                    ada_bias(n, l, cols, NT)
                    for i in range(4):
                        ada_fill(fill + i, used + i // 2, l, slice(i * 2 * P, (i + 1) * 2 * P), cols, NT)

                in_tile(0, layer(l, 0, G1))
                with sp.Fori(0, 4) as t:
                    for i in range(4):
                        weights(Pos(4 + i, (l, G1), (t, 4)), w_in, i * KG * P, bass.ds(t * NT + NT, NT))
                        ada_fill(Pos(ADA_FILLS + i, (l, FILLS), (t, 4)), Pos(ADA_FILLS // 2 + i // 2, (l, FILLS // 2), (t, 2)),
                                 l, bass.ds(t * (2 * P) + i // 2 * P, P), slice(2 * D + i % 2 * NT, 2 * D + (i % 2 + 1) * NT), NT)
                ada_bias(layer(l, ADA_N, SUMS), l, slice(2 * D, 3 * D), D)
                in_tile(5, layer(l, 20, G1))
                with sp.Fori(0, PAIRS - 1) as t:
                    in_tile(t + (T_IN - PAIRS + 1), Pos(4 * (T_IN - PAIRS + 1), (l, G1), (t, 4)))
                    ada_half(t, Pos(ADA_N + 1, (l, SUMS), (t, 1)), Pos(ADA_FILLS + 16, (l, FILLS), (t, 4)),
                             Pos(ADA_FILLS // 2 + 8, (l, FILLS // 2), (t, 2)))
                at = G_IN
                for w, groups in ((dr["w_attn_br"][ls], 2), (dr["w_conv_pw"][ls], 2), (dr["w_out"][ls], 4)):
                    for t, g in [(t, g) for t in range(2) for g in range(2)] if groups == 2 else OUT_ORDER:
                        weights(layer(l, at, G1), w, g * KG * P, slice(t * NT, (t + 1) * NT))
                        at += 1
                    if at == G_IN + G_HALF:
                        ada_half(PAIRS - 1, layer(l, ADA_N + PAIRS, SUMS), layer(l, ADA_FILLS + 12 + 4 * PAIRS, FILLS),
                                 layer(l, ADA_FILLS // 2 + 6 + 2 * PAIRS, FILLS // 2))

                def up(f, pos):
                    for g in range(4):
                        weights(pos + g, w_up, g * KG * P, bass.ds(f * NT, NT) if not isinstance(f, int)
                                else slice(f * NT, (f + 1) * NT))

                def down(f, pos):
                    for t in range(2):
                        for g in range(2):
                            weights(pos + (2 * t + g), w_down, bass.ds(f * NT + g * KG * P, KG * P)
                                    if not isinstance(f, int) else f * NT + g * KG * P, slice(t * NT, (t + 1) * NT))

                def gate2_rows(rows, n):
                    sp.wait_ge(gate2_used, n.count(1))
                    sp.dma_start(gate2_raw, dr["w_ada"][ls, rows, 5 * D:6 * D].rearrange("a p n -> (a p) n")).then_inc(gate2_in, 16)

                up(0, layer(l, at, G1))
                ada_bias(layer(l, ADA_N + SUMS - 1, SUMS), l, slice(5 * D, 6 * D), D)
                with sp.Fori(0, T_FF - 1) as f:
                    up(f + 1, Pos(at + 4, (l, G1), (f, 8)))
                    sp.wait_ge(u2_ready, layer(l, TOKS - 1, TOKS).count(1))
                    gate2_rows(bass.ds(f * P, P), Pos(0, (l, T_FF), (f, 1)))
                    down(f, Pos(at + 8, (l, G1), (f, 8)))
                gate2_rows(slice((T_FF - 1) * P, T_FF * P), layer(l, T_FF - 1, T_FF))
                down(T_FF - 1, layer(l, at + 4 + 8 * (T_FF - 1), G1))

        @block.gpsimd
        def _(pool):
            def norm_rstd(n, ready, done, tok):
                pool.wait_ge(ready, n)
                pool.tensor_tensor(var_eps[:, tok:tok + 1], mv[:, tok, 1:2], eps, ALU.add)
                pool.drain()
                pool.tensor_tensor(rstd[:, tok:tok + 1], var_eps[:, tok:tok + 1], half_neg, ALU.pow).then_inc(done, 1)

            bias_rows.send(pool)
            with pool.Fori(0, LAYERS) as l:
                pool.wait_ge(x_ready, layer(l, 0, TOKS).count(1))
                settle(pool, passed)
                ls = bass.ds(l, 1)
                pool.dma_start(conv_rows[0:CONV_K, :], dr["conv_dw_w"][ls].rearrange("a k c -> (a k) c")).then_inc(vec_in, 16)
                pool.dma_start(conv_rows[CONV_K:CONV_K + 1, :], dr["conv_dw_b"][ls, :]).then_inc(vec_in, 16)
                for n, name in enumerate(("conv_ln_g", "conv_ln_b")):
                    pool.dma_start(cln_vec[:, n, :], dr[name][ls, :].to_broadcast([P, CW])).then_inc(vec_in, 16)
                for tok in range(TOKS):
                    norm_rstd(layer(l, tok, TOKS).count(1), conv_mv, conv_rstd, tok)
                pool.wait_ge(conv_y, layer(l, TOKS - 1, TOKS).count(1))
                settle(pool, passed)
                for n, name in enumerate(("ln_mix_g", "ln_mix_b")):
                    pool.dma_start(ln_vec[:, n, :], dr[name][ls, :].to_broadcast([P, D])).then_inc(vec_in, 16)
                for m in range(2):
                    if m == 1:
                        pool.wait_ge(x_normed, layer(l, 0, 1).count(1))
                        settle(pool, passed)
                        for n, name in enumerate(("ln_ffn_g", "ln_ffn_b")):
                            pool.dma_start(ln_vec[:, n, :], dr[name][ls, :].to_broadcast([P, D])).then_inc(vec_in, 16)
                    for tok in range(TOKS):
                        norm_rstd(layer(l, 2 * m + tok, 2 * TOKS).count(1), ln_stats, ln_rstd, tok)

        @block.scalar
        def _(act):
            def split(pos, n=4):
                for g in range(n):
                    W.split_hi(act, pos + g)

            def take_tile(tile, last_group, outs, func=ACT.Copy, scale=1.0, done=None):
                for tok, out in enumerate(outs):
                    W.wait_tile(act, tok, tile, last_group)
                    act.activation(out, prod[tok][:, :], func, scale=scale).then_inc(prod_free[tok], 1)

            def ada_take(n, out, banks):
                act.wait_ge(ada_summed, n.count(3))
                for h, bank in enumerate(banks):
                    a = act.copy(out[:, h * NT:(h + 1) * NT], bank[:, :])
                a.then_inc(ada_taken, 1)

            act.wait_ge(first_in, 32)
            act.activation(c_act[:, :], c_col[:, :], ACT.Tanh, scale=0.5).then_inc(c_tanh, 1)
            act.wait_ge(ang_ready, 1)
            act.activation(trig[:, :, :, :], ang[:, :, :, :], ACT.Sin).then_inc(trig_ready, 1)
            bias_rows.copy(act, prod[0])
            with act.Fori(0, LAYERS) as l:
                for n, v, banks in ((0, 1, acc[2:4]), (1, 0, acc[0:2])):
                    ada_take(layer(l, n, 2), ada_first[:, bass.ds(l, 1), v, :].rearrange("p a n -> p (a n)"), banks)

            with act.Fori(0, LAYERS) as l:
                split(layer(l, 0, G1))
                act.wait_ge(bias_rows.in_dram, 16)
                for n in range(4):
                    T.take_hi(act, layer(l, F_U + n, F_ALL),
                              uT[0][:, 4 * (n % 2):4 * (n % 2) + 4, n // 2 * P:(n // 2 + 1) * P],
                              view=lambda s: s.rearrange("p (c t) -> p c t", c=4))
                with act.Fori(0, 4) as t:
                    split(Pos(4, (l, G1), (t, 4)), 3)
                    take_tile(Pos(0, (l, N_TILES), (t, 1)), Pos(3, (l, G1), (t, 4)),
                              [proj[:, tok, bass.ds(t * NT, NT)] for tok in range(TOKS)])
                    split(Pos(7, (l, G1), (t, 4)), 1)
                for n in range(2):
                    T.take(act, layer(l, F_W + n, F_ALL), conv_wT[:, 2 * n:2 * n + 2, :], cols=2 * (CONV_K + 1),
                           view=lambda s: s.rearrange("p (c k) -> p c k", c=2))
                split(layer(l, 20, G1), 3)
                for tok in range(TOKS):
                    W.wait_tile(act, tok, layer(l, 4, N_TILES), layer(l, 19, G1))
                    act.activation(proj[:, tok, G0:G0 + CW], prod[tok][:, :], ACT.Tanh, scale=0.5)\
                       .then_inc(prod_free[tok], 1)
                split(layer(l, 23, G1), 1)
                ada_take(layer(l, ADA_N, SUMS), ada_rest[:, 0, :], acc[2:4])

                def conv_take(t, turn):
                    cols = bass.ds(t * P, P) if not isinstance(t, int) else slice(t * P, (t + 1) * P)
                    T.take(act, turn, conv_tok[:, :, cols], cols=SEQ, view=lambda s: s.rearrange("p (t c) -> p t c", t=TOKS))

                def hpad_take(turn):
                    T.take(act, turn, hpad[:, CONV_K - 1:], cols=SEQ, scale=0.5)

                hpad_take(layer(l, F_PAIR, F_ALL))

                def pair(t):
                    last = isinstance(t, int)
                    at = lambda k, per, step: in_pair(l, t, k, per, step)
                    chunk = lambda a, n, at=0: a[..., at + t * n:at + (t + 1) * n] if last else a[..., bass.ds(t * n + at, n)]
                    n, fill = at(0, PAIRS, 1), at(F_PAIR + 1, F_ALL, 4)
                    this, nt, nxt = at(20, G1, 4), at(5, N_TILES, 1), at(24, G1, 4)
                    W.split_hi(act, nxt)
                    T.take(act, fill, H.qkT[:, 0, 0:SEQ], cols=SEQ)
                    T.take(act, fill + 1, H.qkT[:, 1, 0:SEQ], cols=SEQ)
                    W.split_hi(act, nxt + 1)
                    for h in range(2):
                        H.exps(act, n, h)
                    W.split_hi(act, nxt + 2)
                    take_tile(nt, this + 3, [chunk(proj[:, tok, :], NT, GA0) for tok in range(TOKS)], ACT.Tanh, 0.5)
                    W.split_hi(act, nxt + 3)
                    for h in range(2):
                        H.take(act, n, h)
                    H.out_hi_part(act, n, aT[0][:, t, :] if last else aT[0][:, bass.ds(t, 1), :].rearrange("p a s -> p (a s)"))
                    conv_take(t, fill + 2)
                    if not last:
                        hpad_take(fill + 3)
                    ada_take(at(ADA_N + 1, SUMS, 1), chunk(mod2, NT), acc[0:1])

                with act.Fori(0, PAIRS - 1) as t:
                    pair(t)
                pair(PAIRS - 1)
                for tok in range(TOKS):
                    act.wait_ge(conv_y, layer(l, tok, TOKS).count(1))
                    act.activation(conv_sig[:, tok, :], conv_tok[:, tok, :], ACT.Tanh, scale=0.5).then_inc(conv_tanh, 1)
                split(layer(l, G_IN + G_HALF, G1), 3)
                for n in range(2):
                    T.take_hi(act, layer(l, F_CONV + n, F_ALL), cT[0][:, :, n * P:(n + 1) * P], scale=0.5,
                              view=lambda s: s.rearrange("p (c t) -> p c t", c=4))
                split(layer(l, G_IN + G_HALF + 3, G1), 1)
                at = G_IN + 2 * G_HALF
                for j in range(2):
                    split(layer(l, at + 2 * j, G1), 2)
                    for tok in range(TOKS):
                        T.take_hi(act, layer(l, F_M + 2 * j + tok, F_ALL), uT[0][:, 4 * j:4 * j + 4, tok * P:(tok + 1) * P],
                                  scale=0.5, view=lambda s: s.rearrange("p (c t) -> p c t", c=4))
                at += 4
                split(layer(l, at, G1))
                split(layer(l, at + 4, G1))
                for n in range(4):
                    T.take_hi(act, layer(l, F_U2 + n, F_ALL),
                              uT[0][:, 4 * (n % 2):4 * (n % 2) + 4, n // 2 * P:(n // 2 + 1) * P],
                              view=lambda s: s.rearrange("p (c t) -> p c t", c=4))
                at += 4

                def hidden(tile, last_group, fill, before, after):
                    split(before, 3)
                    for tok in range(TOKS):
                        W.wait_tile(act, tok, tile, last_group)
                        act.activation(r_rows[:, tok, :], prod[tok][:, :], ACT.Relu).then_inc(prod_free[tok], 1)
                    split(before + 3, 1 + after)
                    for tok in range(TOKS):
                        T.take_hi(act, fill + tok, aT[0][:, :, tok * P:(tok + 1) * P],
                                  view=lambda s: s.rearrange("p (c t) -> p c t", c=4))

                hidden(layer(l, N_TILES - T_FF, N_TILES), layer(l, at + 3, G1), layer(l, F_H, F_ALL), layer(l, at + 4, G1), 0)
                with act.Fori(1, T_FF) as f:
                    hidden(Pos(N_TILES - T_FF, (l, N_TILES), (f, 1)), Pos(at - 1, (l, G1), (f, 8)),
                           Pos(F_H, (l, F_ALL), (f, 2)), Pos(at, (l, G1), (f, 8)), 4)
                ada_take(layer(l, ADA_N + SUMS - 1, SUMS), ada_rest[:, 3, :], prod)

        @block.vector
        def _(dve):
            def split(pos, n=4):
                for g in range(n):
                    W.split_lo(dve, pos + g)

            def ada_chunk(l, k):
                n = layer(l, 2 * k, 2 * DC)
                raw = ada_raw[:, n.slot(4), :]
                if k > 0:
                    dve.drain()
                dve.wait_ge(ada_in[n.slot(4)], n.over(4).count(1, 16))
                if k == 0:
                    dve.wait_ge(ada_summed, layer(l, 1, 2).count(1))
                    dve.tensor_scalar(ada_acc, raw, c_act[:, 0:1], None, ALU.mult).then_inc(ada_used[0], 1)
                else:
                    dve.scalar_tensor_tensor(ada_acc, raw, c_act[:, k:k + 1], ada_acc, ALU.mult, ALU.add).then_inc(ada_used[0], 1)
                if k == DC - 1:
                    dve.drain().then_inc(ada_acc_done, 1)

            def modulate(out, x, scale, shift):
                dve.scalar_tensor_tensor(out, scale, 1.0, x, ALU.add, ALU.mult)
                dve.drain()
                return dve.tensor_tensor(out, out, shift, ALU.add)

            def part_stats(rows, tok, h):
                dve.bn_stats(stats[:, tok, h, :], rows[:, h * NT:(h + 1) * NT])

            def mean_var(tok, parts, done):
                dve.drain()
                dve.bn_aggr(mv[:, tok, :], stats[:, tok, 0:parts, :].rearrange("p a s -> p (a s)")).then_inc(done, 1)

            def normed(out, rows, tok, g, b):
                dve.scalar_tensor_tensor(out, rows, mv[:, tok, 0:1], g, ALU.subtract, ALU.mult)
                dve.drain()
                return dve.scalar_tensor_tensor(out, out, rstd[:, tok:tok + 1], b, ALU.mult, ALU.add)

            for s, n in ((W.lo_done, RING), (W.used, RING), (ada_used[0], 2), (ada_used[1], 2), (ada_summed, 2), (ada_taken, 2), (x_ready, 1), (gate2_used, 1),
                         (prod_free[0], 1), (prod_free[1], 1), (T.free[0], 1), (T.free[1], 1), (H.out_done, 1)):
                dve.sem_inc(s, n)
            dve.memset(hpad[:, 0:CONV_K - 1], 0.0)
            dve.wait_ge(c_tanh, 1)
            dve.scalar_tensor_tensor(c_act[:, :], c_act[:, :], 1.0, c_col[:, :], ALU.add, ALU.mult)
            dve.drain()
            dve.tensor_scalar(c_act[:, :], c_act[:, :], 0.5, None, ALU.mult)
            dve.drain()
            for k in range(DC):
                dve.tensor_scalar(c_wide[:, k, :], ones[:, :], c_act[:, k:k + 1], None, ALU.mult)
            dve.drain().then_inc(c_ready, 1)
            dve.wait_ge(freq_in, 16)
            dve.tensor_copy(pos_f[:, :], pos_i[:, :])
            dve.drain()
            for f in range(2):
                for tok in range(TOKS):
                    dve.tensor_scalar(ang[:, f, tok, :], freq[:, :], pos_f[:, tok:tok + 1], None, ALU.mult)
            dve.drain()
            for f in range(2):
                dve.tensor_scalar(turns_k[:, f], ang[:, f], 0.5 / np.pi, 0.25 * (1 - f), ALU.mult, ALU.add)
            dve.drain()
            dve.tensor_scalar(turns_k[:, :], turns_k[:, :], MAGIC, None, ALU.add)
            dve.drain()
            dve.tensor_scalar(turns_k[:, :], turns_k[:, :], MAGIC, None, ALU.subtract)
            flat = lambda t: t[:, :, :, :].rearrange("p f t r -> p (f t r)")
            for part in TWO_PI_PARTS:
                dve.drain()
                dve.scalar_tensor_tensor(flat(ang), flat(turns_k), -part, flat(ang), ALU.mult, ALU.add)
            dve.drain()
            dve.tensor_scalar(ang[:, 0], ang[:, 0], 0.5 * np.pi, None, ALU.add)
            dve.drain()
            dve.tensor_scalar(flat(ang), flat(ang), PI_BELOW, -PI_BELOW, ALU.min, ALU.max).then_inc(ang_ready, 1)
            with dve.Fori(0, LAYERS) as l:
                for k in range(DC):
                    ada_chunk(l, k)

            with dve.Fori(0, LAYERS) as l:
                first = lambda v: ada_first[:, bass.ds(l, 1), v, :].rearrange("p a n -> p (a n)")
                dve.wait_ge(consts_in, 48)
                dve.wait_ge(ada_taken, ADA_N + 2)
                for tok in range(TOKS):
                    dve.drain()
                    modulate(u_rows[:, tok, :], x_res[:, tok, :], first(1), first(0)).then_inc(u_ready, 1)
                for n in range(4):
                    if n % 2 == 0:
                        split(layer(l, n // 2, G1), 1)
                    place = lambda p: p[:, 4 * (n % 2):4 * (n % 2) + 4, n // 2 * P:(n // 2 + 1) * P]
                    T.take_lo(dve, layer(l, F_U + n, F_ALL), layer(l, S_U + n, S_ALL), place(uT[1]), place(uT[0]),
                              view=lambda s: s.rearrange("p (c t) -> p c t", c=4))
                split(layer(l, 2, G1), 2)
                dve.memset(gate1_acc, 0.0)
                with dve.Fori(0, 4) as t:
                    for i in range(4):
                        W.split_lo(dve, Pos(4 + i, (l, G1), (t, 4)))
                        if i % 2 == 0:
                            dve.drain()
                        fill, half = Pos(ADA_FILLS + i, (l, FILLS), (t, 4)), gate1_acc[:, i % 2 * NT:(i % 2 + 1) * NT]
                        dve.wait_ge(ada_in[i], fill.over(4).count(1, 16))
                        dve.scalar_tensor_tensor(half, ada_raw[:, i, 0:NT], c_act[:, bass.ds(t * 2 + i // 2, 1)], half,
                                                 ALU.mult, ALU.add).then_inc(ada_used[i % 2], 1)
                dve.drain().then_inc(gate1_done, 1)
                split(layer(l, 20, G1))
                dve.wait_ge(trig_ready, 1)
                for tok in range(TOKS):
                    dve.wait_ge(prod_free[tok], layer(l, 4, N_TILES).count(2))

                def gated(t):
                    last = isinstance(t, int)
                    chunk = lambda at: proj[:, :, at + t * P:at + (t + 1) * P] if last else proj[:, :, bass.ds(t * P + at, P)]
                    dve.scalar_tensor_tensor(glu_rows[:, :, :], chunk(G0), 1.0, chunk(A0), ALU.add, ALU.mult)\
                       .then_inc(glu_staged, 1)

                for turn in range(2):
                    T.taken(dve, layer(l, F_W + turn, F_ALL))
                gated(0)
                cos, sin = (trig[:, f].unsqueeze(2).to_broadcast([P, TOKS, HEADS, RH]) for f in range(2))
                for col in (Q0, K0):
                    rope(dve, proj[:, :, col:col + AW].rearrange("p t (h e) -> p t h e", h=HEADS), cos, sin, RH,
                         [t[:, :, :, :] for t in rope_tmp])
                def taps(ks):
                    for k in ks:
                        out, rows, w = conv_acc[k % 2][:, :], hpad[:, k:k + SEQ], conv_w[:, k:k + 1]
                        if k == 0:
                            dve.tensor_scalar(out, rows, w, conv_w[:, CONV_K:CONV_K + 1], ALU.mult, ALU.add)
                        elif k == 1:
                            dve.tensor_scalar(out, rows, w, None, ALU.mult)
                        else:
                            if k % 2 == 0:
                                dve.drain()
                            dve.scalar_tensor_tensor(out, rows, w, out, ALU.mult, ALU.add)

                def pair(t):
                    last = isinstance(t, int)
                    at = lambda k, per, step: in_pair(l, t, k, per, step)
                    some = lambda n, at=0: slice(at + t * n, at + (t + 1) * n) if last else bass.ds(t * n + at, n)
                    n, nxt = at(0, PAIRS, 1), at(24, G1, 4)
                    cols = proj[:, :, 0:2 * AW].rearrange("p t (x c) -> p t x c", x=2)
                    dve.tensor_copy(H.qk[:, 0:TOKS * 2 * P].rearrange("p (t x c) -> p t x c", t=TOKS, x=2), cols[:, :, :, some(P)])
                    dve.tensor_copy(H.v[:, :, :], proj[:, :, some(P, V0)]).then_inc(H.v_staged, 1)
                    dve.tensor_copy(conv_w[:, :], conv_wT[:, some(1), :].rearrange("p a k -> p (a k)"))
                    dve.drain().then_inc(H.staged, 1)
                    T.taken(dve, at(F_PAIR, F_ALL, 4))
                    if not last:
                        gated(t + 1)
                    taps(range(0, 14))
                    W.split_lo(dve, nxt)
                    taps(range(14, 18))
                    for h in range(2):
                        H.lows(dve, n, h, HD ** -0.5, hide)
                    W.split_lo(dve, nxt + 1)
                    for h in range(2):
                        H.norm(dve, n, h)
                    taps(range(18, 22))
                    W.split_lo(dve, nxt + 2)
                    taps(range(22, CONV_K))
                    dve.drain()
                    dve.tensor_tensor(conv_acc[0][:, :], conv_acc[0][:, :], conv_acc[1][:, :], ALU.add).then_inc(conv_done, 1)
                    W.split_lo(dve, nxt + 3)
                    flat_t = lambda p: p[:, some(1), :].rearrange("p a s -> p (a s)")
                    H.out_lo_part(dve, n, flat_t(aT[1]), flat_t(aT[0]))

                with dve.Fori(0, PAIRS - 1) as t:
                    pair(t)
                pair(PAIRS - 1)
                dve.wait_ge(vec_in, layer(l, 4, 8).count(0, 16))
                T.taken(dve, layer(l, F_CONV - 1, F_ALL))
                for tok in range(TOKS):
                    part_stats(conv_tok[:, tok, :], tok, 0)
                    mean_var(tok, 1, conv_mv)
                for tok in range(TOKS):
                    dve.wait_ge(conv_rstd, layer(l, tok, TOKS).count(1))
                    normed(conv_tok[:, tok, :], conv_tok[:, tok, :], tok, cln_vec[:, 0, :], cln_vec[:, 1, :])\
                        .then_inc(conv_y, 1)
                at = G_IN
                for j in range(2):
                    for tok in range(TOKS):
                        W.wait_tile(dve, tok, layer(l, T_IN + j, N_TILES), layer(l, at + 2 * j + 1, G1))
                        dve.scalar_tensor_tensor(y_rows[:, tok, j * NT:(j + 1) * NT],
                                                 proj[:, tok, GA0 + j * NT:GA0 + (j + 1) * NT], 1.0, (prod, acc[2:4])[j][tok][:, :],
                                                 ALU.add, ALU.mult).then_inc(prod_free[tok], 1)
                    if j == 0:
                        for tok in range(TOKS):
                            dve.wait_ge(conv_tanh, layer(l, tok, TOKS).count(1))
                            dve.scalar_tensor_tensor(conv_tok[:, tok, :], conv_sig[:, tok, :], 1.0, conv_tok[:, tok, :],
                                                     ALU.add, ALU.mult).then_inc(conv_ready, 1)
                    W.split_lo(dve, layer(l, at + 4 + 2 * j, G1))
                    W.split_lo(dve, layer(l, at + 5 + 2 * j, G1))
                    if j == 0:
                        for n in range(2):
                            place = lambda p: p[:, :, n * P:(n + 1) * P]
                            T.take_lo(dve, layer(l, F_CONV + n, F_ALL), layer(l, S_CONV + n, S_ALL), place(cT[1]), place(cT[0]),
                                      scale=0.5, view=lambda s: s.rearrange("p (c t) -> p c t", c=4))
                at += G_HALF
                for j in range(2):
                    W.split_lo(dve, layer(l, at + 4 + 2 * j, G1))
                    for tok in range(TOKS):
                        W.wait_tile(dve, tok, layer(l, T_IN + 2 + j, N_TILES), layer(l, at + 2 * j + 1, G1))
                        dve.scalar_tensor_tensor(tmp_rows[:, tok, :], proj[:, tok, GC0 + j * NT:GC0 + (j + 1) * NT],
                                                 1.0, (prod, acc[0:2])[j][tok][:, :], ALU.add, ALU.mult).then_inc(prod_free[tok], 1)
                    dve.drain()
                    for tok in range(TOKS):
                        y = y_rows[:, tok, j * NT:(j + 1) * NT]
                        dve.tensor_tensor(y, y, tmp_rows[:, tok, :], ALU.add).then_inc(merged, 1)
                    dve.drain()
                    W.split_lo(dve, layer(l, at + 5 + 2 * j, G1))
                    if j == 1:
                        dve.wait_ge(ada_taken, layer(l, ADA_N + SUMS - 2, SUMS).count(3))
                        dve.wait_ge(vec_in, layer(l, 6, 8).count(0, 16))
                        shift, scale = ada_rest[:, 1, :], ada_rest[:, 2, :]
                        dve.scalar_tensor_tensor(u2_rows[:, 0, :], scale, 1.0, ln_vec[:, 1, :], ALU.add, ALU.mult)
                        dve.scalar_tensor_tensor(scale, scale, 1.0, ln_vec[:, 0, :], ALU.add, ALU.mult)
                        dve.drain()
                        dve.tensor_tensor(shift, shift, u2_rows[:, 0, :], ALU.add)
                    for tok in range(TOKS):
                        place = lambda p: p[:, 4 * j:4 * j + 4, tok * P:(tok + 1) * P]
                        T.take_lo(dve, layer(l, F_M + 2 * j + tok, F_ALL), layer(l, S_M + 2 * j + tok, S_ALL),
                                  place(uT[1]), place(uT[0]), scale=0.5, view=lambda s: s.rearrange("p (c t) -> p c t", c=4))
                at += G_HALF

                def residual(j, tok, psum, gate, left=None):
                    cols = slice(j * NT, (j + 1) * NT)
                    y = dve.scalar_tensor_tensor(tmp_rows[:, tok, :], ada_rest[:, gate, cols], 1.0, psum, ALU.add, ALU.mult)
                    if left:
                        y.then_inc(left, 1)
                    dve.drain()
                    dve.scalar_tensor_tensor(x_res[:, tok, cols], x_res[:, tok, cols], ALPHA, tmp_rows[:, tok, :],
                                             ALU.mult, ALU.add)
                    dve.drain()
                    part_stats(x_res[:, tok, :], tok, j)
                    if j == 1:
                        mean_var(tok, 2, ln_stats)

                split(layer(l, at + 4, G1))
                for j in range(2):
                    for tok in range(TOKS):
                        W.wait_tile(dve, tok, layer(l, T_IN + 4 + j, N_TILES), layer(l, at + OUT_LAST[j], G1))
                        residual(j, tok, (prod, acc[2:4])[j][tok][:, :], 0, prod_free[tok])
                for tok in range(TOKS):
                    dve.wait_ge(ln_rstd, layer(l, tok, 2 * TOKS).count(1))
                    normed(u2_rows[:, tok, :], x_res[:, tok, :], tok, scale, shift).then_inc(u2_ready, 1)
                for n in range(4):
                    if n % 2 == 0:
                        split(layer(l, at + 8 + n // 2, G1), 1)
                    place = lambda p: p[:, 4 * (n % 2):4 * (n % 2) + 4, n // 2 * P:(n // 2 + 1) * P]
                    T.take_lo(dve, layer(l, F_U2 + n, F_ALL), layer(l, S_U2 + n, S_ALL), place(uT[1]), place(uT[0]),
                              view=lambda s: s.rearrange("p (c t) -> p c t", c=4))
                split(layer(l, at + 10, G1), 2)
                at += G_SQ

                def gate2_chunk(f=0):
                    first = isinstance(f, int)
                    dve.wait_ge(gate2_in, Pos(0, (l, T_FF), *(() if first else ((f, 1),))).count(1, 16))
                    if first:
                        dve.tensor_scalar(ada_acc, gate2_raw, c_act[:, 0:1], None, ALU.mult).then_inc(gate2_used, 1)
                    else:
                        dve.scalar_tensor_tensor(ada_acc, gate2_raw, c_act[:, bass.ds(f, 1)], ada_acc, ALU.mult, ALU.add)\
                           .then_inc(gate2_used, 1)

                def hidden(tile, fill, split_n, f=0, after=None):
                    for tok in range(TOKS):
                        dve.wait_ge(prod_free[tok], tile.count(2))
                        dve.tensor_tensor(h_rows[:, tok, :], r_rows[:, tok, :], r_rows[:, tok, :], ALU.mult)\
                           .then_inc(h_ready, 1)
                    gate2_chunk(f)
                    if after:
                        split(after)
                    else:
                        x_itself(1)
                        dve.drain().then_inc(x_normed, 1)
                    for tok in range(TOKS):
                        place = lambda p: p[:, :, tok * P:(tok + 1) * P]
                        T.take_lo(dve, fill + tok, split_n + tok, place(aT[1]), place(aT[0]),
                                  view=lambda s: s.rearrange("p (c t) -> p c t", c=4))

                def x_itself(tok):
                    normed(x_res[:, tok, :], x_res[:, tok, :], tok, ln_vec[:, 0, :], ln_vec[:, 1, :])

                split(layer(l, at + 4, G1), 2)
                x_itself(0)
                split(layer(l, at + 6, G1), 2)
                hidden(layer(l, N_TILES - T_FF, N_TILES), layer(l, F_H, F_ALL), layer(l, S_H, S_ALL))
                dve.drain()
                with dve.Fori(1, T_FF) as f:
                    split(Pos(at, (l, G1), (f, 8)))
                    hidden(Pos(N_TILES - T_FF, (l, N_TILES), (f, 1)), Pos(F_H, (l, F_ALL), (f, 2)),
                           Pos(S_H, (l, S_ALL), (f, 2)), f, Pos(at + 4, (l, G1), (f, 8)))
                    dve.drain()
                dve.wait_ge(ada_taken, layer(l, ADA_N + SUMS - 1, SUMS).count(3))
                for j in range(2):
                    dve.wait_ge(W.used, layer(l, G1 - 3 + 2 * j, G1).count(RING + 1))
                    for tok in range(TOKS):
                        residual(j, tok, acc[2 * j + tok][:, :], 3)
                dve.wait_ge(vec_in, layer(l, 8, 8).count(0, 16))
                for tok in range(TOKS):
                    dve.wait_ge(ln_rstd, layer(l, TOKS + tok, 2 * TOKS).count(1))
                    normed(x_res[:, tok, :], x_res[:, tok, :], tok, ln_vec[:, 0, :], ln_vec[:, 1, :]).then_inc(x_ready, 1)

        @block.tensor
        def _(pe):
            def vacated(tile_n):
                return lambda tok: pe.wait_ge(prod_free[tok], tile_n.count(1))

            def tile(pos, tile_n, lhs, k0, groups, outs):
                for g in range(groups):
                    W.multiply(pe, pos + g, lhs, k0 + KG * g, NT, KG, outs, g == 0, g == groups - 1,
                               vacant=vacated(tile_n) if g == 0 else None)

            def add_bias(banks, bias):
                for h, bank in enumerate(banks):
                    mm = pe.matmul(bank[:, :], ones[0:1, :], bias(h), start=False, stop=True)
                mm.then_inc(ada_summed, 1)

            def later_bias(h):
                return ada_b[:, h * NT:(h + 1) * NT]

            def first_bias(l, v):
                return lambda h: first_b[:, bass.ds(l * (2 * D) + (v * D + h * NT), NT)]

            def sum_rows(banks, rows):
                for h, bank in enumerate(banks):
                    pe.matmul(bank[:, :], ones[:, :], rows[:, h * NT:(h + 1) * NT], start=True, stop=False)

            def rows_turn(pos, rows, chunk0):
                T.turn(pe, pos, [(P, slice(c * P, (c + 1) * P), rows[:, (chunk0 + c) * P:(chunk0 + c + 1) * P])
                                 for c in range(4)])

            outs = [prod[tok][:, :] for tok in range(TOKS)]
            bias_rows.multiply(pe, prod[0])
            with pe.Fori(0, LAYERS) as l:
                pe.wait_ge(c_ready, 1)
                pe.wait_ge(ada_taken, layer(l, 0, 2).count(1))
                for k in range(DC):
                    n = layer(l, 2 * k + 1, 2 * DC)
                    pe.wait_ge(ada_in[n.slot(4)], n.over(4).count(1, 16))
                    for h in range(2):
                        mm = pe.matmul(acc[2 + h][:, :], c_wide[:, k, :], ada_raw[:, n.slot(4), h * NT:(h + 1) * NT],
                                       start=k == 0, stop=False)
                    mm.then_inc(ada_used[1], 1)
                pe.wait_ge(first_b_in, 16)
                add_bias(acc[2:4], first_bias(l, 1))
                pe.wait_ge(ada_taken, layer(l, 1, 2).count(1))
                pe.wait_ge(ada_acc_done, layer(l, 0, 1).count(1))
                sum_rows(acc[0:2], ada_acc)
                add_bias(acc[0:2], first_bias(l, 0))
            with pe.Fori(0, LAYERS) as l:
                pe.wait_ge(consts_in, 48)
                for n in range(4):
                    pe.wait_ge(u_ready, layer(l, n // 2, TOKS).count(1))
                    rows_turn(layer(l, F_U + n, F_ALL), u_rows[:, n // 2, :], 4 * (n % 2))
                with pe.Fori(0, 4) as t:
                    for n in range(2, 4):
                        T.taken(pe, layer(l, F_U + n, F_ALL))
                    tile(Pos(0, (l, G1), (t, 4)), Pos(0, (l, N_TILES), (t, 1)), uT, 0, 4, outs)
                pe.wait_ge(vec_in, layer(l, 4, 8).count(0, 16))
                for n in range(2):
                    T.turn(pe, layer(l, F_W + n, F_ALL),
                           [(P, slice(c * (CONV_K + 1), (c + 1) * (CONV_K + 1)),
                             conv_rows[:, (2 * n + c) * P:(2 * n + c + 1) * P]) for c in range(2)])
                tile(layer(l, 16, G1), layer(l, 4, N_TILES), uT, 0, 4, outs)
                pe.wait_ge(ada_taken, layer(l, ADA_N - 1, SUMS).count(3))
                pe.wait_ge(gate1_done, layer(l, 0, 1).count(1))
                sum_rows(acc[2:4], gate1_acc)
                pe.wait_ge(ada_b_in, layer(l, 0, SUMS).count(1, 16))
                add_bias(acc[2:4], later_bias)

                def conv_turn(turn, n):
                    pe.wait_ge(conv_done, n.count(1))
                    T.turn(pe, turn, [(P, slice(tok * P, (tok + 1) * P), conv_acc[0][:, tok * P:(tok + 1) * P])
                                          for tok in range(TOKS)])

                def gated_turn(turn, n):
                    pe.wait_ge(glu_staged, n.count(1))
                    T.turn(pe, turn, [(P, slice(tok * P, (tok + 1) * P), glu_rows[:, tok, :]) for tok in range(TOKS)])

                gated_turn(layer(l, F_PAIR, F_ALL), layer(l, 0, PAIRS))

                def pair(t):
                    last = isinstance(t, int)
                    at = lambda k, per, step: in_pair(l, t, k, per, step)
                    n, fill = at(0, PAIRS, 1), at(F_PAIR + 1, F_ALL, 4)
                    this, nt = at(20, G1, 4), at(5, N_TILES, 1)

                    def mod_rows(fills):
                        for i in fills:
                            rows_in = at(ADA_FILLS + 16 + i, FILLS, 4)
                            pe.wait_ge(ada_in[i], rows_in.over(4).count(1, 16))
                            for k in range(2):
                                mm = pe.matmul(acc[0][:, :], c_wide[:, 2 * i + k, :], ada_raw[:, i, k * NT:(k + 1) * NT],
                                               start=i + k == 0, stop=False)
                            mm.then_inc(ada_used[i % 2], 1)

                    W.multiply(pe, this, uT, 0, NT, KG, outs, True, False, vacant=vacated(nt))
                    pe.wait_ge(H.staged, n.count(1))
                    rows = H.qk[:, 0:TOKS * 2 * P].rearrange("p (t x c) -> p t x c", t=TOKS, x=2)
                    for x in range(2):
                        T.turn(pe, fill + x, [(P, slice(tok * P, (tok + 1) * P), rows[:, tok, x, :]) for tok in range(TOKS)])
                    W.multiply(pe, this + 1, uT, 2, NT, KG, outs, False, False)
                    pe.wait_ge(ada_taken, at(ADA_N + 1, SUMS, 1).count(2))
                    H.scores(pe, n, T, fill, True)
                    W.multiply(pe, this + 2, uT, 4, NT, KG, outs, False, False)
                    W.multiply(pe, this + 3, uT, 6, NT, KG, outs, False, True)
                    for h in range(2):
                        H.turn(pe, n, h, ident)
                    mod_rows(range(2))
                    H.mix(pe, n)
                    mod_rows(range(2, 4))
                    conv_turn(fill + 2, n)
                    if not last:
                        gated_turn(fill + 3, n + 1)
                    pe.wait_ge(ada_b_in, at(1, SUMS, 1).count(1, 16))
                    add_bias(acc[0:1], later_bias)

                with pe.Fori(0, PAIRS - 1) as t:
                    pair(t)
                pair(PAIRS - 1)
                pe.wait_ge(H.out_done, layer(l, PAIRS - 1, PAIRS).count(2))
                at = G_IN
                tile(layer(l, at, G1), layer(l, T_IN, N_TILES), aT, 0, 2, outs)
                early, late = [b[:, :] for b in acc[0:2]], [b[:, :] for b in acc[2:4]]
                W.multiply(pe, layer(l, at + 2, G1), aT, 0, NT, KG, late, True, False)
                for n in range(2):
                    pe.wait_ge(conv_ready, layer(l, n, TOKS).count(1))
                    rows_turn(layer(l, F_CONV + n, F_ALL), conv_tok[:, n, :], 0)
                W.multiply(pe, layer(l, at + 3, G1), aT, 2, NT, KG, late, False, True)
                for n in range(2):
                    T.taken(pe, layer(l, F_CONV + n, F_ALL))
                at += G_HALF

                def merged_turns(j):
                    for tok in range(TOKS):
                        pe.wait_ge(merged, layer(l, 2 * j + tok, 4).count(1))
                        rows_turn(layer(l, F_M + 2 * j + tok, F_ALL), y_rows[:, tok, :], 4 * j)

                tile(layer(l, at, G1), layer(l, T_IN + 1, N_TILES), cT, 0, 2, outs)
                W.multiply(pe, layer(l, at + 2, G1), cT, 0, NT, KG, early, True, False)
                merged_turns(0)
                W.multiply(pe, layer(l, at + 3, G1), cT, 2, NT, KG, early, False, True)
                at += G_HALF
                for i, (j, g) in enumerate(OUT_ORDER):
                    if i == 2:
                        merged_turns(1)
                    if i % 4 == 0:
                        for tok in range(TOKS):
                            T.taken(pe, layer(l, F_M + i // 2 + tok, F_ALL))
                    W.multiply(pe, layer(l, at + i, G1), uT, KG * g, NT, KG, (outs, late)[j], g == 0, g == 3,
                               vacant=vacated(layer(l, T_IN + 3, N_TILES)) if i == 0 else None)
                for n in range(4):
                    pe.wait_ge(u2_ready, layer(l, n // 2, TOKS).count(1))
                    rows_turn(layer(l, F_U2 + n, F_ALL), u2_rows[:, n // 2, :], 4 * (n % 2))
                for n in range(2, 4):
                    T.taken(pe, layer(l, F_U2 + n, F_ALL))
                at += G_SQ

                def hidden_turn(f, per):
                    for tok in range(TOKS):
                        pe.wait_ge(h_ready, Pos(tok, (l, TOKS * T_FF), *per(TOKS)).count(f * TOKS + 1))
                        rows_turn(Pos(F_H + tok + 2 * f, (l, F_ALL), *per(2)), h_rows[:, tok, :], 0)

                def down(pos, first, last, fill):
                    for tok in range(TOKS):
                        T.taken(pe, fill + tok)
                    for j in range(2):
                        for g in range(2):
                            W.multiply(pe, pos + (2 * j + g), aT, KG * g, NT, KG,
                                       [acc[2 * j + tok][:, :] for tok in range(TOKS)],
                                       first and g == 0, last and g == 1, tile_end=False)

                tile(layer(l, at, G1), layer(l, N_TILES - T_FF, N_TILES), uT, 0, 4, outs)

                def step(f, first):
                    per = (lambda c: ()) if isinstance(f, int) else (lambda c: ((f, c),))
                    k = f if isinstance(f, int) else 0
                    up, nt = Pos(at + 4 + 8 * k, (l, G1), *per(8)), Pos(N_TILES - T_FF + 1 + k, (l, N_TILES), *per(1))
                    W.multiply(pe, up, uT, 0, NT, KG, outs, True, False, vacant=vacated(nt))
                    W.multiply(pe, up + 1, uT, 2, NT, KG, outs, False, False)
                    hidden_turn(k, per)
                    W.multiply(pe, up + 2, uT, 4, NT, KG, outs, False, False)
                    W.multiply(pe, up + 3, uT, 6, NT, KG, outs, False, True)
                    down(up + 4, first, False, Pos(F_H + 2 * k, (l, F_ALL), *per(2)))

                step(0, True)
                with pe.Fori(1, T_FF - 1) as f:
                    step(f, False)
                hidden_turn(T_FF - 1, lambda c: ())
                pe.wait_ge(ada_b_in, layer(l, SUMS - 1, SUMS).count(1, 16))
                pe.wait_ge(gate2_used, layer(l, T_FF - 1, T_FF).count(2))
                sum_rows(prod, ada_acc)
                add_bias(prod, later_bias)
                down(layer(l, G1 - 4, G1), False, True, layer(l, F_ALL - 2, F_ALL))



HTILES = FF2 // HT
QA, KA, VA, QB, KB, VB, CQ = (n * AW for n in range(7))
CKV = CQ + QR
KR = CKV + KVR
UQ_W, UKV = QR // 2, CV * 2 * HEADS
LAT_TILES = 4
G2_UQ = IN2_T * 4
G2_UKV = G2_UQ + 6
G2_GATE = G2_UKV + 4
G2_AB = G2_GATE + 24
G2_C = G2_AB + 8
G2_O = G2_C + 4
G2_FF = G2_O + 8
G2 = G2_FF + HTILES * 6
N2_UQ, N2_UKV, N2_GATE = IN2_T, IN2_T + 2, IN2_T + 4
N2_AB = N2_GATE + 6
N2_C = N2_AB + 4
N2_O = N2_C + 2
N2_FF = N2_O + 2
N2 = N2_FF + HTILES
F2_LAT, F2_A = 4, 8
F2_B = F2_A + 2 * PAIRS
F2_M = F2_B + 3 * BH + 2 * PAIRS
F2_U2 = F2_M + 4
F2_H = F2_U2 + 4
F2 = F2_H + 2 * HTILES
S2_LAT, S2_B = 4, 8
S2_M = S2_B + BH
S2_U2 = S2_M + 4
S2_H = S2_U2 + 4
S2 = S2_H + 2 * HTILES
PER = PAIRS + BH + PAIRS
N_VEC = 10


def qk_turn(l, n):
    b = n - PAIRS
    return Pos(F2_A + 2 * n if b <= 2 else F2_B + (3 * b - 2 if b < BH + 2 else 2 * b + BH), (l, F2))


def out_turn(l, b):
    return Pos(F2_B + 6 + 3 * b, (l, F2))


class BiasRows:

    def __init__(self, nc, ctx, dr, scratch):
        sem = lambda n: ctx.enter_context(nc.semaphore(n))
        self.dr, self.scratch = dr, scratch
        self.tables_in, self.summed, self.copied, self.in_dram = (
            sem(n) for n in ("bias_tables_in", "bias_summed", "bias_copied", "bias_in_dram"))

    def lay(self, cols):
        self.buckets = cols[0:BUCKETS + 2, 0:REL]
        self.rows = cols[0:AH + BH, REL:2 * REL]
        self.table = cols[0:BUCKETS + 2, 2 * REL:2 * REL + AH + BH]

    def load(self, sp):
        for place, src in ((self.buckets, self.dr["bias_rows"]), (self.table[0:BUCKETS, :], self.dr["rel_bias_table_2"]),
                           (self.table[BUCKETS:BUCKETS + 2, :], self.dr["bias_kinds"])):
            sp.dma_start(place, src).then_inc(self.tables_in, 16)

    def multiply(self, pe, bank):
        pe.wait_ge(self.tables_in, 48)
        pe.matmul(bank[0:AH + BH, 0:REL], self.table, self.buckets, start=True, stop=True).then_inc(self.summed, 1)

    def copy(self, act, bank):
        act.wait_ge(self.summed, 1)
        act.copy(self.rows, bank[0:AH + BH, 0:REL]).then_inc(self.copied, 1)

    def send(self, pool):
        pool.wait_ge(self.copied, 1)
        pool.dma_start(self.scratch, self.rows).then_inc(self.in_dram, 16)


def second_block(nc, dr, scratch, bias_rows, x_res, ident, hide, ones, small):
    ctx = ExitStack()
    with ctx:
        sb = lambda n, s, dt=F32: ctx.enter_context(nc.sbuf_tensor(n, s, dt))
        sem = lambda n: ctx.enter_context(nc.semaphore(n))
        bank = lambda n: ctx.enter_context(nc.psum_tensor(n, [P, NT], F32))

        W = Weights(nc, ctx, "b", 2)
        prod = [bank(f"prod{t}_b") for t in range(TOKS)]
        acc = [bank(f"acc{n}_b") for n in range(4)]
        T = Turns(nc, ctx, "b", ident)
        H = Heads(nc, ctx, "b", acc[0:2], acc[2:4])

        uT = (sb("hT_hi", [P, DC, SEQ], F32R), sb("hT_lo", [P, DC, SEQ], F32R))
        aT = (sb("yaT_hi", [P, 4, SEQ], F32R), sb("yaT_lo", [P, 4, SEQ], F32R))
        bT = (sb("ybT_hi", [P, 4, SEQ], F32R), sb("ybT_lo", [P, 4, SEQ], F32R))
        cT = tuple(part[:, 4:8, :] for part in uT)
        proj = sb("proj_b", [P, TOKS, IN2])
        h_rows, y_rows, u2_rows = (proj[:, :, 0:D] for _ in range(3))
        tmp_rows = proj[:, :, D:D + NT]
        act_rows, hid_rows = proj[:, :, D:D + HT], proj[:, :, D + NT:D + NT + HT]
        q_up = proj[:, :, CQ:CQ + QR]
        kv_up = sb("kv_up", [P, TOKS, UKV])
        gates = sb("gates", [P, TOKS, 3 * D])
        bias = sb("bias", [P, AH + BH, TRI])
        mix_g, ffn_g = sb("mix_g", [P, D]), sb("ffn_g", [P, D])
        lat_g = sb("lat_g", [P, QR + KVR])
        sub_g = sb("sub_g", [P, 2 * HD])
        lam_vec, lam_prod = sb("lam_vec", [P, 4, HD]), sb("lam_prod", [P, 2, HD])
        lam_const = sb("lam_const", [P, 2])
        lam_sum, lam_exp = sb("lam_sum", [P, 2]), sb("lam_exp", [P, 2])
        lam_neg = sb("lam_neg", [P, 1])
        trig = sb("trig_b", [P, TOKS, ROPE])
        rope_tmp = [proj[:, 0, n * HT:(n + 1) * HT].rearrange("p (t h e) -> p t h e", t=TOKS, h=HEADS)
                    for n in range(4)]
        rope_tmp_k = [gates[:, 1, n * ROPE:(n + 1) * ROPE].rearrange("p (t e) -> p t e", t=TOKS) for n in range(4)]
        yb_rows = sb("yb_rows", [P, TOKS, 2 * HD])
        x_sq, x_squares, x_rstd = sb("x_sq", [P, 2, TOKS]), sb("x_squares", [P, TOKS]), sb("x_rstd", [P, TOKS])
        lat_squares, lat_rstd = sb("lat_squares", [P, 4]), sb("lat_rstd", [P, 4])
        sub_sq = sb("sub_sq", [P, TOKS * P])
        sub_squares, sub_rstd = sb("sub_squares", [P, TOKS]), sb("sub_rstd", [P, TOKS])
        flip = proj[:, 1, 2 * D + REL:2 * D + REL + P]
        bias_flipped = gates[:, 1, :].rearrange("p (h k) -> p h k", h=AH + BH)

        consts_in, bias_in, bias_turned, bias_out = (sem(n) for n in ("consts_in_b", "bias_in", "bias_turned", "bias_out"))
        mix_in, vec_in = sem("mix_g_in"), sem("vec_in_b")
        vec_free = sem("vec_free")
        x_halves, x_sq_done, x_rstd_done = sem("x_halves"), sem("x_sq_done"), sem("x_rstd_done")
        lat_sq_done, lat_rstd_done = sem("lat_sq_done"), sem("lat_rstd_done")
        lam_ready, lam_exped = sem("lam_ready"), sem("lam_exped")
        h_ready, lat_ready, u2_ready = sem("h_ready_b"), sem("lat_ready"), sem("u2_ready_b")
        prod_free = [sem(f"prod_free{t}_b") for t in range(TOKS)]
        gate_done, sub_done = sem("gate_done"), sem("sub_done")
        merged, act_done = sem("merged_b"), sem("act_done")
        four = lambda s: s.rearrange("p (c t) -> p c t", c=4)
        two = lambda s: s.rearrange("p (c t) -> p c t", c=2)
        flat = lambda a: a.rearrange("p a k -> p (a k)")

        def layer(r, const, per):
            return Pos(const, (r, per))

        def pair(l, n, *regs):
            return Pos(n, (l, PER), *regs)

        def gate_tile(l, n, *regs):
            return Pos(N2_GATE + n, (l, N2), *regs)

        def take_bias(copy, eng, b):
            eng.wait_ge(bias_turned, b + 1)
            rows = (prod + acc)[b][:, :].rearrange("p (h k) -> p h k", h=2)
            copy(bias[:, 2 * b:2 * b + 2, P:TRI], rows)
            return copy(bias[:, 2 * b:2 * b + 2, 0:P], rows[:, :, P:SEQ])

        block = ctx.enter_context(nc.Block())

        @block.sync
        def _(sp):
            def rows(pos, src, row, col, width):
                part = lambda c: ((lambda place: place[:, c * width:(c + 1) * width]),
                                  src[:, bass.ds(row + c * P, P), col].rearrange("a p n -> (a p) n"))
                W.load(sp, pos, part(0), part(1))

            sp.dma_start(flip, dr["flip"]).then_inc(consts_in, 16)
            sp.dma_start(trig[:, :, :], dr["trig_2"].rearrange("(t p) e -> p t e", p=P)).then_inc(consts_in, 16)
            with sp.Fori(0, LAYERS) as l:
                ls = bass.ds(l, 1)
                ws = {n: dr[n + "_2"][ls] for n in ("w_in", "w_uq", "w_ukv", "w_gate", "w_br_a", "w_br_b", "w_br_c",
                                                    "w_o", "w_ffn_gate", "w_ffn_up", "w_ffn_down")}

                def in_tile(t, pos):
                    for g in range(4):
                        rows(pos + g, ws["w_in"], g * KG * P, bass.ds(t * IN2_W, IN2_W), IN2_W)

                sp.wait_ge(vec_free, layer(l, 0, 1).count(1))
                row = lambda name, n: dr[name + "_2"][ls, :].to_broadcast([P, n])
                sp.dma_start(mix_g[:, :], row("ln_mix_g", D)).then_inc(mix_in, 16)
                in_tile(IN2_T - LAT_TILES, layer(l, 0, G2))
                sp.dma_start(lat_g[:, 0:QR], row("mla_q_norm_g", QR)).then_inc(vec_in, 16)
                sp.dma_start(lat_g[:, QR:QR + KVR], row("mla_kv_norm_g", KVR)).then_inc(vec_in, 16)
                for n, name in enumerate(("lambda_q1", "lambda_q2", "lambda_k1", "lambda_k2")):
                    sp.dma_start(lam_vec[:, n, :], row(name, HD)).then_inc(vec_in, 16)
                sp.dma_start(lam_const[:, :], dr["lam_const"][ls, :].to_broadcast([P, 2])).then_inc(vec_in, 16)
                sp.dma_start(sub_g[:, :], row("diff_subln_g", 2 * HD)).then_inc(vec_in, 16)
                sp.dma_start(gates[:, 0, :], row("b_gate", 3 * D)).then_inc(vec_in, 16)
                sp.dma_start(ffn_g[:, :], row("ln_ffn_g", D)).then_inc(vec_in, 16)
                with sp.Fori(1, LAT_TILES) as t:
                    in_tile(t + (IN2_T - LAT_TILES), Pos(0, (l, G2), (t, 4)))
                with sp.Fori(0, IN2_T - LAT_TILES) as t:
                    in_tile(t, Pos(4 * LAT_TILES, (l, G2), (t, 4)))
                for t in range(2):
                    for g in range(3):
                        rows(layer(l, G2_UQ + 3 * t + g, G2), ws["w_uq"], g * KG * P, bass.ds(t * UQ_W, UQ_W), UQ_W)
                for t in range(2):
                    for c in range(2):
                        part = lambda h: ((lambda place: place[:, h * HT:(h + 1) * HT]),
                                          ws["w_ukv"][:, c * P:(c + 1) * P, t * NT + h * HT:t * NT + (h + 1) * HT]
                                          .rearrange("a p n -> (a p) n"))
                        W.load(sp, layer(l, G2_UKV + 2 * t + c, G2), part(0), part(1))
                with sp.Fori(0, 6) as t:
                    for g in range(4):
                        rows(Pos(G2_GATE + g, (l, G2), (t, 4)), ws["w_gate"], g * KG * P, bass.ds(t * NT, NT), NT)
                with sp.Fori(0, 2) as t:
                    for b, name in enumerate(("w_br_a", "w_br_b")):
                        for g in range(2):
                            rows(Pos(G2_AB + 2 * b + g, (l, G2), (t, 4)), ws[name], g * KG * P, bass.ds(t * NT, NT), NT)
                for name, at, order in (("w_br_c", G2_C, [(t, g) for t in range(2) for g in range(2)]), ("w_o", G2_O, OUT_ORDER)):
                    for i, (t, g) in enumerate(order):
                        rows(layer(l, at + i, G2), ws[name], g * KG * P, bass.ds(t * NT, NT), NT)

                def gate_up(k, pos):
                    for g in range(4):
                        part = lambda h, name: (
                            (lambda place: place.rearrange("p (c n) -> p c n", c=KG)[:, :, h * HT:(h + 1) * HT]),
                            ws[name][:, g * KG * P:(g + 1) * KG * P, bass.ds(k * HT, HT)]
                            .rearrange("a (c p) n -> p (a c) n", p=P))
                        W.load(sp, pos + g, part(0, "w_ffn_gate"), part(1, "w_ffn_up"))

                def down(k, pos):
                    for j in range(2):
                        rows(pos + j, ws["w_ffn_down"], k * HT, bass.ds(j * NT, NT), NT)

                gate_up(0, layer(l, G2_FF, G2))
                with sp.Fori(0, HTILES // 2) as i:
                    for e in range(2):
                        at = Pos(G2_FF + 4 + 6 * e, (l, G2), (i, 12))
                        gate_up(i * 2 + (1 + e), at)
                        down(i * 2 + e, at + 4)
                down(HTILES - 1, layer(l, G2 - 2, G2))
            sp.wait_ge(vec_free, LAYERS + 1)
            sp.dma_start(mix_g[:, :], dr["final_norm_g_2"].rearrange("(a n) -> a n", a=1).to_broadcast([P, D]))\
              .then_inc(mix_in, 16)

        @block.gpsimd
        def _(pool):
            pool.wait_ge(bias_rows.in_dram, 16)
            pool.dma_start(bias_flipped, bass.AP(tensor=scratch.tensor, offset=0,
                                                 ap=[[1, P], [REL, AH + BH], [1, SEQ]])).then_inc(bias_in, 16)

            def root(out, sq, n):
                pool.tensor_tensor(sq, sq, small[:, 1, 0:n], ALU.add)
                pool.drain()
                return pool.tensor_tensor(out, sq, small[:, 2, 0:n], ALU.pow)

            def x_root(n):
                for tok in range(TOKS):
                    pool.wait_ge(x_sq_done, Pos(4 * n.k + 2 + tok, *((r, 4 * s) for r, s in n.regs)).count(1))
                    pool.tensor_tensor(x_squares[:, tok:tok + 1], x_sq[:, 0, tok:tok + 1], x_sq[:, 1, tok:tok + 1], ALU.add)
                    pool.drain()
                    root(x_rstd[:, tok:tok + 1], x_squares[:, tok:tok + 1], 1).then_inc(x_rstd_done, 1)

            with pool.Fori(0, LAYERS) as l:
                x_root(layer(l, 0, 2))
                pool.wait_ge(lat_sq_done, layer(l, 0, 1).count(1))
                root(lat_rstd[:, :], lat_squares[:, :], 4).then_inc(lat_rstd_done, 1)
                with pool.Fori(0, BH) as b:
                    pool.wait_ge(H.out_hi, pair(l, PAIRS, (b, 1)).count(1))
                    root(sub_rstd[:, :], sub_squares[:, :], TOKS).then_inc(sub_done, 1)
                x_root(layer(l, 1, 2))
            x_root(Pos(2 * LAYERS))

        @block.scalar
        def _(act):
            def split(pos, n, cols=KG * NT):
                for g in range(n):
                    W.split_hi(act, pos + g, cols)

            def take_tile(tile, last_group, outs, cols):
                for tok, out in enumerate(outs):
                    W.wait_tile(act, tok, tile, last_group)
                    act.copy(out, prod[tok][:, 0:cols]).then_inc(prod_free[tok], 1)

            def mean_squares(rows, n, place):
                return act.activation(kv_up[:, place % 2, 0:n], rows, ACT.Square, scale=float(n) ** -0.5,
                                      accum_out=lat_squares[:, place:place + 1])

            def square_x(n):
                for j in range(2):
                    for tok in range(TOKS):
                        half = Pos(4 * n.k + TOKS * j + tok, *((r, 4 * s) for r, s in n.regs))
                        act.wait_ge(x_halves, half.count(1))
                        act.activation(kv_up[:, tok, j * NT:(j + 1) * NT], x_res[:, tok, j * NT:(j + 1) * NT], ACT.Square,
                                       scale=float(D) ** -0.5, accum_out=x_sq[:, j, tok:tok + 1]).then_inc(x_sq_done, 1)

            def gate_tanh(tile, cols):
                for tok in range(TOKS):
                    act.wait_ge(prod_free[tok], tile.count(2))
                    act.activation(gates[:, tok, cols], gates[:, tok, cols], ACT.Tanh, scale=0.5).then_inc(gate_done, 1)

            for b in range(1, 6, 2):
                take_bias(act.copy, act, b).then_inc(bias_out, 1)
            with act.Fori(0, LAYERS) as l:
                square_x(layer(l, 0, 2))
                split(layer(l, 0, G2), 4, KG * IN2_W)
                for n in range(4):
                    T.take_hi(act, layer(l, n, F2), uT[0][:, 4 * (n % 2):4 * (n % 2) + 4, n // 2 * P:(n // 2 + 1) * P],
                              view=four)
                in_cols = lambda t: [proj[:, tok, bass.ds(t * IN2_W, IN2_W)] for tok in range(TOKS)]
                with act.Fori(0, LAT_TILES) as t:
                    split(Pos(4, (l, G2), (t, 4)), 3, KG * IN2_W)
                    take_tile(Pos(0, (l, N2), (t, 1)), Pos(3, (l, G2), (t, 4)), in_cols(t + (IN2_T - LAT_TILES)), IN2_W)
                    split(Pos(7, (l, G2), (t, 4)), 1, KG * IN2_W)
                def in_step(t, at, tile):
                    split(at, 3, KG * IN2_W)
                    take_tile(tile, at + (-1), in_cols(t), IN2_W)
                    split(at + 3, 1, KG * IN2_W)

                in_step(0, layer(l, 4 + 4 * LAT_TILES, G2), layer(l, LAT_TILES, N2))
                act.wait_ge(lam_ready, layer(l, 0, 1).count(1))
                act.activation(lam_exp[:, :], lam_sum[:, :], ACT.Exp).then_inc(lam_exped, 1)
                act.drain()
                for tok in range(TOKS):
                    mean_squares(proj[:, tok, CQ:CQ + QR], QR, tok)
                act.drain()
                for tok in range(TOKS):
                    sq = mean_squares(proj[:, tok, CKV:CKV + KVR], KVR, 2 + tok)
                sq.then_inc(lat_sq_done, 1)
                with act.Fori(1, IN2_T - LAT_TILES - 1) as t:
                    in_step(t, Pos(4 + 4 * LAT_TILES, (l, G2), (t, 4)), Pos(LAT_TILES, (l, N2), (t, 1)))
                for tok in range(TOKS):
                    for n in range(2 * tok, 2 * tok + 2):
                        T.take_hi(act, layer(l, F2_LAT + n, F2), (aT, bT)[n % 2][0][:, :, tok * P:(tok + 1) * P], view=four)
                    split(layer(l, G2_UQ + 2 * tok, G2), 2 - tok, KG * UQ_W)
                take_tile(layer(l, IN2_T - 1, N2), layer(l, G2_UQ - 1, G2), in_cols(IN2_T - LAT_TILES - 1), IN2_W)
                split(layer(l, G2_UQ + 3, G2), 1, KG * UQ_W)
                split(layer(l, G2_UQ + 4, G2), 2, KG * UQ_W)
                take_tile(layer(l, N2_UQ, N2), layer(l, G2_UQ + 2, G2), [q_up[:, tok, 0:UQ_W] for tok in range(TOKS)], UQ_W)
                split(layer(l, G2_UKV, G2), 3, NT)
                take_tile(layer(l, N2_UQ + 1, N2), layer(l, G2_UQ + 5, G2),
                          [q_up[:, tok, UQ_W:QR] for tok in range(TOKS)], UQ_W)
                split(layer(l, G2_UKV + 3, G2), 1, NT)

                def take_qk(fill):
                    for x in range(2):
                        T.take(act, fill + x, H.qkT[:, x, 0:SEQ], cols=SEQ)

                take_qk(qk_turn(l, 0))
                for j in range(2):
                    split(layer(l, G2_GATE + 2 * j, G2), 2)
                    take_tile(layer(l, N2_UKV + j, N2), layer(l, G2_UKV + 2 * j + 1, G2),
                              [kv_up[:, tok, j * NT:(j + 1) * NT] for tok in range(TOKS)], NT)

                with act.Fori(0, PAIRS) as t:
                    n = pair(l, 0, (t, 1))
                    nxt = Pos(G2_GATE + 4, (l, G2), (t, 4))
                    for h in range(2):
                        H.exps(act, n, h)
                    split(nxt, 2)
                    take_qk(Pos(F2_A + 2, (l, F2), (t, 2)))
                    for h in range(2):
                        H.take(act, n, h)
                    split(nxt + 2, 1)
                    H.out_hi_part(act, n, flat(aT[0][:, bass.ds(t, 1), :]))
                    split(nxt + 3, 1)
                    gate_tanh(gate_tile(l, 0, (t, 1)), bass.ds(t * NT, NT))

                def take_rows(m):
                    for h in range(2):
                        T.take(act, qk_turn(l, m) + h, H.qkT[0:QH, h, :], rows=QH)

                for b in range(BH):
                    m = PAIRS + b
                    n, nxt = pair(l, m), layer(l, G2_GATE + 20 + 2 * b, G2)
                    H.exps(act, n, 0)
                    H.exps(act, n, 1)
                    if b < BH - 1:
                        take_qk(qk_turn(l, m + 1))
                    else:
                        take_rows(m + 1)
                    split(nxt, 1)
                    if b > 0:
                        T.take_hi(act, out_turn(l, b - 1), bT[0][:, b - 1, :], cols=SEQ)
                    act.wait_ge(H.pT_full, twice(n, 1).count(1))
                    act.copy(H.pT[0][:, :], H.T[0][:, 0:TRI]).then_inc(H.pT_ready, 2)
                    act.wait_ge(H.out_full, n.count(1))
                    for tok in range(TOKS):
                        sq = act.activation(sub_sq[:, tok * P:(tok + 1) * P], H.T[1][:, tok * P:(tok + 1) * P],
                                            ACT.Square, scale=float(2 * HD) ** -0.5,
                                            accum_out=sub_squares[:, tok:tok + 1])
                    sq.then_inc(H.out_hi, 1)
                    split(nxt + 1, 1)
                    if b % 2:
                        gate_tanh(gate_tile(l, 4 + b // 2), slice(2 * D + b // 2 * NT, 2 * D + (b // 2 + 1) * NT))
                for c in range(PAIRS):
                    m = PAIRS + BH + c
                    n, nxt = pair(l, m), layer(l, G2_AB + 4 + 2 * c, G2)
                    H.exps(act, n, 0)
                    if c < PAIRS - 1:
                        take_rows(m + 1)
                    H.exps(act, n, 1)
                    split(nxt, 1)
                    if c == 0:
                        T.take_hi(act, out_turn(l, BH - 1), bT[0][:, BH - 1, :], cols=SEQ)
                    for h in range(2):
                        H.take(act, n, h)
                    H.out_hi_part(act, n, cT[0][:, c, :])
                    split(nxt + 1, 1)
                for j in range(2):
                    split(layer(l, G2_O + 2 * j, G2), 2)
                    for tok in range(TOKS):
                        T.take_hi(act, layer(l, F2_M + 2 * j + tok, F2), uT[0][:, 4 * j:4 * j + 4, tok * P:(tok + 1) * P],
                                  scale=0.5, view=four)
                split(layer(l, G2_O + 4, G2), 7)
                square_x(layer(l, 1, 2))
                split(layer(l, G2_FF + 3, G2), 1)
                for n in range(4):
                    T.take_hi(act, layer(l, F2_U2 + n, F2),
                              uT[0][:, 4 * (n % 2):4 * (n % 2) + 4, n // 2 * P:(n // 2 + 1) * P], view=four)

                def take_hidden(fill, out):
                    for tok in range(TOKS):
                        T.take_hi(act, fill + tok, out[0][:, 0:2, tok * P:(tok + 1) * P], cols=SEQ, scale=0.5, view=two)

                def gated(tile, last_group, banks=prod):
                    for tok in range(TOKS):
                        W.wait_tile(act, tok, tile, last_group)
                        act.activation(act_rows[:, tok, :], banks[tok][:, 0:HT], ACT.Tanh, scale=0.5).then_inc(act_done, 1)

                split(layer(l, G2_FF + 4, G2), 2)
                gated(layer(l, N2_FF, N2), layer(l, G2_FF + 3, G2), acc[2:4])
                with act.Fori(0, HTILES // 2) as i:
                    for e in range(2):
                        at = Pos(G2_FF + 4 + 6 * e, (l, G2), (i, 12))
                        split(at + 2, 2)
                        take_hidden(Pos(F2_H + 2 * e, (l, F2), (i, 4)), (aT, bT)[e])
                        split(at + 4, 2)
                        gated(Pos(N2_FF + 1 + e, (l, N2), (i, 2)), at + 3)
                        split(at + 6, 2)
                take_hidden(layer(l, F2 - 2, F2), aT)
            square_x(Pos(2 * LAYERS))

        @block.vector
        def _(dve):
            def split(pos, n, cols=KG * NT):
                for g in range(n):
                    W.split_lo(dve, pos + g, cols)

            def rms(out, rows, scale, g):
                return dve.scalar_tensor_tensor(out, rows, scale, g, ALU.mult, ALU.mult)

            def x_norm(n, out, g, ready=None):
                for tok in range(TOKS):
                    dve.wait_ge(x_rstd_done, Pos(TOKS * n.k + tok, *((r, TOKS * s) for r, s in n.regs)).count(1))
                    y = rms(out[:, tok, :], x_res[:, tok, :], x_rstd[:, tok:tok + 1], g[:, :])
                    if ready:
                        y.then_inc(ready, 1)

            def times_gate(out, gate_cols, tok, banks=prod):
                return dve.scalar_tensor_tensor(out, gates[:, tok, gate_cols], 1.0, banks[tok][:, :], ALU.add, ALU.mult)

            def add_gate_bias(tile, last_group, cols):
                for tok in range(TOKS):
                    W.wait_tile(dve, tok, tile, last_group)
                for tok in (1, 0):
                    dve.tensor_tensor(gates[:, tok, cols], gates[:, 0, cols], prod[tok][:, :], ALU.add)\
                       .then_inc(prod_free[tok], 1)

            def stage_qk(qk_cols):
                dve.tensor_copy(H.qk[:, 0:TOKS * 2 * P].rearrange("p (t x c) -> p t x c", t=TOKS, x=2),
                                qk_cols).then_inc(H.staged, 1)

            def stage_v(v_cols):
                dve.tensor_copy(H.v[:, :, :], v_cols).then_inc(H.v_staged, 1)

            for b in range(0, 6, 2):
                take_bias(dve.tensor_copy, dve, b)
            dve.drain()
            dve.wait_ge(bias_out, 3)
            for s, n in ((W.lo_done, RING), (W.used, RING), (prod_free[0], 1), (prod_free[1], 1),
                         (T.free[0], 1), (T.free[1], 1), (H.out_done, 1), (vec_free, 1), (x_halves, 4)):
                dve.sem_inc(s, n)
            with dve.Fori(0, LAYERS) as l:
                dve.wait_ge(mix_in, layer(l, 0, 1).count(1, 16))
                x_norm(layer(l, 0, 2), h_rows, mix_g, h_ready)
                for n in range(4):
                    if n % 2 == 0:
                        split(layer(l, n // 2, G2), 1, KG * IN2_W)
                    place = lambda p: p[:, 4 * (n % 2):4 * (n % 2) + 4, n // 2 * P:(n // 2 + 1) * P]
                    T.take_lo(dve, layer(l, n, F2), layer(l, n, S2), place(uT[1]), place(uT[0]), view=four)
                split(layer(l, 2, G2), 2, KG * IN2_W)
                dve.wait_ge(vec_in, layer(l, N_VEC, N_VEC).count(0, 16))
                dve.tensor_tensor(lam_prod[:, :, :], lam_vec[:, 0:2, :], lam_vec[:, 2:4, :], ALU.mult)
                dve.tensor_scalar(sub_g[:, :], sub_g[:, :], lam_const[:, 1:2], None, ALU.mult)
                dve.drain()
                dve.tensor_reduce(lam_sum[:, :], lam_prod[:, :, :], AX, ALU.add).then_inc(lam_ready, 1)
                with dve.Fori(0, LAT_TILES) as t:
                    split(Pos(4, (l, G2), (t, 4)), 4, KG * IN2_W)
                split(layer(l, 4 + 4 * LAT_TILES, G2), 4, KG * IN2_W)
                dve.wait_ge(lam_exped, layer(l, 0, 1).count(1))
                dve.scalar_tensor_tensor(lam_neg[:, :], lam_exp[:, 1:2], lam_exp[:, 0:1], lam_const[:, 0:1],
                                         ALU.subtract, ALU.add)
                split(layer(l, 8 + 4 * LAT_TILES, G2), 1, KG * IN2_W)
                dve.wait_ge(lat_rstd_done, layer(l, 0, 1).count(1))
                for tok in range(TOKS):
                    rms(proj[:, tok, CQ:CKV], proj[:, tok, CQ:CKV], lat_rstd[:, tok:tok + 1], lat_g[:, 0:QR])
                    rms(proj[:, tok, CKV:KR], proj[:, tok, CKV:KR], lat_rstd[:, 2 + tok:3 + tok], lat_g[:, QR:])\
                        .then_inc(lat_ready, 1)
                cos, sin = trig[:, :, 0:ROPE // 2], trig[:, :, ROPE // 2:]
                dve.wait_ge(consts_in, 16 * 2)
                split(layer(l, 9 + 4 * LAT_TILES, G2), 2, KG * IN2_W)
                rope(dve, proj[:, :, KR:], cos, sin, ROPE // 2, rope_tmp_k)
                split(layer(l, 11 + 4 * LAT_TILES, G2), 1, KG * IN2_W)
                with dve.Fori(2, IN2_T - LAT_TILES - 1) as t:
                    split(Pos(4 + 4 * LAT_TILES, (l, G2), (t, 4)), 4, KG * IN2_W)
                for tok in range(TOKS):
                    for n in range(2 * tok, 2 * tok + 2):
                        place = lambda p: p[:, :, tok * P:(tok + 1) * P]
                        lat = (aT, bT)[n % 2]
                        T.take_lo(dve, layer(l, F2_LAT + n, F2), layer(l, S2_LAT + n, S2), place(lat[1]), place(lat[0]), view=four)
                    split(layer(l, G2_UQ + 2 * tok, G2), 2, KG * UQ_W)
                two_cols = lambda col: proj[:, :, col:col + 2 * AW].rearrange("p t (x c) -> p t x c", x=2)
                for tok in range(TOKS):
                    dve.wait_ge(prod_free[tok], layer(l, IN2_T - 1, N2).count(2))
                stage_qk(two_cols(QA)[..., 0:P])
                split(layer(l, G2_UQ + 4, G2), 2, KG * UQ_W)
                split(layer(l, G2_UKV, G2), 4, NT)
                split(layer(l, G2_GATE, G2), 4)
                rope_q = lambda: rope(dve, q_up.rearrange("p t (h e) -> p t h e", h=HEADS)[..., NOPE:QH],
                     *(f.unsqueeze(2).to_broadcast([P, TOKS, HEADS, ROPE // 2]) for f in (cos, sin)), ROPE // 2,
                     [t[:, :, :, :] for t in rope_tmp])
                def branch_a(t, last):
                    per = (lambda c: ()) if last else (lambda c: ((t, c),))
                    k = t if last else 0
                    of = lambda a, at, size: a[..., at:at + size] if last else a[..., bass.ds(at, size)]
                    n, nxt = pair(l, k, *per(1)), Pos(G2_GATE + 4 + 4 * k, (l, G2), *per(4))
                    row = lambda a, at: a[:, at, :] if last else flat(a[:, bass.ds(at, 1), :])
                    for h in range(2):
                        H.lows(dve, n, h, HD ** -0.5, row(bias, t * 2 + h))
                    stage_qk(two_cols(QB)[..., 0:P] if last else two_cols(QA)[:, :, :, bass.ds(t * P + P, P)])
                    stage_v(of(proj, t * P + VA, P))
                    for h in range(2):
                        H.norm(dve, n, h)
                    split(nxt, 3)
                    add_gate_bias(gate_tile(l, k, *per(1)), nxt + (-1), slice(t * NT, (t + 1) * NT) if last else bass.ds(t * NT, NT))
                    H.out_lo_part(dve, n, row(aT[1], t), row(aT[0], t))
                    if not last:
                        split(nxt + 3, 1)

                with dve.Fori(0, PAIRS - 1) as t:
                    branch_a(t, False)
                for tok in range(TOKS):
                    dve.wait_ge(prod_free[tok], layer(l, N2_UKV + 1, N2).count(2))
                rope_q()
                branch_a(PAIRS - 1, True)

                def stage_c(c):
                    qk = H.qk[:, :].rearrange("p (t h x c) -> p t h x c", t=TOKS, h=2, x=2)
                    kv = kv_up[:, :, c * 2 * P:(c + 1) * 2 * P].rearrange("p t (h c) -> p t h c", h=2)
                    dve.tensor_copy(qk[:, :, :, 0, :], q_up[:, :, c * 2 * QH:(c + 1) * 2 * QH].rearrange("p t (h c) -> p t h c", h=2))
                    dve.tensor_copy(qk[:, :, :, 1, 0:NOPE], kv[:, :, :, 0:NOPE])
                    dve.tensor_copy(qk[:, :, :, 1, NOPE:], proj[:, :, KR:].unsqueeze(2).to_broadcast([P, TOKS, 2, ROPE]))
                    dve.drain().then_inc(H.staged, 1)
                    return kv[:, :, :, NOPE:]

                def branch_b_out(b):
                    dve.wait_ge(sub_done, layer(l, b, BH).count(1))
                    for tok in range(TOKS):
                        y = rms(yb_rows[:, tok, :], H.T[1][:, tok * P:(tok + 1) * P], sub_rstd[:, tok:tok + 1], sub_g[:, :])
                    y.then_inc(H.out_done, 1)

                def branch_b_lo(b):
                    T.take_lo(dve, out_turn(l, b), layer(l, S2_B + b, S2), bT[1][:, b, :], bT[0][:, b, :], cols=SEQ)

                for b in range(BH):
                    n, nxt = pair(l, PAIRS + b), layer(l, G2_GATE + 20 + 2 * b, G2)
                    H.lows(dve, n, 0, HD ** -0.5, bias[:, AH + b, :])
                    if b < BH - 1:
                        stage_qk(two_cols(QB)[..., (b + 1) * P:(b + 2) * P])
                    else:
                        v_c = stage_c(0)
                    H.lows(dve, n, 1, HD ** -0.5, bias[:, AH + b, :])
                    if b > 0:
                        branch_b_out(b - 1)
                    stage_v(proj[:, :, VB + b * P:VB + (b + 1) * P])
                    tiles = ((slice(0, P), 0), (slice(P, TRI), 1))
                    dve.wait_ge(H.exp_done, twice(n, 0).count(1))
                    dve.reciprocal(H.inv[:, 0, :], H.sum[:, 0, :])
                    dve.drain()
                    for cols, tok in tiles:
                        dve.tensor_scalar(H.p[0][:, cols], H.p[0][:, cols], H.inv[:, 0, tok:tok + 1], None, ALU.mult)
                    dve.wait_ge(H.exp_done, twice(n, 1).count(1))
                    dve.reciprocal(H.inv[:, 1, :], H.sum[:, 1, :])
                    dve.drain()
                    dve.tensor_scalar(H.inv[:, 1, :], H.inv[:, 1, :], lam_neg[:, 0:1], None, ALU.mult)
                    dve.drain()
                    for cols, tok in tiles:
                        p = dve.scalar_tensor_tensor(H.p[0][:, cols], H.p[1][:, cols], H.inv[:, 1, tok:tok + 1],
                                                     H.p[0][:, cols], ALU.mult, ALU.add)
                    p.then_inc(H.p_ready, 2)
                    split(nxt + (-1), 2)
                    if b > 0:
                        branch_b_lo(b - 1)
                    if b % 2:
                        add_gate_bias(gate_tile(l, 4 + b // 2), nxt + (-3), slice(2 * D + b // 2 * NT, 2 * D + (b // 2 + 1) * NT))
                for c in range(PAIRS):
                    n, nxt = pair(l, PAIRS + BH + c), layer(l, G2_AB + 4 + 2 * c, G2)
                    i, e = c // 2, c % 2
                    cols = slice(i * NT, (i + 1) * NT)
                    H.lows(dve, n, 0, QH ** -0.5, hide)
                    v_now = v_c
                    if c < PAIRS - 1:
                        v_c = stage_c(c + 1)
                    H.lows(dve, n, 1, QH ** -0.5, hide)
                    if c == 0:
                        branch_b_out(BH - 1)
                    dve.tensor_copy(H.v[:, :, :].rearrange("p t (h c) -> p t h c", h=2), v_now).then_inc(H.v_staged, 1)
                    for h in range(2):
                        H.norm(dve, n, h)
                    split(nxt + (-1), 2)
                    if c == 0:
                        branch_b_lo(BH - 1)
                        dve.wait_ge(gate_done, layer(l, 6 * TOKS, 6 * TOKS).count(0))
                    for tok in range(TOKS):
                        W.wait_tile(dve, tok, layer(l, N2_AB + c, N2), nxt + (-3))
                        times_gate(tmp_rows[:, tok, :] if e else y_rows[:, tok, cols], slice(e * D + i * NT, e * D + (i + 1) * NT), tok)\
                            .then_inc(prod_free[tok], 1)
                    H.out_lo_part(dve, n, cT[1][:, c, :], cT[0][:, c, :])
                    if c == PAIRS - 1:
                        split(nxt + 1, 1)
                    if e:
                        dve.drain()
                        dve.tensor_tensor(y_rows[:, :, cols], y_rows[:, :, cols], tmp_rows, ALU.add)
                        dve.drain()
                for j in range(2):
                    split(layer(l, G2_O + 2 * j, G2), 1)
                    for tok in range(TOKS):
                        W.wait_tile(dve, tok, layer(l, N2_C + j, N2), layer(l, G2_C + 2 * j + 1, G2))
                        times_gate(tmp_rows[:, tok, :], slice(2 * D + j * NT, 2 * D + (j + 1) * NT), tok, (acc[0:2], prod)[j])\
                            .then_inc(prod_free[tok], 1)
                    dve.drain()
                    for tok in range(TOKS):
                        y = y_rows[:, tok, j * NT:(j + 1) * NT]
                        dve.tensor_tensor(y, y, tmp_rows[:, tok, :], ALU.add).then_inc(merged, 1)
                    dve.drain()
                    split(layer(l, G2_O + 2 * j + 1, G2), 1)
                    for tok in range(TOKS):
                        place = lambda p: p[:, 4 * j:4 * j + 4, tok * P:(tok + 1) * P]
                        T.take_lo(dve, layer(l, F2_M + 2 * j + tok, F2), layer(l, S2_M + 2 * j + tok, S2), place(uT[1]), place(uT[0]),
                                  scale=0.5, view=four)
                split(layer(l, G2_O + 4, G2), 4)
                for j in range(2):
                    if j == 1:
                        split(layer(l, G2_FF, G2), 3)
                    for tok in range(TOKS):
                        W.wait_tile(dve, tok, layer(l, N2_O + j, N2), layer(l, G2_O + OUT_LAST[j], G2))
                        x = x_res[:, tok, j * NT:(j + 1) * NT]
                        dve.tensor_tensor(x, x, (acc[2:4], acc[0:2])[j][tok][:, :], ALU.add).then_inc(prod_free[tok], 1)
                        dve.drain().then_inc(x_halves, 1)
                x_norm(layer(l, 1, 2), u2_rows, ffn_g, u2_ready)
                dve.drain().then_inc(vec_free, 1)
                split(layer(l, G2_FF + 3, G2), 1)
                for n in range(4):
                    place = lambda p: p[:, 4 * (n % 2):4 * (n % 2) + 4, n // 2 * P:(n // 2 + 1) * P]
                    T.take_lo(dve, layer(l, F2_U2 + n, F2), layer(l, S2_U2 + n, S2), place(uT[1]), place(uT[0]), view=four)

                def take_hidden(fill, split_n, out):
                    for tok in range(TOKS):
                        place = lambda p: p[:, 0:2, tok * P:(tok + 1) * P]
                        T.take_lo(dve, fill + tok, split_n + tok, place(out[1]), place(out[0]), cols=SEQ, scale=0.5, view=two)

                def gated(tile, last_group, n, banks=prod):
                    for tok in range(TOKS):
                        dve.wait_ge(act_done, n.count(tok + 1))
                        dve.scalar_tensor_tensor(act_rows[:, tok, :], act_rows[:, tok, :], 1.0, banks[tok][:, 0:HT],
                                                 ALU.add, ALU.mult)
                    dve.drain()
                    for tok in range(TOKS):
                        dve.tensor_tensor(hid_rows[:, tok, :], act_rows[:, tok, :], banks[tok][:, HT:NT], ALU.mult)\
                           .then_inc(prod_free[tok], 1)

                split(layer(l, G2_FF + 4, G2), 2)
                gated(layer(l, N2_FF, N2), layer(l, G2_FF + 3, G2), layer(l, 0, TOKS * HTILES), acc[2:4])
                with dve.Fori(0, HTILES // 2) as i:
                    for e in range(2):
                        at = Pos(G2_FF + 4 + 6 * e, (l, G2), (i, 12))
                        split(at + 2, 2)
                        take_hidden(Pos(F2_H + 2 * e, (l, F2), (i, 4)), Pos(S2_H + 2 * e, (l, S2), (i, 4)), (aT, bT)[e])
                        split(at + 4, 2)
                        gated(Pos(N2_FF + 1 + e, (l, N2), (i, 2)), at + 3, Pos(TOKS * (1 + e), (l, TOKS * HTILES), (i, 2 * TOKS)))
                        split(at + 6, 2)
                take_hidden(layer(l, F2 - 2, F2), layer(l, S2 - 2, S2), aT)
                for j in range(2):
                    dve.wait_ge(W.used, layer(l, G2 - 2 + j, G2).count(RING + 1))
                    for tok in range(TOKS):
                        x = x_res[:, tok, j * NT:(j + 1) * NT]
                        dve.tensor_tensor(x, x, acc[2 * j + tok][:, :], ALU.add).then_inc(x_halves, 1)
            dve.wait_ge(mix_in, 16 * (LAYERS + 1))
            x_norm(Pos(2 * LAYERS), x_res, mix_g)

        @block.tensor
        def _(pe):
            outs = lambda width: [prod[tok][:, 0:width] for tok in range(TOKS)]

            def vacated(tile_n):
                return lambda tok: pe.wait_ge(prod_free[tok], tile_n.count(1))

            def tile(pos, tile_n, lhs, k0, groups, width=NT):
                for g in range(groups):
                    W.multiply(pe, pos + g, lhs, k0 + KG * g, width, KG, outs(width), g == 0, g == groups - 1,
                               vacant=vacated(tile_n) if g == 0 else None)

            def rows_turn(pos, rows, chunk0, n=4):
                T.turn(pe, pos, [(P, slice(c * P, (c + 1) * P), rows[:, (chunk0 + c) * P:(chunk0 + c + 1) * P])
                                 for c in range(n)])

            def qk_turns(n, fill):
                pe.wait_ge(H.staged, n.count(1))
                rows = H.qk[:, 0:TOKS * 2 * P].rearrange("p (t x c) -> p t x c", t=TOKS, x=2)
                for x in range(2):
                    T.turn(pe, fill + x, [(P, slice(tok * P, (tok + 1) * P), rows[:, tok, x, :]) for tok in range(TOKS)])

            pe.wait_ge(consts_in, 16 * 2)
            pe.wait_ge(bias_in, 16)
            for b, flipped in enumerate(prod + acc):
                for h in range(2):
                    mm = pe.matmul(flipped[:, h * SEQ:(h + 1) * SEQ], flip, bias_flipped[:, 2 * b + h, :], start=True, stop=True)
                mm.then_inc(bias_turned, 1)
            with pe.Fori(0, LAYERS) as l:
                for n in range(4):
                    pe.wait_ge(h_ready, layer(l, n // 2, TOKS).count(1))
                    rows_turn(layer(l, n, F2), h_rows[:, n // 2, :], 4 * (n % 2))
                with pe.Fori(0, IN2_T - 1) as t:
                    for n in range(2, 4):
                        T.taken(pe, layer(l, n, F2))
                    tile(Pos(0, (l, G2), (t, 4)), Pos(0, (l, N2), (t, 1)), uT, 0, 4, IN2_W)

                def latent_turns(tok):
                    for n in range(2 * tok, 2 * tok + 2):
                        pe.wait_ge(lat_ready, layer(l, tok, TOKS).count(1))
                        rows_turn(layer(l, F2_LAT + n, F2), proj[:, tok, CQ:KR], 4 * (n % 2))

                for g in range(4):
                    if g % 2 == 0:
                        latent_turns(g // 2)
                    W.multiply(pe, layer(l, 4 * IN2_T - 4 + g, G2), uT, KG * g, IN2_W, KG, outs(IN2_W), g == 0, g == 3,
                               vacant=vacated(layer(l, IN2_T - 1, N2)) if g == 0 else None)
                for n in range(2, 4):
                    T.taken(pe, layer(l, F2_LAT + n, F2))
                for j in range(2):
                    for g, (lhs, k0) in enumerate(((aT, 0), (aT, 2), (bT, 0))):
                        W.multiply(pe, layer(l, G2_UQ + 3 * j + g, G2), lhs, k0, UQ_W, KG, outs(UQ_W), g == 0, g == 2,
                                   vacant=vacated(layer(l, N2_UQ + j, N2)) if g == 0 else None)
                qk_turns(pair(l, 0), qk_turn(l, 0))
                for j in range(2):
                    for g in range(2):
                        W.multiply(pe, layer(l, G2_UKV + 2 * j + g, G2), bT, 2 + g, NT, 1, outs(NT), g == 0, g == 1,
                                   vacant=vacated(layer(l, N2_UKV + j, N2)) if g == 0 else None)
                with pe.Fori(0, PAIRS) as t:
                    n, fill = pair(l, 0, (t, 1)), Pos(F2_A, (l, F2), (t, 2))
                    this = Pos(G2_GATE, (l, G2), (t, 4))
                    H.scores(pe, n, T, fill, True)
                    W.multiply(pe, this, uT, 0, NT, KG, outs(NT), True, False, vacant=vacated(gate_tile(l, 0, (t, 1))))
                    W.multiply(pe, this + 1, uT, 2, NT, KG, outs(NT), False, False)
                    qk_turns(n + 1, fill + 2)
                    W.multiply(pe, this + 2, uT, 4, NT, KG, outs(NT), False, False)
                    for h in range(2):
                        H.turn(pe, n, h, ident)
                    W.multiply(pe, this + 3, uT, 6, NT, KG, outs(NT), False, True)
                    H.mix(pe, n)

                def row_turns(m):
                    pe.wait_ge(H.staged, pair(l, m).count(1))
                    qk = H.qk[:, :].rearrange("p (t h x c) -> p t h x c", t=TOKS, h=2, x=2)
                    for h in range(2):
                        T.turn(pe, qk_turn(l, m) + h, [(QH, slice(x * SEQ + tok * P, x * SEQ + (tok + 1) * P), qk[:, tok, h, x, :])
                                                       for x in range(2) for tok in range(TOKS)])

                def branch_b_turn(b):
                    pe.wait_ge(H.out_done, pair(l, PAIRS + b).count(2))
                    T.turn(pe, out_turn(l, b), [(P, slice(tok * P, (tok + 1) * P), yb_rows[:, tok, :]) for tok in range(TOKS)])

                for b in range(BH):
                    m, e = PAIRS + b, b % 2
                    n, this = pair(l, m), layer(l, G2_GATE + 16 + 2 * b, G2)
                    H.scores(pe, n, T, qk_turn(l, m), True)
                    W.multiply(pe, this, uT, 4 * e, NT, KG, outs(NT), e == 0, False,
                               vacant=vacated(gate_tile(l, 4 + b // 2)) if e == 0 else None)
                    if b < BH - 1:
                        qk_turns(n + 1, qk_turn(l, m + 1))
                    else:
                        row_turns(m + 1)

                    def turn_p():
                        if b > 0:
                            branch_b_turn(b - 1)
                        pe.wait_ge(H.p_ready, twice(n, 1).count(1))
                        pe.wait_ge(H.out_done, n.count(1))
                        for k in range(3):
                            turned = pe.transpose(H.T[0][:, k * P:(k + 1) * P], H.p[0][:, k * P:(k + 1) * P], ident)
                        turned.then_inc(H.pT_full, 2)

                    W.multiply(pe, this + 1, uT, 4 * e + 2, NT, KG, outs(NT), False, e == 1, between=turn_p)
                    pe.wait_ge(H.pT_ready, twice(n, 1).count(1))
                    pe.wait_ge(H.v_staged, n.count(1))
                    o = [H.T[1][:, tok * P:(tok + 1) * P] for tok in range(TOKS)]
                    pe.matmul(o[0], H.pT[0][:, 0:P], H.v[:, 0, :], start=True, stop=True)
                    pe.matmul(o[1], H.pT[0][:, P:2 * P], H.v[:, 0, :], start=True, stop=False)
                    pe.matmul(o[1], H.pT[0][:, 2 * P:3 * P], H.v[:, 1, :], start=False, stop=True).then_inc(H.out_full, 1)
                for c in range(PAIRS):
                    m, lhs = PAIRS + BH + c, (aT, bT)[c % 2]
                    n, this = pair(l, m), layer(l, G2_AB + 2 * c, G2)
                    H.scores(pe, n, T, qk_turn(l, m), False)
                    if c == 1:
                        T.taken(pe, out_turn(l, BH - 1))
                    W.multiply(pe, this, lhs, 0, NT, KG, outs(NT), True, False, vacant=vacated(layer(l, N2_AB + c, N2)))
                    if c < PAIRS - 1:
                        row_turns(m + 1)

                    def turn_p():
                        if c == 0:
                            branch_b_turn(BH - 1)
                        for h in range(2):
                            H.turn(pe, n, h, ident)

                    W.multiply(pe, this + 1, lhs, 2, NT, KG, outs(NT), False, True, between=turn_p)
                    H.mix(pe, n)
                pe.wait_ge(H.out_done, pair(l, PER - 1).count(2))
                def merged_turns(j):
                    for tok in range(TOKS):
                        pe.wait_ge(merged, layer(l, 2 * j + tok, 4).count(1))
                        rows_turn(layer(l, F2_M + 2 * j + tok, F2), y_rows[:, tok, :], 4 * j)

                early, late = [b[:, :] for b in acc[0:2]], [b[:, :] for b in acc[2:4]]
                for g in range(2):
                    W.multiply(pe, layer(l, G2_C + g, G2), cT, KG * g, NT, KG, early, g == 0, g == 1)
                W.multiply(pe, layer(l, G2_C + 2, G2), cT, 0, NT, KG, outs(NT), True, False, vacant=vacated(layer(l, N2_C, N2)))
                merged_turns(0)
                W.multiply(pe, layer(l, G2_C + 3, G2), cT, 2, NT, KG, outs(NT), False, True)
                for i, (j, g) in enumerate(OUT_ORDER):
                    if i == 2:
                        merged_turns(1)
                    if i % 4 == 0:
                        for tok in range(TOKS):
                            T.taken(pe, layer(l, F2_M + i // 2 + tok, F2))
                    W.multiply(pe, layer(l, G2_O + i, G2), uT, KG * g, NT, KG, (late, early)[j], g == 0, g == 3,
                               vacant=vacated(layer(l, N2_C + 1, N2)) if i == 2 else None)
                for n in range(4):
                    pe.wait_ge(u2_ready, layer(l, n // 2, TOKS).count(1))
                    rows_turn(layer(l, F2_U2 + n, F2), u2_rows[:, n // 2, :], 4 * (n % 2))
                for n in range(2, 4):
                    T.taken(pe, layer(l, F2_U2 + n, F2))

                def hidden_turn(tile_n, fill):
                    for tok in range(TOKS):
                        pe.wait_ge(prod_free[tok], tile_n.count(2))
                        rows_turn(fill + tok, hid_rows[:, tok, :], 0, 2)

                def down(pos, lhs, fill, first, last):
                    for tok in range(TOKS):
                        T.taken(pe, fill + tok)
                    for j in range(2):
                        W.multiply(pe, pos + j, lhs, 0, NT, KG, [acc[2 * j + tok][:, :] for tok in range(TOKS)],
                                   first, last, tile_end=False)

                def step(at, tile_n, fill, lhs, first):
                    W.multiply(pe, at, uT, 0, NT, KG, outs(NT), True, False, vacant=vacated(tile_n + (-1) if first else tile_n))
                    W.multiply(pe, at + 1, uT, 2, NT, KG, outs(NT), False, False)
                    hidden_turn(tile_n + (-1), fill)
                    W.multiply(pe, at + 2, uT, 4, NT, KG, outs(NT), False, False)
                    W.multiply(pe, at + 3, uT, 6, NT, KG, outs(NT), False, True)
                    down(at + 4, lhs, fill, first, False)

                for g in range(4):
                    W.multiply(pe, layer(l, G2_FF + g, G2), uT, KG * g, NT, KG, late, g == 0, g == 3)
                for e in range(2):
                    step(layer(l, G2_FF + 4 + 6 * e, G2), layer(l, N2_FF + 1 + e, N2), layer(l, F2_H + 2 * e, F2),
                         (aT, bT)[e], e == 0)
                with pe.Fori(1, HTILES // 2) as i:
                    for e in range(2):
                        step(Pos(G2_FF + 4 + 6 * e, (l, G2), (i, 12)), Pos(N2_FF + 1 + e, (l, N2), (i, 2)),
                             Pos(F2_H + 2 * e, (l, F2), (i, 4)), (aT, bT)[e], False)
                hidden_turn(layer(l, N2 - 1, N2), layer(l, F2 - 2, F2))
                down(layer(l, G2 - 2, G2), aT, layer(l, F2 - 2, F2), False, True)



def program(nc, dr, out, scratch):
    with ExitStack() as ctx:
        sb = lambda n, s, dt=F32: ctx.enter_context(nc.sbuf_tensor(n, s, dt))
        x_res = sb("x_res", [P, TOKS, D])
        ident, hide = sb("ident", [P, P]), sb("hide", [P, TRI])
        ones, small = sb("ones", [P, P]), sb("small", [P, 3, 4])
        consts_in = ctx.enter_context(nc.semaphore("consts_in"))

        bias_rows = BiasRows(nc, ctx, dr, scratch)

        def load_constants(sp):
            sp.dma_start(x_res[:, :, :], dr["x"].rearrange("a (t p) d -> p (a t) d", p=P)).then_inc(consts_in, 16)
            sp.dma_start(ident[:, :], dr["identity"]).then_inc(consts_in, 16)
            sp.dma_start(hide[:, :], dr["causal"]).then_inc(consts_in, 16)

        with nc.Block() as block:
            @block.vector
            def _(dve):
                dve.memset(ones[:, :], 1.0)
                for n, value in enumerate((LN_EPS, RMS_EPS, -0.5)):
                    dve.memset(small[:, n, :], value)
                dve.drain()

        first_block(nc, dr, x_res, ident[:, :], hide[:, :], ones, small, load_constants, consts_in, bias_rows)
        second_block(nc, dr, scratch, bias_rows, x_res, ident[:, :], hide[:, :], ones, small)
        out_done = ctx.enter_context(nc.semaphore("out_done"))
        with nc.Block() as block:
            @block.sync
            def _(sp):
                sp.dma_start(out.rearrange("a (t p) d -> p (a t) d", p=P), x_res[:, :, :]).then_inc(out_done, 16)
                sp.wait_ge(out_done, 16)


def shape_constants():
    pos = np.arange(SEQ)
    keys = np.concatenate([np.arange(P), np.arange(SEQ)])
    queries = np.arange(P)[:, None] + np.repeat([0, P], [P, SEQ])[None, :]
    dist = SEQ - 1 - np.arange(REL)
    far = np.log(np.maximum(dist, 1).astype(np.float32) / 16) / np.float32(np.log(128.0)) * 16
    bucket = np.where(dist < 16, np.maximum(dist, 0), np.minimum(16 + far.astype(np.int32), BUCKETS - 1))
    past = dist >= 0
    patterns = ((dist <= P) & past).astype(int) + ((dist % 4 == 0) & past) + ((dist % 16 == 0) & past)
    rows = np.zeros((BUCKETS + 2, REL), np.float32)
    rows[bucket[past], np.arange(REL)[past]] = -1.0
    rows[BUCKETS] = np.where(patterns > 0, -np.log(np.maximum(patterns, 1)), BIG)
    rows[BUCKETS + 1] = np.where(past, 0.0, BIG)
    kinds = np.zeros((2, AH + BH), np.float32)
    kinds[0, :AH], kinds[1, AH:] = 1.0, 1.0
    lam_init = [0.8 - 0.6 * np.exp(-0.3 * l) for l in range(LAYERS)]
    theta = lambda base, n: (base ** (-np.arange(0, n, 2, dtype=np.float32) / n)).astype(np.float32)
    angles = pos.astype(np.float32)[:, None] * theta(np.float32(10000.0), ROPE)[None, :]
    return {
        "flip": np.eye(P, dtype=np.float32)[::-1],
        "bias_rows": rows,
        "bias_kinds": kinds,
        "trig_2": np.concatenate([np.cos(angles), np.sin(angles)], 1).astype(np.float32),
        "lam_const": np.array([[-x, 1.0 - x] for x in lam_init], np.float32),
        "identity": np.eye(P, dtype=np.float32),
        "causal": np.where(keys[None, :] <= queries, 0.0, BIG).astype(np.float32),
        "inv_freq": theta(np.float32(500000.0), ROT)[None, :],
    }


def kernel(**inputs):
    import concourse.bacc as _bacc
    from concourse.bass_utils import run_bass_kernel_spmd as _run

    nc = _bacc.Bacc("TRN2", target_bir_lowering=False, num_devices=1)
    arrays, dr = {}, {}
    for name, value in {**inputs, **shape_constants()}.items():
        a = np.ascontiguousarray(value)
        arrays[f"in_{name}_dram"] = a
        dr[name] = nc.dram_tensor(f"in_{name}_dram", a.shape, mybir.dt.from_np(a.dtype), kind="ExternalInput").ap()
    out = nc.dram_tensor("out_0_dram", (1, SEQ, D), F32, kind="ExternalOutput").ap()
    scratch = nc.dram_tensor("bias_rows_dram", (AH + BH, REL), F32, kind="Internal").ap()
    program(nc, dr, out, scratch)
    r = _run(nc, [arrays], core_ids=[0])
    return r.results[0]["out_0_dram"]
```
